# Optimizing a Trainium2 kernel written in Bass

```python
import jax
import jax.numpy as jnp
from jax import lax
import numpy as np
import math
import jax, jax.numpy as jnp

D_MODEL = 1024
BATCH = 1
SEQ = 512
DEPTH = 1

NSA_HEADS = 8
NSA_KV_GROUPS = 2
NSA_HEAD_DIM = 64
CMP_LEN = 32
CMP_STRIDE = 16
CMP_HIDDEN = 128
SLC_LEN = 64
N_SELECT = 16
WINDOW = 512
Q_BLOCK = 128
FORCE_SCORE = 1e4
HGRN_HEADS = 4
HGRN_KEY_DIM = 128
HGRN_VAL_DIM = 128
HGRN_CHUNK = 64
D_FF = -(-8 * D_MODEL // (3 * 256)) * 256
RMS_EPS = 1e-6

NSA_WIDTH = NSA_HEADS * NSA_HEAD_DIM
NSA_KV_WIDTH = NSA_KV_GROUPS * NSA_HEAD_DIM
HGRN_KEY_WIDTH = HGRN_HEADS * HGRN_KEY_DIM
HGRN_VAL_WIDTH = HGRN_HEADS * HGRN_VAL_DIM
MIX_WIDTH = NSA_WIDTH + HGRN_VAL_WIDTH
IN_SIZES = (NSA_WIDTH,) + (NSA_KV_WIDTH,) * 6 + (3 * NSA_HEADS, HGRN_KEY_WIDTH, HGRN_KEY_WIDTH, HGRN_VAL_WIDTH, HGRN_VAL_WIDTH)
IN_WIDTH = sum(IN_SIZES)


def rms_norm(x, g):
    xf = x.astype(jnp.float32)
    y = xf * lax.rsqrt(jnp.mean(xf * xf, axis=-1, keepdims=True) + RMS_EPS)
    return (y * g.astype(jnp.float32)).astype(x.dtype)

def masked_softmax(s, mask):
    s = jnp.where(mask, s.astype(jnp.float32), -1e30)
    p = jax.nn.softmax(s, axis=-1)
    return jnp.where(mask, p, 0.0)

def compress(seq, pos, w1, w2):
    B, T, G, dh = seq.shape
    ratio = CMP_LEN // CMP_STRIDE
    nseg = T // CMP_STRIDE
    ncmp = nseg - ratio + 1
    seg = seq.reshape(B, nseg, CMP_STRIDE, G, dh)
    blocks = jnp.concatenate([seg[:, r:r + ncmp] for r in range(ratio)], axis=2)
    blocks = blocks + pos[None, None, :, None, :]
    flat = blocks.transpose(0, 1, 3, 2, 4).reshape(B, ncmp, G, CMP_LEN * dh)
    return jax.nn.gelu(flat @ w1) @ w2

def nsa_mixer(q, kc, vc, ks, vs, kw, vw, gates):
    B, T, H, dh = q.shape
    G = NSA_KV_GROUPS
    R = H // G
    ncmp = kc.shape[1]
    nslc = T // SLC_LEN
    n_sel = min(N_SELECT, nslc)
    scale = dh ** -0.5
    cmp_start = jnp.arange(ncmp) * CMP_STRIDE
    cmp_end = cmp_start + CMP_LEN - 1
    slc_start = jnp.arange(nslc) * SLC_LEN
    overlap = ((cmp_start[:, None] < slc_start[None, :] + SLC_LEN)
               & (cmp_start[:, None] + CMP_LEN > slc_start[None, :])).astype(jnp.float32)
    ks_blk = ks.reshape(B, nslc, SLC_LEN, G, dh).transpose(0, 3, 1, 2, 4)
    vs_blk = vs.reshape(B, nslc, SLC_LEN, G, dh).transpose(0, 3, 1, 2, 4)
    pad = ((0, 0), (WINDOW, 0), (0, 0), (0, 0))
    kw_pad = jnp.pad(kw, pad)
    vw_pad = jnp.pad(vw, pad)
    bi = jnp.arange(B)[:, None, None, None]
    gi = jnp.arange(G)[None, :, None, None]
    j = jnp.arange(nslc)

    def block(qb):
        s = qb * Q_BLOCK
        t = s + jnp.arange(Q_BLOCK)
        qblk = lax.dynamic_slice_in_dim(q, s, Q_BLOCK, 1).reshape(B, Q_BLOCK, G, R, dh)
        sc = jnp.einsum('bqgrd,bngd->bgrqn', qblk, kc) * scale
        p_cmp = masked_softmax(sc, cmp_end[None, :] <= t[:, None])
        o_cmp = jnp.einsum('bgrqn,bngd->bqgrd', p_cmp, vc.astype(jnp.float32))
        imp = jnp.einsum('bgrqn,nj->bgqj', p_cmp, overlap)
        jcur = t // SLC_LEN
        forced = (j[None, :] == 0) | (j[None, :] == jcur[:, None]) | (j[None, :] == jcur[:, None] - 1)
        future = j[None, :] > jcur[:, None]
        imp = jnp.where(forced, FORCE_SCORE, jnp.where(future, -1.0, imp))
        _, idx = lax.top_k(imp, n_sel)
        k_sel = ks_blk[bi, gi, idx].reshape(B, G, Q_BLOCK, n_sel * SLC_LEN, dh)
        v_sel = vs_blk[bi, gi, idx].reshape(B, G, Q_BLOCK, n_sel * SLC_LEN, dh)
        pos_sel = (idx[..., None] * SLC_LEN + jnp.arange(SLC_LEN)).reshape(B, G, Q_BLOCK, n_sel * SLC_LEN)
        ss = jnp.einsum('bqgrd,bgqkd->bgrqk', qblk, k_sel) * scale
        p_sel = masked_softmax(ss, (pos_sel <= t[None, None, :, None])[:, :, None])
        o_sel = jnp.einsum('bgrqk,bgqkd->bqgrd', p_sel, v_sel.astype(jnp.float32))
        k_win = lax.dynamic_slice_in_dim(kw_pad, s, WINDOW + Q_BLOCK, 1)
        v_win = lax.dynamic_slice_in_dim(vw_pad, s, WINDOW + Q_BLOCK, 1)
        pos_win = s - WINDOW + jnp.arange(WINDOW + Q_BLOCK)
        diff = t[:, None] - pos_win[None, :]
        win_mask = (diff >= 0) & (diff < WINDOW) & (pos_win[None, :] >= 0)
        sw = jnp.einsum('bqgrd,bkgd->bgrqk', qblk, k_win) * scale
        p_win = masked_softmax(sw, win_mask)
        o_win = jnp.einsum('bgrqk,bkgd->bqgrd', p_win, v_win.astype(jnp.float32))
        g = lax.dynamic_slice_in_dim(gates, s, Q_BLOCK, 1).reshape(B, Q_BLOCK, G, R, 3)
        o = g[..., 0:1] * o_cmp + g[..., 1:2] * o_sel + g[..., 2:3] * o_win
        return o.reshape(B, Q_BLOCK, H * dh)

    out = lax.map(block, jnp.arange(T // Q_BLOCK))
    return out.transpose(1, 0, 2, 3).reshape(B, T, H * dh)

def hgrn2_mixer(hq, hf, hi, hg, lb, o_gain):
    B, T, _ = hq.shape
    H, dk, dv, C = HGRN_HEADS, HGRN_KEY_DIM, HGRN_VAL_DIM, HGRN_CHUNK
    f32 = jnp.float32
    q = jax.nn.silu(hq.astype(f32)).reshape(B, T, H, dk)
    f = lb + (1.0 - lb) * jax.nn.sigmoid(hf.astype(f32))
    logf = jnp.log(f).reshape(B, T, H, dk)
    k = (1.0 - f).reshape(B, T, H, dk)
    v = hi.astype(f32).reshape(B, T, H, dv)
    nc = T // C

    def to_chunks(a):
        return a.reshape(B, nc, C, H, a.shape[-1]).transpose(1, 0, 3, 2, 4)

    causal = jnp.tril(jnp.ones((C, C), dtype=bool))

    def step(S, xs):
        qc, kc, vc, gc = xs
        b = jnp.cumsum(gc, axis=-2)
        b_last = b[:, :, -1:, :]
        o_inter = jnp.einsum('bhcd,bhde->bhce', qc * jnp.exp(b), S)
        decay = jnp.exp(jnp.where(causal[:, :, None], b[:, :, :, None, :] - b[:, :, None, :, :], -jnp.inf))
        attn = jnp.einsum('bhtd,bhsd,bhtsd->bhts', qc, kc, decay)
        o = o_inter + jnp.einsum('bhts,bhse->bhte', attn, vc)
        S = jnp.exp(b_last[:, :, 0, :])[..., None] * S + jnp.einsum('bhsd,bhse->bhde', kc * jnp.exp(b_last - b), vc)
        return S, o

    S0 = jnp.zeros((B, H, dk, dv), f32)
    _, o = lax.scan(step, S0, (to_chunks(q), to_chunks(k), to_chunks(v), to_chunks(logf)))
    o = o.transpose(1, 0, 3, 2, 4).reshape(B, T, H, dv)
    o = rms_norm(o, o_gain) * jax.nn.silu(hg.astype(f32)).reshape(B, T, H, dv)
    return o.reshape(B, T, H * dv)

def first_inputs(seed: int = 0) -> dict:
    key = jax.random.key(seed)
    k = jax.random.split(key, 17)
    f32 = jnp.float32
    dh = NSA_HEAD_DIM

    def nrm(kk, shape, scale):
        return jax.random.normal(kk, shape, f32) * scale

    return {
        'x': nrm(k[0], (BATCH, SEQ, D_MODEL), 1.0),
        'norm_mix': 1.0 + nrm(k[1], (DEPTH, D_MODEL), 0.02),
        'w_in': nrm(k[2], (DEPTH, D_MODEL, IN_WIDTH), D_MODEL ** -0.5),
        'q_norm': 1.0 + nrm(k[3], (DEPTH, dh), 0.02),
        'k_norm': 1.0 + nrm(k[4], (DEPTH, 3, dh), 0.02),
        'cmp_pos_k': nrm(k[5], (DEPTH, CMP_LEN, dh), 0.5),
        'cmp_pos_v': nrm(k[6], (DEPTH, CMP_LEN, dh), 0.5),
        'cmp_k_w1': nrm(k[7], (DEPTH, CMP_LEN * dh, CMP_HIDDEN), (CMP_LEN * dh) ** -0.5),
        'cmp_k_w2': nrm(k[8], (DEPTH, CMP_HIDDEN, dh), CMP_HIDDEN ** -0.5),
        'cmp_v_w1': nrm(k[9], (DEPTH, CMP_LEN * dh, CMP_HIDDEN), (CMP_LEN * dh) ** -0.5),
        'cmp_v_w2': nrm(k[10], (DEPTH, CMP_HIDDEN, dh), CMP_HIDDEN ** -0.5),
        'hgrn_lb_logits': nrm(k[11], (DEPTH + 1, HGRN_KEY_WIDTH), 0.5),
        'hgrn_o_norm': 1.0 + nrm(k[12], (DEPTH, HGRN_VAL_DIM), 0.02),
        'w_out': nrm(k[13], (DEPTH, MIX_WIDTH, D_MODEL), MIX_WIDTH ** -0.5),
        'norm_ffn': 1.0 + nrm(k[14], (DEPTH, D_MODEL), 0.02),
        'w_gate_up': nrm(k[15], (DEPTH, D_MODEL, 2 * D_FF), D_MODEL ** -0.5),
        'w_down': nrm(k[16], (DEPTH, D_FF, D_MODEL), D_FF ** -0.5),
    }

def first_block(x, norm_mix, w_in, q_norm, k_norm, cmp_pos_k, cmp_pos_v, cmp_k_w1, cmp_k_w2, cmp_v_w1, cmp_v_w2,
              hgrn_lb_logits, hgrn_o_norm, w_out, norm_ffn, w_gate_up, w_down):
    B, T, _ = x.shape
    H, G, dh = NSA_HEADS, NSA_KV_GROUPS, NSA_HEAD_DIM
    split_points = [int(v) for v in np.cumsum(IN_SIZES)[:-1]]
    lower_bounds = jnp.cumsum(jax.nn.softmax(hgrn_lb_logits.astype(jnp.float32), axis=0), axis=0)
    for l in range(DEPTH):
        h = rms_norm(x, norm_mix[l])
        proj = h @ w_in[l]
        (q, kc_raw, vc_raw, ks, vs, kw, vw, gate_logits, hq, hf, hi, hg) = jnp.split(proj, split_points, axis=-1)
        q = rms_norm(q.reshape(B, T, H, dh), q_norm[l])
        kc = rms_norm(compress(kc_raw.reshape(B, T, G, dh), cmp_pos_k[l], cmp_k_w1[l], cmp_k_w2[l]), k_norm[l, 0])
        vc = compress(vc_raw.reshape(B, T, G, dh), cmp_pos_v[l], cmp_v_w1[l], cmp_v_w2[l])
        ks = rms_norm(ks.reshape(B, T, G, dh), k_norm[l, 1])
        kw = rms_norm(kw.reshape(B, T, G, dh), k_norm[l, 2])
        gates = jax.nn.sigmoid(gate_logits.astype(jnp.float32)).reshape(B, T, H, 3)
        o_nsa = nsa_mixer(q, kc, vc, ks, vs.reshape(B, T, G, dh), kw, vw.reshape(B, T, G, dh), gates)
        o_hgrn = hgrn2_mixer(hq, hf, hi, hg, lower_bounds[l], hgrn_o_norm[l])
        mix = jnp.concatenate([o_nsa.astype(x.dtype), o_hgrn.astype(x.dtype)], axis=-1)
        x = x + mix @ w_out[l]
        h = rms_norm(x, norm_ffn[l])
        gate, up = jnp.split(h @ w_gate_up[l], 2, axis=-1)
        x = x + (jax.nn.silu(gate) * up) @ w_down[l]
    return x


DEPTH_2 = 2

HEAD_DIM = 64
ROPE_THETA = 10000.0
BLOCK = 128
NORM_EPS = 1e-6
NEG_INF = -1e30
DA_HEADS = D_MODEL // (2 * HEAD_DIM)
DA_QK = DA_HEADS * 2 * HEAD_DIM
DA_V = DA_HEADS * 2 * HEAD_DIM
WINDOW_2 = 128
SW_HEADS = D_MODEL // HEAD_DIM
SW_KV_HEADS = 4
SW_GROUP = SW_HEADS // SW_KV_HEADS
FFN_HIDDEN = ((8 * D_MODEL // 3 + 255) // 256) * 256
N_A = DEPTH_2 // 2
N_B = DEPTH_2 - N_A


def rms_norm_2(x, g):
    xf = x.astype(jnp.float32)
    y = xf * lax.rsqrt(jnp.mean(xf * xf, axis=-1, keepdims=True) + NORM_EPS)
    return (y * g.astype(jnp.float32)).astype(x.dtype)

def rope_tables(positions):
    inv = 1.0 / (ROPE_THETA ** (jnp.arange(0, HEAD_DIM, 2, dtype=jnp.float32) / HEAD_DIM))
    ang = positions.astype(jnp.float32)[..., None] * inv
    return jnp.cos(ang), jnp.sin(ang)

def apply_rope(x, cos, sin):
    extra = x.ndim - 3
    shp = cos.shape[:2] + (1,) * extra + cos.shape[-1:]
    c = cos.reshape(shp)
    s = sin.reshape(shp)
    x1, x2 = jnp.split(x.astype(jnp.float32), 2, axis=-1)
    return jnp.concatenate([x1 * c - x2 * s, x2 * c + x1 * s], axis=-1).astype(x.dtype)

def swiglu(h, w_gate_up, w_down):
    g, u = jnp.split(h @ w_gate_up, 2, axis=-1)
    return (jax.nn.silu(g) * u) @ w_down

def diff_attention(h, cos, sin, w_qkv, q_norm, k_norm, lam_p, subln, w_o, layer_idx):
    B, S, _ = h.shape
    lambda_init = 0.8 - 0.6 * math.exp(-0.3 * layer_idx)
    q, k, v = jnp.split(h @ w_qkv, [DA_QK, 2 * DA_QK], axis=-1)
    q = apply_rope(rms_norm_2(q.reshape(B, S, DA_HEADS, 2, HEAD_DIM), q_norm), cos, sin)
    k = apply_rope(rms_norm_2(k.reshape(B, S, DA_HEADS, 2, HEAD_DIM), k_norm), cos, sin)
    v = v.reshape(B, S, DA_HEADS, 2 * HEAD_DIM)
    lp = lam_p.astype(jnp.float32)
    lam = jnp.exp(jnp.sum(lp[0] * lp[1])) - jnp.exp(jnp.sum(lp[2] * lp[3])) + lambda_init
    scale = 1.0 / math.sqrt(HEAD_DIM)
    nb = S // BLOCK
    qb = jnp.moveaxis(q.reshape(B, nb, BLOCK, DA_HEADS, 2, HEAD_DIM), 1, 0)
    kpos = jnp.arange(S)

    def one_block(args):
        qblk, i = args
        s = jnp.einsum('bqhcd,bkhcd->bhcqk', qblk, k).astype(jnp.float32) * scale
        qpos = i * BLOCK + jnp.arange(BLOCK)
        causal = kpos[None, :] <= qpos[:, None]
        p = jax.nn.softmax(jnp.where(causal, s, NEG_INF), axis=-1)
        a = p[:, :, 0] - lam * p[:, :, 1]
        return jnp.einsum('bhqk,bkhe->bqhe', a.astype(v.dtype), v)

    o = lax.map(one_block, (qb, jnp.arange(nb)))
    o = jnp.moveaxis(o, 0, 1).reshape(B, S, DA_HEADS, 2 * HEAD_DIM)
    o = rms_norm_2(o, subln) * (1.0 - lambda_init)
    return o.reshape(B, S, DA_V) @ w_o

def shared_kv(x, cos, sin, kv_norm, w_kv, k_norm):
    B, S, _ = x.shape
    k, v = jnp.split(rms_norm_2(x, kv_norm) @ w_kv, 2, axis=-1)
    k = apply_rope(rms_norm_2(k.reshape(B, S, SW_KV_HEADS, HEAD_DIM), k_norm), cos, sin)
    v = v.reshape(B, S, SW_KV_HEADS, HEAD_DIM)
    nb = S // WINDOW_2

    def band(t):
        tp = jnp.pad(t, ((0, 0), (WINDOW_2, 0), (0, 0), (0, 0))).reshape(B, nb + 1, WINDOW_2, SW_KV_HEADS, HEAD_DIM)
        return jnp.concatenate([tp[:, :-1], tp[:, 1:]], axis=2)

    return band(k), band(v)

def swa_sink_attention(h, cos, sin, w_q, q_norm, sinks, w_o, kw, vw):
    B, S, _ = h.shape
    nb = S // WINDOW_2
    q = (h @ w_q).reshape(B, S, SW_KV_HEADS, SW_GROUP, HEAD_DIM)
    q = apply_rope(rms_norm_2(q, q_norm), cos, sin)
    qb = q.reshape(B, nb, WINDOW_2, SW_KV_HEADS, SW_GROUP, HEAD_DIM)
    s = jnp.einsum('bnqhgd,bnkhd->bnhgqk', qb, kw).astype(jnp.float32) * (1.0 / math.sqrt(HEAD_DIM))
    qi = jnp.arange(WINDOW_2)[:, None]
    kj = jnp.arange(2 * WINDOW_2)[None, :]
    in_band = (kj > qi) & (kj <= qi + WINDOW_2)
    valid = in_band[None] & ((jnp.arange(nb)[:, None, None] > 0) | (kj >= WINDOW_2)[None])
    s = jnp.where(valid[None, :, None, None], s, NEG_INF)
    sink = sinks.astype(jnp.float32).reshape(SW_KV_HEADS, SW_GROUP)[None, None, :, :, None, None]
    m = jnp.maximum(jnp.max(s, axis=-1, keepdims=True), sink)
    e = jnp.exp(s - m)
    p = e / (jnp.sum(e, axis=-1, keepdims=True) + jnp.exp(sink - m))
    o = jnp.einsum('bnhgqk,bnkhd->bnqhgd', p.astype(vw.dtype), vw)
    return o.reshape(B, S, SW_HEADS * HEAD_DIM) @ w_o

def second_inputs(seed: int = 0) -> dict:
    key = jax.random.key(seed)
    ks = jax.random.split(key, 24)
    f32 = jnp.float32

    def w(k, shape, fan_in):
        return jax.random.normal(k, shape, f32) * (fan_in ** -0.5)

    def gain(k, shape):
        return 1.0 + 0.02 * jax.random.normal(k, shape, f32)

    x = jax.random.normal(ks[0], (BATCH, SEQ, D_MODEL), f32)
    offset = jax.random.randint(ks[1], (BATCH, 1), 0, 4096, dtype=jnp.int32)
    positions = jnp.arange(SEQ, dtype=jnp.int32)[None, :] + offset
    return {
        'x': x,
        'positions': positions,
        'attn_norm': gain(ks[2], (DEPTH_2, D_MODEL)),
        'ffn_norm': gain(ks[3], (DEPTH_2, D_MODEL)),
        'w_gate_up': w(ks[4], (DEPTH_2, D_MODEL, 2 * FFN_HIDDEN), D_MODEL),
        'w_down': w(ks[5], (DEPTH_2, FFN_HIDDEN, D_MODEL), FFN_HIDDEN),
        'da_w_qkv': w(ks[6], (N_A, D_MODEL, 2 * DA_QK + DA_V), D_MODEL),
        'da_q_norm': gain(ks[7], (N_A, 2, HEAD_DIM)),
        'da_k_norm': gain(ks[8], (N_A, 2, HEAD_DIM)),
        'da_lambda': 0.1 * jax.random.normal(ks[9], (N_A, 4, HEAD_DIM), f32),
        'da_subln': gain(ks[10], (N_A, 2 * HEAD_DIM)),
        'da_w_o': w(ks[11], (N_A, DA_V, D_MODEL), DA_V),
        'kv_norm': gain(ks[12], (D_MODEL,)),
        'w_kv': w(ks[13], (D_MODEL, 2 * SW_KV_HEADS * HEAD_DIM), D_MODEL),
        'k_norm': gain(ks[14], (HEAD_DIM,)),
        'sw_w_q': w(ks[15], (N_B, D_MODEL, SW_HEADS * HEAD_DIM), D_MODEL),
        'sw_q_norm': gain(ks[16], (N_B, HEAD_DIM)),
        'sw_sinks': 0.5 * jax.random.normal(ks[17], (N_B, SW_HEADS), f32),
        'sw_w_o': w(ks[18], (N_B, SW_HEADS * HEAD_DIM, D_MODEL), SW_HEADS * HEAD_DIM),
    }

def second_block(x, positions, attn_norm, ffn_norm, w_gate_up, w_down, da_w_qkv, da_q_norm, da_k_norm,
              da_lambda, da_subln, da_w_o, kv_norm, w_kv, k_norm, sw_w_q, sw_q_norm, sw_sinks, sw_w_o):
    cos, sin = rope_tables(positions)
    kw = vw = None
    for l in range(DEPTH_2):
        h = rms_norm_2(x, attn_norm[l])
        if l < N_A:
            x = x + diff_attention(h, cos, sin, da_w_qkv[l], da_q_norm[l], da_k_norm[l],
                                   da_lambda[l], da_subln[l], da_w_o[l], l)
        else:
            if l == N_A:
                kw, vw = shared_kv(x, cos, sin, kv_norm, w_kv, k_norm)
                h = rms_norm_2(x, attn_norm[l])
            j = l - N_A
            x = x + swa_sink_attention(h, cos, sin, sw_w_q[j], sw_q_norm[j], sw_sinks[j], sw_w_o[j], kw, vw)
        x = x + swiglu(rms_norm_2(x, ffn_norm[l]), w_gate_up[l], w_down[l])
    return x


def setup_inputs(seed=0):
    out = dict(first_inputs(seed))
    for name, value in second_inputs(seed + 1).items():
        if name != "x":
            out[name + "_2"] = value
    return out


def reference(
    x, norm_mix, w_in, q_norm, k_norm, cmp_pos_k, cmp_pos_v, cmp_k_w1, cmp_k_w2, cmp_v_w1,
    cmp_v_w2, hgrn_lb_logits, hgrn_o_norm, w_out, norm_ffn, w_gate_up, w_down, positions_2,
    attn_norm_2, ffn_norm_2, w_gate_up_2, w_down_2, da_w_qkv_2, da_q_norm_2, da_k_norm_2,
    da_lambda_2, da_subln_2, da_w_o_2, kv_norm_2, w_kv_2, k_norm_2, sw_w_q_2, sw_q_norm_2,
    sw_sinks_2, sw_w_o_2,
):
    x = first_block(
        x, norm_mix, w_in, q_norm, k_norm, cmp_pos_k, cmp_pos_v, cmp_k_w1, cmp_k_w2, cmp_v_w1,
        cmp_v_w2, hgrn_lb_logits, hgrn_o_norm, w_out, norm_ffn, w_gate_up, w_down,
    )
    return second_block(
        x, positions_2, attn_norm_2, ffn_norm_2, w_gate_up_2, w_down_2, da_w_qkv_2, da_q_norm_2,
        da_k_norm_2, da_lambda_2, da_subln_2, da_w_o_2, kv_norm_2, w_kv_2, k_norm_2, sw_w_q_2,
        sw_q_norm_2, sw_sinks_2, sw_w_o_2,
    )


_drawn_inputs = setup_inputs


def setup_inputs(seed=0):
    import zlib

    import numpy as np

    out = dict(_drawn_inputs(seed))
    spreads = {}
    factors = {'norm_mix': 2.956,
     'q_norm': 8.0,
     'k_norm': 8.0,
     'hgrn_o_norm': 5.601,
     'norm_ffn': 3.302,
     'attn_norm_2': 3.063,
     'ffn_norm_2': 3.749,
     'da_q_norm_2': 6.359,
     'da_k_norm_2': 6.313,
     'da_subln_2': 4.28,
     'kv_norm_2': 8.0,
     'k_norm_2': 8.0,
     'sw_q_norm_2': 8.0,
     'sw_sinks_2': 195.788}
    for name, (base, spread) in spreads.items():
        noise = np.random.default_rng([zlib.crc32(name.encode()), seed]).standard_normal(out[name].shape)
        drawn = base * np.exp(spread * noise) if base else spread * noise
        out[name] = jnp.asarray(drawn.astype(out[name].dtype))
    for name, factor in factors.items():
        out[name] = (out[name] * factor).astype(out[name].dtype)
    return out
```

```python
from contextlib import ExitStack

import numpy as np
import concourse.bass as bass
from concourse import mybir

F = mybir.dt.float32
R = mybir.dt.float32r
BF = mybir.dt.bfloat16
I32 = mybir.dt.int32
U8 = mybir.dt.uint8
ALU = mybir.AluOpType
ACT = mybir.ActivationFunctionType
AX = mybir.AxisListType

T = 512
KT8 = 8
EPS = 1e-6
PARTS = (8, 8, 6)
CH = 1024

C_ID, C_BO, C_ON, C_PM, C_MC, C_VA, C_INV, C_EPS, C_HPI, C_RM = 0, 128, 256, 384, 512, 640, 644, 645, 646, 704
C_N = 704 + 512
G_MIX, G_FFN, G_AT0, G_AT1, G_F0, G_F1, G_KV = 0, 8, 16, 24, 32, 40, 48
G_Q, G_KS, G_KW, G_DQ, G_DK, G_SUB, G_SQ, G_SK, G_HO = 56, 57, 58, 59, 60, 61, 62, 63, 64
G_LB, G_PK, G_PV, G_KC, G_SINK, G_LAM = 65, 73, 105, 137, 201, 217
G_N = 217 + 256
LAMBDA_INIT = 0.2


class Tok:

    def __init__(self, eng, val=0):
        self.eng, self.val, self.need = eng, val, False


class Slot:

    def __init__(self, ap):
        self.ap, self.free = ap, []


class Ring:
    def __init__(self, aps):
        self.slots, self.n = [Slot(a) for a in aps], 0

    def take(self):
        s = self.slots[self.n % len(self.slots)]
        self.n += 1
        return s


def flat(after):
    for a in after:
        if a is None:
            continue
        if isinstance(a, (list, tuple)):
            yield from flat(a)
        else:
            yield a


class Queues:

    def __init__(self):
        self.q = {k: [] for k in ("pe", "act", "dve", "pool", "sp")}

    def put(self, eng, fn, *after):
        tok = Tok(eng)
        waits = [a for a in flat(after) if not (eng == "pe" and a.eng == "pe")]
        for a in waits:
            a.need = True
        self.q[eng].append((fn, waits, tok))
        return tok

    def dma(self, eng, dsem, out, in_, *after):
        dsem[1] += 1
        tok = Tok(dsem[0], 16 * dsem[1])
        waits = list(flat(after))
        for a in waits:
            a.need = True
        sem = dsem[0]
        self.q[eng].append((lambda e: e.dma_start(out, in_).then_inc(sem, 16), waits, None))
        return tok

    def count(self):
        for q in self.q.values():
            n = 0
            for _, _, tok in q:
                if tok is not None and tok.need:
                    n += 1
                    tok.val = n

    def emit(self, name, eng, sems):
        seen = {}
        for fn, waits, tok in self.q[name]:
            need = {}
            for a in waits:
                need[a.eng] = max(need.get(a.eng, 0), a.val)
            for k, v in need.items():
                if seen.get(k, 0) < v:
                    eng.wait_ge(sems[k] if isinstance(k, str) else k, v)
                    seen[k] = v
            ins = fn(eng)
            if tok is not None and tok.need:
                ins.then_inc(sems[name], 1)


def fence_of(queues):
    return [q[-1][2] for k, q in queues.q.items() if k != "sp" and q]


def interleave(a, b, na=1, nb=1):
    live = [True, True]
    while any(live):
        for n, (g, k) in enumerate(((a, na), (b, nb))):
            for _ in range(k):
                if live[n]:
                    try:
                        next(g)
                    except StopIteration:
                        live[n] = False


def drain(g):
    for _ in g:
        pass


def pipeline(steps):
    n = len(steps)
    for t in range(n + 2):
        for k in range(3):
            if 0 <= t - k < n:
                steps[t - k][k]()
        yield


def program(nc, D, out):
    Q = Queues()
    put = Q.put
    ctx = ExitStack()

    def sbt(stack, name, cols, dt=F, parts=128):
        return stack.enter_context(nc.sbuf_tensor(name, [parts, cols], dt))

    def sem(name):
        return ctx.enter_context(nc.semaphore(name))

    with ctx:
        XT = sbt(ctx, "XT", 8 * T)
        HH = sbt(ctx, "HH", 8 * T, R)
        HL = sbt(ctx, "HL", 8 * T, R)
        RAW = sbt(ctx, "RAW", 3 * CH)
        WH = sbt(ctx, "WH", 3 * CH, R)
        WL = sbt(ctx, "WL", 3 * CH, R)
        CF = sbt(ctx, "CF", C_N)
        CB = sbt(ctx, "CB", 128 * 5, BF)
        CI = sbt(ctx, "CI", 128 * 8, U8)
        GP = sbt(ctx, "GP", G_N)
        RC = sbt(ctx, "RC", T)
        RSN = sbt(ctx, "RSN", T)
        SQB = sbt(ctx, "SQB", 2 * T)
        ACC = sbt(ctx, "ACC", T)
        RST = sbt(ctx, "RST", T)
        TMP = sbt(ctx, "TMP", 4 * T)
        PB = sbt(ctx, "PB", 6 * T)
        SM = sbt(ctx, "SM", 256)
        LBT = sbt(ctx, "LBT", 64)

        banks = [Slot(ctx.enter_context(nc.psum_tensor(f"bank{i}", [128, 512], F))[:, :]) for i in range(8)]
        sems = {k: sem("s_" + k) for k in ("pe", "act", "dve", "pool", "sp")}
        d_raw = [[sem(f"d_raw{i}"), 0] for i in range(3)]
        d_one = {}

        def dsem(name):
            d_one[name] = [sem("d_" + name), 0]
            return d_one[name]

        ident = CF[:, C_ID:C_ID + 128]
        bones = CF[:, C_BO:C_BO + 128]
        ones = CF[:, C_ON:C_ON + 128]
        perm = CF[:, C_PM:C_PM + 128]
        eps = CF[:, C_EPS:C_EPS + 1]
        identb = CB[:, 0:128]
        m_fl = CB[:, 128:384]
        m_l = CB[:, 256:384]
        m_ul = CB[:, 384:640]

        t_cf = Q.dma("sp", dsem("cf"), CF[:, :], D["c_f"])
        t_gp = Q.dma("sp", dsem("gp"), GP[:, :], D["gp"])
        t_x = [Q.dma("sp", dsem(f"x{m}"), XT[:, m * T:(m + 1) * T], D["xT"][:, m, :]) for m in range(8)]
        t_cb = Q.dma("sp", dsem("cb"), CB[:, :], D["c_b"])

        raw = [RAW[:, i * CH:(i + 1) * CH] for i in range(3)]
        whs = [WH[:, i * CH:(i + 1) * CH] for i in range(3)]
        wls = [WL[:, i * CH:(i + 1) * CH] for i in range(3)]
        units = []
        st = {"load": 0, "split": 0, "use": 0}
        t_load, t_split, t_used = {}, {}, {}

        def pump():
            j = st["use"]
            while st["split"] <= min(j + 2, len(units) - 1):
                load_to(st["split"])
                s = st["split"]
                n = units[s].shape[1]
                i = s % 3
                th = put("act", lambda e, i=i, n=n: e.activation(whs[i][:, 0:n], raw[i][:, 0:n], ACT.Copy),
                         t_load[s], t_used.get(s - 3))
                tl = put("dve", lambda e, i=i, n=n: e.tensor_tensor(
                    wls[i][:, 0:n], raw[i][:, 0:n], whs[i][:, 0:n].bitcast(F), ALU.subtract), th)
                t_split[s] = (th, tl)
                st["split"] += 1
            load_to(min(j + 5, len(units) - 1))

        def load_to(j):
            while st["load"] <= j:
                s = st["load"]
                n = units[s].shape[1]
                t_load[s] = Q.dma("sp", d_raw[s % 3], raw[s % 3][:, 0:n], units[s], t_split.get(s - 3))
                st["load"] += 1

        def next_unit():
            pump()
            j = st["use"]
            st["use"] += 1
            return j, whs[j % 3], wls[j % 3], t_split[j]

        hh = [HH[:, k * T:(k + 1) * T] for k in range(8)]
        hl = [HL[:, k * T:(k + 1) * T] for k in range(8)]
        sqr = Ring([SQB[:, i * T:(i + 1) * T] for i in range(2)])
        tmp = Ring([TMP[:, i * T:(i + 1) * T] for i in range(4)])
        dring = Ring([None, None])
        dring.slots = banks[0:2]
        xt = [XT[:, m * T:(m + 1) * T] for m in range(8)]
        x_tok = [[t] for t in t_x]
        h_busy = [[]]
        acc_st = {"n": 0, "tok": None, "free": []}
        rst_free = [[]]
        last_pe = [None]
        g_tok = [None]

        def three(bank, w, x, first, last, wait, n=None, tok_major=False):
            (wh_, wl_), (xh_, xl_) = w, x
            pairs = ((wh_, xh_), (wh_, xl_), (wl_, xh_))
            t = None
            for k, (a, b) in enumerate(pairs):
                l_, r_ = (b, a) if tok_major else (a, b)
                t = put("pe", lambda e, l_=l_, r_=r_, s=(first and k == 0), p=(last and k == 2): e.matmul(
                    bank, l_, r_, start=s, stop=p), wait if k == 0 else ())
            return t

        def fm(n_m, xs, x_toks, evac, k_units=((0, 8),)):
            for m in range(n_m):
                bank = dring.take()
                tok = None
                for u, (k0, k1) in enumerate(k_units):
                    j, w_h, w_l, w_t = next_unit()
                    for k in range(k0, k1):
                        c = (k - k0) * 128
                        tok = three(bank.ap, (w_h[:, c:c + 128], w_l[:, c:c + 128]), (xs[0][k], xs[1][k]),
                                    k == 0, k == k_units[-1][1] - 1,
                                    [w_t, x_toks[k], bank.free if k == 0 else None])
                    t_used[j] = tok
                evac(m, bank, tok)
                last_pe[0] = tok
                yield

        def tm(ncols, per_unit, x_toks, evac):
            k = 0
            for u in range(8 // per_unit):
                j, w_h, w_l, w_t = next_unit()
                for kk in range(per_unit):
                    c = kk * ncols
                    for i in range(4):
                        tok = three(banks[i].ap[:, 0:ncols], (w_h[:, c:c + ncols], w_l[:, c:c + ncols]),
                                    (hh[k][:, i * 128:(i + 1) * 128], hl[k][:, i * 128:(i + 1) * 128]),
                                    k == 0, k == 7, [w_t, x_toks[k], banks[i].free if k == 0 else None],
                                    tok_major=True)
                        if k == 7:
                            evac(i, banks[i], tok)
                    k += 1
                t_used[j] = tok
                last_pe[0] = tok
                if u < 8 // per_unit - 1:
                    yield
            yield

        def stat_add(m):
            s = sqr.take()
            t = put("act", lambda e: e.activation(s.ap, xt[m], ACT.Square), x_tok[m], s.free)
            x_tok[m] = x_tok[m] + [t]
            if acc_st["n"] == 0:
                acc_st["tok"] = put("pool", lambda e: e.tensor_copy(ACC[:, :], s.ap), t, acc_st["free"])
            else:
                acc_st["tok"] = put("pool", lambda e: e.tensor_tensor(ACC[:, :], ACC[:, :], s.ap, ALU.add),
                                    t, acc_st["tok"])
            s.free = [acc_st["tok"]]
            acc_st["n"] = (acc_st["n"] + 1) % 8

        def rstd_from(bank, tok, scale, dst, dst_free):
            s = tmp.take()
            t1 = put("act", lambda e: e.activation(s.ap, bank.ap, ACT.Ln, bias=eps, scale=scale), tok, s.free)
            bank.free = [t1]
            t2 = put("act", lambda e: e.activation(dst, s.ap, ACT.Exp, scale=-0.5), t1, dst_free)
            s.free = [t2]
            return t2

        def stat_finish():
            b = banks[3]
            t = put("pe", lambda e: e.matmul(b.ap, ones, ACC[:, :], start=True, stop=True),
                    acc_st["tok"], b.free, t_cf)
            acc_st["free"] = [t]
            return rstd_from(b, t, 1.0 / 1024, RST[:, :], rst_free[0])

        def split_to(dh, dl, src, tok, busy):
            th = put("act", lambda e: e.activation(dh, src, ACT.Copy), tok, busy)
            tl = put("dve", lambda e: e.tensor_tensor(dl, src, dh.bitcast(F), ALU.subtract), th, busy)
            return [th, tl]

        def norm_apply(g0, t_rs):
            toks = []
            busy = h_busy[0]
            rst_free[0] = []
            for k in range(8):
                s = tmp.take()
                t = put("dve", lambda e, k=k, s=s: e.scalar_tensor_tensor(
                    s.ap, xt[k], GP[:, g0 + k:g0 + k + 1], RST[:, :], ALU.mult, ALU.mult), t_rs, x_tok[k], s.free, t_gp)
                x_tok[k] = x_tok[k] + [t]
                rst_free[0].append(t)
                pair = split_to(hh[k], hl[k], s.ap, t, busy)
                s.free = pair
                toks.append(pair)
            return toks

        def residual(m, bank, tok, stats):
            t = put("dve", lambda e: e.tensor_tensor(xt[m], bank.ap, xt[m], ALU.add), tok, x_tok[m])
            bank.free = [t]
            x_tok[m] = [t]
            if stats:
                stat_add(m)

        def qk_norm(bank, tok, gcol, rope, dst, dst_free):
            s = sqr.take()
            t0 = put("act", lambda e: e.activation(s.ap, bank.ap, ACT.Square), tok, s.free)
            b3, b2 = banks[3], banks[2]
            t1 = put("pe", lambda e: e.matmul(b3.ap, bones, s.ap, start=True, stop=True), t0, b3.free)
            s.free = [t1]
            r = tmp.take()
            t2 = rstd_from(b3, t1, 1.0 / 64, r.ap, r.free)
            if not rope:
                t3 = put("dve", lambda e: e.scalar_tensor_tensor(
                    dst, bank.ap, gcol, r.ap, ALU.mult, ALU.mult), t2, t0, dst_free, g_tok[0])
                bank.free = [t3]
                r.free = [t3]
                return t3
            n = tmp.take()
            t3 = put("dve", lambda e: e.scalar_tensor_tensor(
                n.ap, bank.ap, gcol, r.ap, ALU.mult, ALU.mult), t2, t0, n.free, g_tok[0])
            bank.free = [t3]
            t4 = put("pe", lambda e: e.matmul(b2.ap, perm, n.ap, start=True, stop=True), t3, b2.free)
            t5 = put("pool", lambda e: e.tensor_tensor(dst, n.ap, RC[:, :], ALU.mult), t3, dst_free, t_rope)
            n.free = [t4, t5]
            t6 = put("dve", lambda e: e.tensor_tensor(r.ap, b2.ap, RSN[:, :], ALU.mult), t4, t_rope, t3)
            b2.free = [t6]
            t7 = put("dve", lambda e: e.tensor_tensor(dst, dst, r.ap, ALU.add), t6, t5)
            r.free = [t7]
            return t7

        def head_norm(bank, tok, gcol, dst, dst_free):
            s = sqr.take()
            t0 = put("act", lambda e: e.activation(s.ap, bank.ap, ACT.Square), tok, s.free)
            b3 = banks[3]
            t1 = put("pe", lambda e: e.matmul(b3.ap, ones, s.ap, start=True, stop=True), t0, b3.free)
            s.free = [t1]
            r = tmp.take()
            t2 = rstd_from(b3, t1, 1.0 / 128, r.ap, r.free)
            t3 = put("dve", lambda e: e.scalar_tensor_tensor(
                dst, bank.ap, gcol, r.ap, ALU.mult, ALU.mult), t2, t0, dst_free, g_tok[0])
            bank.free = [t3]
            r.free = [t3]
            return t3

        ph = ExitStack()
        P1 = sbt(ph, "P1", 40 * T)
        ph.close()

        def p1(a, n):
            return P1[:, a * T:a * T + n]

        ktt = [[p1(2 * b + g, T) for g in range(2)] for b in range(2)]
        qtt = [p1(4 + p, T) for p in range(4)]
        VP, PTC = p1(8, 6 * T), p1(14, 2 * T)
        OM, HV = p1(16, 4 * T), p1(20, 4 * T)
        w1k, w1v = p1(16, 8 * T), p1(24, 8 * T)
        xc = [p1(32, T), p1(33, T)]
        xb = p1(34, 992).rearrange("p (l n) -> p l n", l=32)
        hf, hq, hg = p1(24, 4 * T), p1(28, 4 * T), p1(32, 4 * T)
        h3 = [p1(24 + k, T) for k in range(12)]
        VC = p1(36, T)
        W2, KC, KCT = P1[:, 37 * T:37 * T + 128], P1[:, 37 * T + 128:37 * T + 192], P1[:, 37 * T + 192:37 * T + 320]
        HG = P1[:, 38 * T:38 * T + 256]
        GT = P1[:, 38 * T + 256:38 * T + 352]
        ra, rk, ri = p1(0, T), p1(1, T), p1(2, T)

        t_pos = Q.dma("sp", dsem("pos"), ri.bitcast(I32), D["pos"].partition_broadcast(128))
        t_ci = Q.dma("sp", dsem("ci"), p1(8, 1024), D["c_i"])
        t_w1 = [Q.dma("sp", dsem("w1k"), w1k, D["cmp_w1"][0]), Q.dma("sp", dsem("w1v"), w1v, D["cmp_w1"][1])]
        t_w2 = Q.dma("sp", dsem("w2"), W2, D["cmp_w2"])

        def ffn_units(gu, dn):
            found, j0 = [], 0
            for n in PARTS:
                for j in range(j0, j0 + n):
                    found += [gu[j], gu[22 + j]]
                found += [dn[m, :, j0 * 128:(j0 + n) * 128] for m in range(8)]
                j0 += n
            return found

        for name, n in (("w_in", 8), ("w_ing", 4), ("w_inh", 12), ("w_inv", 4), ("w_out", 8)):
            units += [D[name][u] for u in range(n)]
        units += ffn_units(D["wgu1"], D["wd1"])
        for name, n in (("da_v", 8), ("da_qk", 16), ("da_o", 8)):
            units += [D[name][u] for u in range(n)]
        units += ffn_units(D["wgu2"], D["wd2"])
        for name, n in (("sw_k", 2), ("sw_v", 2), ("sw_q", 8), ("sw_o", 8)):
            units += [D[name][u] for u in range(n)]
        units += ffn_units(D["wgu3"], D["wd3"])

        def rope_tables():
            t = put("dve", lambda e: e.tensor_copy(ra, ri.bitcast(I32)), t_pos)
            t = put("dve", lambda e: e.tensor_scalar(ra, ra, CF[:, C_INV:C_INV + 1], None, ALU.mult), t, t_cf)
            magic = 12582912.0
            c = [6.28125]
            rest = 2 * np.pi - c[0]
            for bits in (7, 7):
                sc = 2.0 ** (bits - 1 - np.floor(np.log2(rest)))
                c.append(float(np.floor(rest * sc) / sc))
                rest -= c[-1]
            c.append(float(rest))
            for big in (4096.0, 1.0):
                t = put("dve", lambda e, big=big: e.tensor_scalar(
                    rk, ra, float(1.0 / (2 * np.pi * big)), magic, ALU.mult, ALU.add), t)
                t = put("dve", lambda e: e.tensor_scalar(rk, rk, -magic, None, ALU.add), t)
                for cc in c:
                    t = put("dve", lambda e, v=-cc * big: e.scalar_tensor_tensor(
                        ra, rk, v, ra, ALU.mult, ALU.add), t)
            pi = 3.1415925
            t = put("dve", lambda e: e.tensor_scalar(ra, ra, -pi, pi, ALU.max, ALU.min), t)
            t1 = put("act", lambda e: e.activation(RSN[:, :], ra, ACT.Sin), t)
            t2 = put("act", lambda e: e.activation(rk, ra, ACT.Abs), t)
            t3 = put("act", lambda e: e.activation(RC[:, :], rk, ACT.Sin, scale=-1.0,
                                                   bias=CF[:, C_HPI:C_HPI + 1]), t2)
            return [t1, t3]

        t_rope = rope_tables()

        for m in range(8):
            stat_add(m)
        h_tok = norm_apply(G_MIX, stat_finish())

        t_xc, t_kt, t_qt = [None, None], {}, [None] * 4
        t_ci = put("pool", lambda e: e.tensor_copy(CI[:, :], p1(8, 1024)), t_ci)
        t_z = put("pool", lambda e: e.memset(VP, 0.0), t_ci)
        t_zc = put("pool", lambda e: e.memset(VC, 0.0))
        t_zk = put("pool", lambda e: e.memset(KC, 0.0))
        t_zg = put("pool", lambda e: e.memset(HG, 0.0))

        def evac_in(m, bank, tok):
            if m < 2:
                t_xc[m] = put("act", lambda e: e.activation(xc[m], bank.ap, ACT.Copy), tok)
                bank.free = [t_xc[m]]
            elif m < 4:
                s = tmp.take()
                t = qk_norm(bank, tok, GP[:, G_KS + m - 2:G_KS + m - 1], False, s.ap, s.free)
                us = []
                for g in range(2):
                    for half in range(2):
                        us.append(put("act", lambda e, g=g, half=half: e.activation(
                            ktt[m - 2][g][64 * half:64 * half + 64, :], s.ap[64 * g:64 * g + 64, :], ACT.Copy),
                            t, t_rope))
                    t_kt[m - 2, g] = us[-2:]
                s.free = us
            else:
                t_qt[m - 4] = qk_norm(bank, tok, gq8[0], False, qtt[m - 4], None)

        t_g8 = put("dve", lambda e: e.tensor_scalar(LBT[:, 32:33], GP[:, G_Q:G_Q + 1], 0.125, None, ALU.mult), t_gp)
        t_g8 = put("dve", lambda e: e.tensor_scalar(LBT[:, 33:34], GP[:, G_DQ:G_DQ + 1], 0.125, None, ALU.mult), t_g8)
        t_g8 = put("dve", lambda e: e.tensor_scalar(LBT[:, 34:35], GP[:, G_SQ:G_SQ + 1], 0.125, None, ALU.mult), t_g8)
        t_g8 = put("dve", lambda e: e.tensor_scalar(LBT[:, 35:36], GP[:, G_SUB:G_SUB + 1], 1.0 - LAMBDA_INIT,
                                                    None, ALU.mult), t_g8)
        gq8 = [LBT[:, 32:33], LBT[:, 33:34], LBT[:, 34:35]]
        g_tok[0] = t_g8

        drain(fm(8, (hh, hl), h_tok, evac_in))

        vp = VP.rearrange("p (i b c) -> p i b c", i=4, b=4)
        t_vp, t_gt = [None] * 4, [None] * 4

        def evac_vg(i, bank, tok):
            t_vp[i] = put("act", lambda e: e.activation(
                vp[:, i, :, 64:128], bank.ap[:, 0:256].rearrange("p (b c) -> p b c", b=4), ACT.Copy), tok, t_z)
            g = GT[:, i * 24:(i + 1) * 24]
            t = put("act", lambda e: e.activation(g, bank.ap[:, 256:280], ACT.Exp, scale=-1.0), tok)
            bank.free = [t_vp[i], t]
            t = put("dve", lambda e: e.tensor_scalar(g, g, 1.0, None, ALU.add), t)
            t_gt[i] = put("dve", lambda e: e.reciprocal(g, g), t)

        drain(tm(280, 2, h_tok, evac_vg))

        t_kc, t_vc = [None, None], []
        xb_free, hg_free = [], [t_zg]
        for kv in range(2):
            w1 = (w1k, w1v)[kv]
            pos0 = (G_PK, G_PV)[kv]
            tb = []
            for r in range(2):
                tb.append(put("dve", lambda e, r=r, kv=kv, pos0=pos0: e.tensor_tensor(
                    xb[:, 16 * r:16 * r + 16, :],
                    xc[kv][:, 16 * r:16 * r + 496].rearrange("p (n l) -> p l n", l=16),
                    GP[:, pos0 + 16 * r:pos0 + 16 * r + 16].unsqueeze(2).to_broadcast([128, 16, 31]),
                    ALU.add), t_xc[kv], t_gp, xb_free))
            tg = []
            for g in range(2):
                bk = banks[4 + g]
                for l in range(32):
                    t = put("pe", lambda e, g=g, l=l, w1=w1, bk=bk: e.matmul(
                        bk.ap[:, 0:31], w1[64 * g:64 * g + 64, l * 128:(l + 1) * 128],
                        xb[64 * g:64 * g + 64, l, :], start=(l == 0), stop=(l == 31)), tb, t_w1[kv], bk.free)
                tg.append(t)
            xb_free = [t]
            tgs = []
            for g in range(2):
                bk = banks[4 + g]
                for r in range(4):
                    tgs.append(put("act", lambda e, bk=bk, r=r, g=g: e.activation(
                        HG[:, g * 128 + r * 32:g * 128 + r * 32 + 31], bk.ap[:, 0:31],
                        ACT.Gelu_apprx_tanh), tg[g], hg_free))
                bk.free = tgs[-4:]
            for g in range(2):
                b6 = banks[6]
                if kv == 0:
                    t = put("pe", lambda e, g=g: e.matmul(
                        b6.ap[0:32, 0:64], HG[:, g * 128:g * 128 + 32], W2[:, 0:64], start=True, stop=True),
                        tgs, t_w2, b6.free)
                    hg_free = [t]
                    o = 8 * g
                    ta = put("act", lambda e, o=o: e.activation(
                        KCT[0:32, 0:64], b6.ap[0:32, 0:64], ACT.Square, accum_out=SM[0:32, o:o + 1]), t, t_kc)
                    ta = put("act", lambda e, o=o: e.activation(
                        SM[0:32, o + 1:o + 2], SM[0:32, o:o + 1], ACT.Ln, bias=eps[0:32, :], scale=1.0 / 64), ta)
                    ta = put("act", lambda e, o=o: e.activation(
                        SM[0:32, o + 2:o + 3], SM[0:32, o + 1:o + 2], ACT.Exp, scale=-0.5), ta)
                    t1 = None
                    for half in range(2):
                        t1 = put("dve", lambda e, o=o, half=half: e.scalar_tensor_tensor(
                            KCT[0:32, 64 * half:64 * half + 64], b6.ap[0:32, 0:64], SM[0:32, o + 2:o + 3],
                            GP[0:32, G_KC:G_KC + 64], ALU.mult, ALU.mult), ta)
                    b7 = banks[7]
                    t2 = put("pe", lambda e: e.transpose(b7.ap[:, 0:32], KCT[0:32, :], ident[0:32, 0:32]), t1, b7.free)
                    b6.free = [t1]
                    t_kc[g] = put("act", lambda e, g=g: e.activation(
                        KC[:, g * 32:g * 32 + 31], b7.ap[:, 0:31], ACT.Copy), t2, t_zk)
                    b7.free = [t_kc[g]]
                else:
                    t = put("pe", lambda e, g=g: e.matmul(
                        b6.ap[:, 0:64], HG[:, g * 128:(g + 1) * 128], W2[:, 64:128], start=True, stop=True),
                        tgs, t_w2, b6.free)
                    cs = []
                    for r in range(4):
                        c = (2 * g + r // 2) * 128 + 64 * (r % 2)
                        cs.append(put("act", lambda e, r=r, c=c: e.activation(
                            VC[32 * r:32 * r + 32, c:c + 64], b6.ap[32 * r:32 * r + 32, 0:64], ACT.Copy), t, t_zc))
                    b6.free = cs
                    t_vc += cs
        t_cmp_pe = xb_free

        pr = Ring([PB[:, i * T:(i + 1) * T] for i in range(4)])
        ptr_ = Ring([PB[:, (4 + i) * T:(5 + i) * T] for i in range(2)])
        t_ptc = []
        for i in range(4):
            for h in range(8):
                half = h % 2
                bk = banks[4 + half]
                t = put("pe", lambda e, h=h, half=half, i=i, bk=bk: e.matmul(
                    bk.ap[:, 32 * (h // 2):32 * (h // 2) + 32], qtt[h // 2][64 * half:64 * half + 64, i * 128:(i + 1) * 128],
                    KC[64 * half:64 * half + 64, 32 * (h // 4):32 * (h // 4) + 32], start=True, stop=True),
                    t_qt[h // 2], t_kc, bk.free)
            p = pr.take()
            p3 = p.ap[:, 0:256].rearrange("p (h n) -> p h n", h=8)
            o = 32 + 32 * (i % 2)
            tms = []
            for half in range(2):
                bk = banks[4 + half]
                tms.append(put("dve", lambda e, i=i, p3=p3, bk=bk, half=half: e.tensor_tensor(
                    p3.rearrange("p (h c) n -> p h c n", c=2)[:, :, half, :],
                    bk.ap[:, 0:128].rearrange("p (h n) -> p h n", h=4),
                    CF[:, C_MC + 32 * i:C_MC + 32 * i + 32].unsqueeze(1).to_broadcast([128, 4, 32]), ALU.add),
                    t, p.free))
                bk.free = [tms[-1]]
            t = tms
            t = put("dve", lambda e, p3=p3, o=o: e.tensor_reduce(SM[:, o:o + 8], p3, AX.X, ALU.max), t)
            t = put("dve", lambda e, p3=p3, o=o: e.tensor_tensor(
                p3, p3, SM[:, o:o + 8].unsqueeze(2).to_broadcast([128, 8, 32]), ALU.subtract), t)
            t = put("act", lambda e, p=p: e.activation(p.ap[:, 0:256], p.ap[:, 0:256], ACT.Exp), t)
            t = put("dve", lambda e, p3=p3, o=o: e.tensor_reduce(SM[:, o + 8:o + 16], p3, AX.X, ALU.add), t)
            t = put("dve", lambda e, o=o: e.reciprocal(SM[:, o + 16:o + 24], SM[:, o + 8:o + 16]), t)
            t = put("dve", lambda e, o=o, i=i: e.scalar_tensor_tensor(
                SM[:, o + 24:o + 32], SM[:, o + 16:o + 24], CF[:, C_VA + i:C_VA + i + 1],
                GT[:, i * 24:(i + 1) * 24].rearrange("p (h c) -> p h c", c=3)[:, :, 0], ALU.mult, ALU.mult),
                t, t_gt[i])
            t = put("dve", lambda e, p3=p3, o=o: e.tensor_tensor(
                p3, p3, SM[:, o + 24:o + 32].unsqueeze(2).to_broadcast([128, 8, 32]), ALU.mult), t)
            b6 = banks[6]
            for g in range(2):
                t2 = put("pe", lambda e, g=g, p=p: e.transpose(
                    b6.ap[:, g * 128:(g + 1) * 128], p.ap[:, g * 128:(g + 1) * 128], ident), t, b6.free)
            p.free = [t2]
            t3 = put("act", lambda e, i=i: e.activation(
                PTC.rearrange("p (g t) -> p g t", g=2)[:, :, i * 128:(i + 1) * 128],
                b6.ap[:, 0:256].rearrange("p (g t) -> p g t", g=2), ACT.Copy), t2)
            b6.free = [t3]
            t_ptc.append(t3)

        sring = Ring([None, None])
        sring.slots = banks[4:6]
        pt_bank, ob = banks[6], banks[7]
        sm_free, sm_n = {}, [0]

        def softmax_stage(lhs, rhs, mask, mcol, n, deps, sink=None):
            bk = sring.take()
            put("pe", lambda e: e.matmul(bk.ap[:, 0:n], lhs, rhs, start=True, stop=False, skip_group_check=True),
                deps, bk.free)
            t = put("pe", lambda e: e.matmul(bk.ap[:, mcol:n], identb, mask, start=False, stop=True,
                                             skip_group_check=True), t_cb)
            o = 96 + 8 * (sm_n[0] % 16)
            sm_n[0] += 1
            p = pr.take()
            t1 = put("dve", lambda e: e.tensor_reduce(SM[:, o:o + 1], bk.ap[:, 0:n], AX.X, ALU.max, negate=True),
                     t, sm_free.get(o))
            t_sink = None
            if sink is not None:
                t1 = put("dve", lambda e: e.tensor_scalar(SM[:, o:o + 1], SM[:, o:o + 1], sink[1], None, ALU.min),
                         t1, sink[2])
            t2 = put("act", lambda e: e.activation(p.ap[:, 0:n], bk.ap[:, 0:n], ACT.Exp, bias=SM[:, o:o + 1],
                                                   accum_out=SM[:, o + 1:o + 2]), t1, p.free)
            bk.free = [t2]
            if sink is not None:
                t_sink = put("act", lambda e: e.activation(SM[:, o + 3:o + 4], sink[0], ACT.Exp,
                                                           bias=SM[:, o:o + 1]), t1)
            return p, o, [t2, t_sink]

        def turn(p, blocks, tok):
            n = len(blocks) * 128
            for k, j in enumerate(blocks):
                t = put("pe", lambda e, j=j, k=k: e.transpose(
                    pt_bank.ap[:, k * 128:(k + 1) * 128], p.ap[:, j * 128:(j + 1) * 128], ident), tok, pt_bank.free)
            p.free = [t]
            s = ptr_.take()
            t2 = put("act", lambda e: e.activation(s.ap[:, 0:n], pt_bank.ap[:, 0:n], ACT.Copy), t, s.free)
            pt_bank.free = [t2]
            return s, t2

        t_om = [None] * 4

        def nsa_step(h, b, i):
            pair, half, g = h // 2, h % 2, h // 4
            n = (i + 1) * 128
            z = {}

            def scores():
                z["p"], z["o"], z["t"] = softmax_stage(
                    qtt[pair][64 * half:64 * half + 64, i * 128:(i + 1) * 128],
                    ktt[b][g][64 * half:64 * half + 64, 0:n], m_l, i * 128, n, [t_qt[pair], t_kt[b, g]])

            def weights():
                o, p = z["o"], z["p"]
                gate = GT[:, i * 24 + 3 * h + 1 + b:i * 24 + 3 * h + 2 + b]
                t = put("dve", lambda e: e.reciprocal(SM[:, o + 2:o + 3], SM[:, o + 1:o + 2]), z["t"])
                t = put("dve", lambda e: e.tensor_scalar(
                    p.ap[:, 0:n], p.ap[:, 0:n], SM[:, o + 2:o + 3], gate, ALU.mult, ALU.mult), t, t_gt[i])
                sm_free[o] = [t]
                z["s"], z["t2"] = turn(p, range(i + 1), t)

            def values():
                if half == 0 and b == 0 and i == 0:
                    cc = (2 * g + pair % 2) * 128
                    put("pe", lambda e: e.matmul(ob.ap, VC[:, cc:cc + 128], PTC[:, g * T:(g + 1) * T],
                                                 start=True, stop=False, skip_group_check=True),
                        t_vc, t_ptc, ob.free)
                last = half == 1 and b == 1 and i == 3
                for j in range(i + 1):
                    v = vp[:, j, 2 * b + g, :]
                    v = v[:, 64:192] if half == 0 else v[:, 0:128]
                    t = put("pe", lambda e, j=j, v=v: e.matmul(
                        ob.ap[:, i * 128:(i + 1) * 128], v, z["s"].ap[:, j * 128:(j + 1) * 128],
                        start=False, stop=(last and j == i), skip_group_check=True), z["t2"], t_vp)
                z["s"].free = [t]
                if last:
                    t_om[pair] = put("act", lambda e: e.activation(OM[:, pair * T:(pair + 1) * T], ob.ap, ACT.Copy),
                                     t, t_cmp_pe)
                    ob.free = [t_om[pair]]
            return scores, weights, values

        t_h3, t_hv = [None] * 12, [None] * 4

        def evac_h(m, bank, tok):
            t_h3[m] = put("act", lambda e: e.activation(h3[m], bank.ap, ACT.Copy), tok, t_cmp_pe)
            bank.free = [t_h3[m]]

        def evac_hv(i, bank, tok):
            t_hv[i] = put("act", lambda e: e.activation(HV[:, i * T:(i + 1) * T], bank.ap, ACT.Copy), tok, t_cmp_pe)
            bank.free = [t_hv[i]]

        def hgrn_proj():
            yield from fm(12, (hh, hl), h_tok, evac_h)
            yield from tm(512, 2, h_tok, evac_hv)

        interleave(pipeline([nsa_step(h, b, i) for h in range(8) for b in range(2) for i in range(4)]),
                   hgrn_proj(), 4, 1)
        h_busy[0] = [last_pe[0]]
        fence = fence_of(Q)
        mix_tok = [split_to(hh[k], hl[k], OM[:, k * T:(k + 1) * T], t_om[k], h_busy[0]) for k in range(4)]

        Bc, Kk, E1, E2, KH, ATD = p1(0, 4 * T), p1(4, 4 * T), p1(8, 4 * T), p1(12, 4 * T), hf, p1(36, 4 * T)
        t_f, t_q, t_g = [], [], []
        for h in range(4):
            s = slice(h * T, (h + 1) * T)
            t_f.append(put("act", lambda e, s=s: e.activation(hf[:, s], hf[:, s], ACT.Sigmoid), t_h3))
            t = put("act", lambda e, s=s: e.activation(E1[:, s], hq[:, s], ACT.Sigmoid), fence)
            t_q.append(put("dve", lambda e, s=s: e.tensor_tensor(hq[:, s], hq[:, s], E1[:, s], ALU.mult), t))
            t = put("act", lambda e, s=s: e.activation(E2[:, s], hg[:, s], ACT.Sigmoid), fence)
            t_g.append(put("dve", lambda e, s=s: e.tensor_tensor(hg[:, s], hg[:, s], E2[:, s], ALU.mult), t))
        l0, l1 = GP[:, G_LB:G_LB + 4], GP[:, G_LB + 4:G_LB + 8]
        t = put("dve", lambda e: e.tensor_tensor(LBT[:, 0:4], l0, l1, ALU.max), t_gp)
        ta = put("dve", lambda e: e.tensor_tensor(LBT[:, 4:8], l0, LBT[:, 0:4], ALU.subtract), t)
        tb = put("dve", lambda e: e.tensor_tensor(LBT[:, 8:12], l1, LBT[:, 0:4], ALU.subtract), t)
        t = put("act", lambda e: e.activation(LBT[:, 4:12], LBT[:, 4:12], ACT.Exp), ta, tb)
        t = put("dve", lambda e: e.tensor_tensor(LBT[:, 0:4], LBT[:, 4:8], LBT[:, 8:12], ALU.add), t)
        t = put("dve", lambda e: e.reciprocal(LBT[:, 0:4], LBT[:, 0:4]), t)
        t = put("dve", lambda e: e.tensor_tensor(LBT[:, 12:16], LBT[:, 4:8], LBT[:, 0:4], ALU.mult), t)
        t_lb = put("dve", lambda e: e.tensor_scalar(LBT[:, 16:20], LBT[:, 12:16], -1.0, 1.0, ALU.mult, ALU.add), t)
        t_k, t_b = [], []
        for h in range(4):
            s = slice(h * T, (h + 1) * T)
            t = put("dve", lambda e, s=s, h=h: e.tensor_scalar(
                hf[:, s], hf[:, s], LBT[:, 16 + h:17 + h], LBT[:, 12 + h:13 + h], ALU.mult, ALU.add), t_f[h], t_lb)
            tk = put("dve", lambda e, s=s: e.tensor_scalar(Kk[:, s], hf[:, s], -1.0, 1.0, ALU.mult, ALU.add),
                     t, fence)
            t_k.append(tk)
            t = put("act", lambda e, s=s: e.activation(hf[:, s], hf[:, s], ACT.Ln), tk)
            t_b.append(put("dve", lambda e, s=s: e.tensor_tensor_scan(
                Bc[:, s], CF[:, C_RM:C_RM + T], hf[:, s], 0.0, ALU.mult, ALU.add), t, fence))

        atd = [ATD[:, i * T:(i + 1) * T].rearrange("p (h t) -> p h t", h=4) for i in range(4)]
        aring = Ring([None] * 4)
        aring.slots = banks[4:8]
        t_atd = []
        for i in range(4):
            bk = aring.take()
            for h in range(4):
                c = h * T + i * 128
                t = put("pe", lambda e, h=h, c=c, bk=bk: e.matmul(
                    bk.ap[:, h * 128:(h + 1) * 128], Kk[:, c:c + 128], hq[:, c:c + 128], start=True, stop=True),
                    t_k[h], t_q[h], bk.free)
            t = put("dve", lambda e, i=i, bk=bk: e.tensor_tensor(
                atd[i], bk.ap.rearrange("p (h t) -> p h t", h=4),
                ident.unsqueeze(1).to_broadcast([128, 4, 128]), ALU.mult), t, fence)
            bk.free = [t]
            t_atd.append(t)
        ebuf = [Slot(E1), Slot(E2)]
        ebuf[0].free, ebuf[1].free = list(t_q), list(t_g)
        for lv in range(7):
            m = 1 << lv
            eb = ebuf[lv % 2]
            v = eb.ap.rearrange("p (n c) -> p n c", c=2 * m)
            b3 = Bc.rearrange("p (n c) -> p n c", c=2 * m)
            k3 = Kk.rearrange("p (n c) -> p n c", c=2 * m)
            q3 = hq.rearrange("p (n c) -> p n c", c=2 * m)
            nb = 2048 // (2 * m)
            edge = b3[:, :, m - 1:m].to_broadcast([128, nb, m])
            t1 = put("dve", lambda e, v=v, b3=b3, edge=edge, m=m: e.tensor_tensor(
                v[:, :, 0:m], edge, b3[:, :, 0:m], ALU.subtract), t_b, eb.free)
            if m < 64:
                t2 = put("dve", lambda e, v=v, b3=b3, edge=edge, m=m: e.tensor_tensor(
                    v[:, :, m:2 * m], b3[:, :, m:2 * m], edge, ALU.subtract), t_b, eb.free)
            else:
                t2 = put("dve", lambda e, v=v, b3=b3, m=m: e.tensor_copy(v[:, :, m:2 * m], b3[:, :, m:2 * m]),
                         t_b, eb.free)
            t = put("act", lambda e, eb=eb: e.activation(eb.ap, eb.ap, ACT.Exp), t1, t2)
            ta = put("dve", lambda e, v=v, k3=k3, m=m: e.tensor_tensor(
                v[:, :, 0:m], v[:, :, 0:m], k3[:, :, 0:m], ALU.mult), t, t_k)
            tb = put("dve", lambda e, v=v, q3=q3, m=m: e.tensor_tensor(
                v[:, :, m:2 * m], v[:, :, m:2 * m], q3[:, :, m:2 * m], ALU.mult), t, t_q)
            for i in range(4):
                bk = aring.take()
                for h in range(4):
                    c = h * T + i * 128
                    t = put("pe", lambda e, h=h, c=c, bk=bk, eb=eb: e.matmul(
                        bk.ap[:, h * 128:(h + 1) * 128], eb.ap[:, c:c + 128], eb.ap[:, c:c + 128],
                        start=True, stop=True), ta, tb, bk.free)
                t_atd[i] = put("dve", lambda e, i=i, bk=bk, lv=lv: e.copy_predicated(
                    atd[i], CI[:, lv * 128:(lv + 1) * 128].unsqueeze(1).to_broadcast([128, 4, 128]),
                    bk.ap.rearrange("p (h t) -> p h t", h=4)), t, t_ci, t_atd[i])
                bk.free = [t_atd[i]]
            eb.free = [t]
        b16 = Bc.rearrange("p (n c) -> p n c", c=128)
        t = put("dve", lambda e: e.tensor_tensor(
            b16[:, :, 64:128], b16[:, :, 64:128], b16[:, :, 63:64].to_broadcast([128, 16, 64]), ALU.add), t2, t1)
        kh16 = KH.rearrange("p (n c) -> p n c", c=128)
        tk = put("dve", lambda e: e.tensor_tensor(
            kh16, b16[:, :, 127:128].to_broadcast([128, 16, 128]), b16, ALU.subtract), t, t_b)
        tk = put("act", lambda e: e.activation(KH, KH, ACT.Exp), tk)
        tk = put("dve", lambda e: e.tensor_tensor(KH, KH, Kk, ALU.mult), tk)
        EB = LBT[:, 40:56].rearrange("p (h i) -> p h i", h=4)
        te = put("act", lambda e: e.activation(LBT[:, 40:56], b16[:, :, 127], ACT.Exp), t)
        tq = put("act", lambda e: e.activation(E1, Bc, ACT.Exp), t, ebuf[0].free)
        tq = put("dve", lambda e: e.tensor_tensor(E1, E1, hq, ALU.mult), tq)
        ks_ = {}
        for h in range(4):
            for n, (j, i) in enumerate(((0, 2), (0, 3), (1, 3))):
                dst = E2[:, (3 * h + n) * 128:(3 * h + n + 1) * 128]
                src = KH[:, h * T + j * 128:h * T + (j + 1) * 128]
                s1 = EB[:, h, j + 1:j + 2]
                s2 = EB[:, h, j + 2:j + 3] if i - j == 3 else None
                tt_ = put("dve", lambda e, dst=dst, src=src, s1=s1, s2=s2: (
                    e.tensor_scalar(dst, src, s1, s2, ALU.mult, ALU.mult) if s2 is not None
                    else e.tensor_scalar(dst, src, s1, None, ALU.mult)), tk, te, ebuf[1].free)
                ks_[h, j, i] = (dst, tt_)
            for j in range(3):
                ks_[h, j, j + 1] = (KH[:, h * T + j * 128:h * T + (j + 1) * 128], tk)
        arr = Ring([PB[:, k * T:(k + 1) * T] for k in range(4)])
        for k in range(4):
            arr.slots[k].free = pr.slots[k].free
        b4 = Ring([None] * 2)
        b4.slots = banks[4:6]
        obr = Ring([None] * 2)
        obr.slots = banks[6:8]
        for h in range(4):
            o_b = obr.take()
            for i in range(4):
                if i:
                    bk = b4.take()
                    for j in range(i):
                        kk_, tt_ = ks_[h, j, i]
                        c = h * T + i * 128
                        t = put("pe", lambda e, j=j, kk_=kk_, c=c, bk=bk: e.matmul(
                            bk.ap[:, j * 128:(j + 1) * 128], kk_, E1[:, c:c + 128], start=True, stop=True),
                            tt_, tq, bk.free)
                    s = arr.take()
                    ts_ = put("act", lambda e, s=s, i=i, bk=bk: e.activation(
                        s.ap[:, 0:i * 128], bk.ap[:, 0:i * 128], ACT.Copy), t, s.free)
                    bk.free = [ts_]
                for j in range(i + 1):
                    rhs = s.ap[:, j * 128:(j + 1) * 128] if j < i else atd[i][:, h, :]
                    t = put("pe", lambda e, i=i, j=j, h=h, rhs=rhs, o_b=o_b: e.matmul(
                        o_b.ap[:, i * 128:(i + 1) * 128], HV[:, j * T + h * 128:j * T + (h + 1) * 128], rhs,
                        start=(i == 0 and j == 0), stop=(i == 3 and j == 3), skip_group_check=True),
                        ts_ if i else None, t_atd[i], t_hv, o_b.free)
                if i:
                    s.free = [t]
            dst = h3[h + 4]
            t1 = head_norm(o_b, t, GP[:, G_HO:G_HO + 1], dst, [tq, t_q])
            t1 = put("dve", lambda e, dst=dst, h=h: e.tensor_tensor(dst, dst, hg[:, h * T:(h + 1) * T], ALU.mult),
                     t1, t_g[h])
            mix_tok.append(split_to(hh[4 + h], hl[4 + h], dst, t1, h_busy[0]))
        for k in range(4):
            pr.slots[k].free = arr.slots[k].free

        def out_proj(tok8):
            dring.slots = banks[0:3]
            drain(fm(8, (hh, hl), tok8, lambda m, bank, tok: residual(m, bank, tok, True)))
            h_busy[0] = [last_pe[0]]

        out_proj(mix_tok)

        def ffn(name, g0, fence, last):
            h_tok = norm_apply(g0, stat_finish())
            st_ = ExitStack()
            FH = sbt(st_, "FH" + name, 8 * T, R)
            FL = sbt(st_, "FL" + name, 8 * T, R)
            st_.close()
            fh = [FH[:, k * T:(k + 1) * T] for k in range(8)]
            fl = [FL[:, k * T:(k + 1) * T] for k in range(8)]
            dring.slots = [banks[0], banks[1], banks[4], banks[5]]
            busy = [fence]
            for part, n in enumerate(PARTS):
                toks, keep = [], {}

                def evac(m, bank, tok, toks=toks, keep=keep, busy=busy):
                    if m % 2 == 0:
                        s = tmp.take()
                        t = put("act", lambda e: e.activation(s.ap, bank.ap, ACT.Silu), tok, s.free)
                        bank.free = [t]
                        keep["s"], keep["t"] = s, t
                    else:
                        s, t0, k = keep["s"], keep["t"], m // 2
                        t = put("dve", lambda e: e.tensor_tensor(s.ap, bank.ap, s.ap, ALU.mult), tok, t0)
                        bank.free = [t]
                        pair = split_to(fh[k], fl[k], s.ap, t, busy[0])
                        s.free = pair
                        toks.append(pair)
                drain(fm(2 * n, (hh, hl), h_tok, evac))
                if part == 2:
                    h_busy[0] = [last_pe[0]]

                def evac_d(m, bank, tok, part=part):
                    residual(m, bank, tok, part == 2 and not last)
                    if part == 2 and last:
                        t_out.append(Q.dma("sp", dsem(f"out{m}"), out[:, m, :], xt[m], x_tok[m]))
                drain(fm(8, (fh, fl), toks, evac_d, ((0, n),)))
                busy = [[last_pe[0]]]
            return fence_of(Q)

        t_out = []
        fence = ffn("a", G_FFN, fence_of(Q), False)

        ph = ExitStack()
        P2 = sbt(ph, "P2", 20 * T)
        ph.close()
        VD, OM2 = P2[:, 0:8 * T], P2[:, 8 * T:16 * T]
        qr = Ring([P2[:, (16 + k) * T:(17 + k) * T] for k in range(2)])
        kr = Ring([P2[:, (18 + k) * T:(19 + k) * T] for k in range(2)])
        for s in qr.slots + kr.slots:
            s.free = [fence]
        h_tok = norm_apply(G_AT0, stat_finish())
        lam = LBT[:, 60:61]
        lp = GP[:, G_LAM:G_LAM + 256]
        tl = []
        for k in range(2):
            t = put("dve", lambda e, k=k: e.tensor_tensor(
                SM[:, 64 * k:64 * k + 64], lp[:, 128 * k:128 * k + 64], lp[:, 128 * k + 64:128 * k + 128], ALU.mult),
                fence, t_gp)
            tl.append(put("dve", lambda e, k=k: e.tensor_reduce(
                LBT[:, 56 + k:57 + k], SM[:, 64 * k:64 * k + 64], AX.X, ALU.add), t))
        t = put("act", lambda e: e.activation(LBT[:, 58:60], LBT[:, 56:58], ACT.Exp), tl)
        t = put("dve", lambda e: e.tensor_tensor(lam, LBT[:, 59:60], LBT[:, 58:59], ALU.subtract), t)
        t_lam = put("dve", lambda e: e.tensor_scalar(lam, lam, -LAMBDA_INIT, None, ALU.add), t)
        sm_free.clear()

        t_vd = []
        for half_ in range(2):
            def evac_v(i, bank, tok, half_=half_):
                c = i * 1024 + half_ * 512
                t = put("act", lambda e: e.activation(VD[:, c:c + 512], bank.ap, ACT.Copy), tok, fence)
                bank.free = [t]
                t_vd.append(t)
            drain(tm(512, 2, h_tok, evac_v))

        heads = {}

        def evac_qk(m, bank, tok):
            ring, gc = (qr, gq8[1]) if m % 2 == 0 else (kr, GP[:, G_DK:G_DK + 1])
            s = ring.take()
            heads[m] = (s, qk_norm(bank, tok, gc, True, s.ap, s.free))

        t_om2 = [None] * 8

        def da_step(hd, i):
            n = (i + 1) * 128
            z = {}

            def scores():
                (qs, tq_), (ks, tk_) = heads[2 * hd], heads[2 * hd + 1]
                for c in range(2):
                    z[c] = softmax_stage(qs.ap[64 * c:64 * c + 64, i * 128:(i + 1) * 128],
                                         ks.ap[64 * c:64 * c + 64, 0:n], m_l, i * 128, n, [tq_, tk_])
                if i == 3:
                    last = Q.q["pe"][-1][2]
                    qs.free, ks.free = [last], [last]

            def weights():
                (p0, o0, t0), (p1_, o1, t1) = z[0], z[1]
                ta = put("dve", lambda e: e.reciprocal(SM[:, o0 + 2:o0 + 3], SM[:, o0 + 1:o0 + 2]), t0)
                tb = put("dve", lambda e: e.reciprocal(SM[:, o1 + 2:o1 + 3], SM[:, o1 + 1:o1 + 2]), t1)
                tb = put("dve", lambda e: e.tensor_scalar(
                    p1_.ap[:, 0:n], p1_.ap[:, 0:n], SM[:, o1 + 2:o1 + 3], lam, ALU.mult, ALU.mult), tb, t_lam)
                t = put("dve", lambda e: e.scalar_tensor_tensor(
                    p0.ap[:, 0:n], p0.ap[:, 0:n], SM[:, o0 + 2:o0 + 3], p1_.ap[:, 0:n], ALU.mult, ALU.add), ta, tb)
                sm_free[o0], sm_free[o1] = [t], [t]
                p1_.free = [t]
                z["s"], z["t2"] = turn(p0, range(i + 1), t)

            def values():
                for j in range(i + 1):
                    t = put("pe", lambda e, j=j: e.matmul(
                        ob.ap[:, i * 128:(i + 1) * 128], VD[:, j * 1024 + hd * 128:j * 1024 + (hd + 1) * 128],
                        z["s"].ap[:, j * 128:(j + 1) * 128], start=(i == 0), stop=(i == 3 and j == 3),
                        skip_group_check=True), z["t2"], t_vd, ob.free)
                z["s"].free = [t]
                if i == 3:
                    t_om2[hd] = head_norm(ob, t, LBT[:, 35:36], OM2[:, hd * T:(hd + 1) * T], fence)
            return scores, weights, values

        dring.slots = banks[0:2]
        att = pipeline([da_step(hd, i) for hd in range(8) for i in range(4)])
        prj = fm(16, (hh, hl), h_tok, evac_qk)
        next(prj)
        next(prj)
        for hd in range(1, 8):
            for _ in range(2):
                next(prj)
                next(att)
                next(att)
        drain(prj)
        h_busy[0] = [last_pe[0]]
        drain(att)
        fence = fence_of(Q)
        out_proj([split_to(hh[k], hl[k], OM2[:, k * T:(k + 1) * T], t_om2[k], h_busy[0]) for k in range(8)])
        fence = ffn("b", G_F0, fence_of(Q), False)

        ph = ExitStack()
        P3 = sbt(ph, "P3", 23 * T)
        ph.close()
        KW = P3[:, 0:4 * 640].rearrange("p (k t) -> p k t", k=4)
        VW = P3[:, 5 * T:11 * T].rearrange("p (i k c) -> p i k c", i=4, k=4)
        OM3 = P3[:, 11 * T:19 * T]
        qw = Ring([P3[:, (19 + k) * T:(20 + k) * T] for k in range(3)])
        for s in qw.slots:
            s.free = [fence]
        t_zp = put("pool", lambda e: e.memset(P3[:, 0:11 * T], 0.0), fence)
        t_rs = stat_finish()
        h_tok = norm_apply(G_KV, t_rs)
        NS = SM[:, 64:80]
        t_ns = put("dve", lambda e: e.tensor_scalar(NS, GP[:, G_SINK:G_SINK + 16], -1.0, None, ALU.mult), fence)
        t_kw, t_vw = {}, []

        def evac_k(m, bank, tok):
            s = tmp.take()
            t = qk_norm(bank, tok, GP[:, G_SK:G_SK + 1], True, s.ap, s.free)
            us = []
            for a in range(2):
                for half in range(2):
                    us.append(put("act", lambda e, a=a, half=half: e.activation(
                        KW[64 * half:64 * half + 64, 2 * m + a, 128:640], s.ap[64 * a:64 * a + 64, :], ACT.Copy),
                        t, t_zp))
                t_kw[2 * m + a] = us[-2:]
            s.free = us

        def evac_vw(i, bank, tok):
            t = put("act", lambda e: e.activation(
                VW[:, i, :, 64:128], bank.ap[:, 0:256].rearrange("p (k c) -> p k c", k=4), ACT.Copy), tok, t_zp)
            bank.free = [t]
            t_vw.append(t)

        dring.slots = banks[0:2]
        drain(fm(2, (hh, hl), h_tok, evac_k))
        drain(tm(256, 4, h_tok, evac_vw))
        h_busy[0] = [last_pe[0]]
        h_tok = norm_apply(G_AT1, t_rs)
        pairs = {}

        def evac_qw(m, bank, tok):
            s = qw.take()
            pairs[m] = (s, qk_norm(bank, tok, gq8[2], True, s.ap, s.free))

        t_om3 = [None] * 8

        def sw_step(h, i):
            pair, half, kv = h // 2, h % 2, h // 4
            z = {}

            def scores():
                qs, tq_ = pairs[pair]
                z["p"], z["o"], z["t"] = softmax_stage(
                    qs.ap[64 * half:64 * half + 64, i * 128:(i + 1) * 128],
                    KW[64 * half:64 * half + 64, kv, i * 128:i * 128 + 256], m_ul if i else m_fl, 0, 256,
                    [tq_, t_kw[kv], t_zp], (GP[:, G_SINK + h:G_SINK + h + 1], NS[:, h:h + 1], t_ns))
                if half == 1 and i == 3:
                    qs.free = [Q.q["pe"][-1][2]]

            def weights():
                o, p = z["o"], z["p"]
                t = put("dve", lambda e: e.tensor_tensor(
                    SM[:, o + 2:o + 3], SM[:, o + 1:o + 2], SM[:, o + 3:o + 4], ALU.add), z["t"])
                t = put("dve", lambda e: e.reciprocal(SM[:, o + 4:o + 5], SM[:, o + 2:o + 3]), t)
                t = put("dve", lambda e: e.tensor_scalar(p.ap[:, 0:256], p.ap[:, 0:256], SM[:, o + 4:o + 5],
                                                         None, ALU.mult), t)
                sm_free[o] = [t]
                z["s"], z["t2"] = turn(p, (0, 1) if i else (1,), t)

            def values():
                js = (i - 1, i) if i else (0,)
                for k, j in enumerate(js):
                    v = VW[:, j, kv, :]
                    v = v[:, 64:192] if half == 0 else v[:, 0:128]
                    t = put("pe", lambda e, k=k, v=v: e.matmul(
                        ob.ap[:, i * 128:(i + 1) * 128], v, z["s"].ap[:, k * 128:(k + 1) * 128],
                        start=(half == 0 and i == 0), stop=(half == 1 and i == 3 and k == 1),
                        skip_group_check=True), z["t2"], t_vw, t_zp, ob.free)
                z["s"].free = [t]
                if half == 1 and i == 3:
                    t_om3[pair] = put("act", lambda e: e.activation(
                        OM3[:, pair * T:(pair + 1) * T], ob.ap, ACT.Copy), t, fence)
                    ob.free = [t_om3[pair]]
            return scores, weights, values

        att = pipeline([sw_step(h, i) for h in range(16) for i in range(4)])
        prj = fm(8, (hh, hl), h_tok, evac_qw)
        next(prj)
        for pair in range(1, 8):
            next(prj)
            for _ in range(8):
                next(att)
        drain(prj)
        h_busy[0] = [last_pe[0]]
        drain(att)
        out_proj([split_to(hh[k], hl[k], OM3[:, k * T:(k + 1) * T], t_om3[k], h_busy[0]) for k in range(8)])
        ffn("c", G_F1, fence_of(Q), True)

        Q.count()
        block = ctx.enter_context(nc.Block())

        @block.sync
        def _(e):
            Q.emit("sp", e, sems)
            for t in t_out:
                e.wait_ge(t.eng, t.val)

        @block.gpsimd
        def _(e):
            Q.emit("pool", e, sems)

        @block.scalar
        def _(e):
            Q.emit("act", e, sems)

        @block.vector
        def _(e):
            Q.emit("dve", e, sems)

        @block.tensor
        def _(e):
            Q.emit("pe", e, sems)


def constants():
    p = np.arange(128)
    cf = np.zeros((128, C_N), np.float32)
    cf[:, C_ID:C_ID + 128] = np.eye(128)
    cf[:, C_BO:C_BO + 128] = (p[:, None] // 64) == (p[None, :] // 64)
    cf[:, C_ON:C_ON + 128] = 1.0
    for d in range(128):
        if d % 64 < 32:
            cf[d + 32, C_PM + d] = -1.0
        else:
            cf[d - 32, C_PM + d] = 1.0
    end = np.arange(32) * 16 + 31
    for i in range(4):
        t = i * 128 + p
        cf[:, C_MC + 32 * i:C_MC + 32 * i + 32] = np.where(end[None, :] <= t[:, None], 0.0, -1e30)
        cf[:, C_MC + 32 * i + 31] = -1e30
        cf[:, C_VA + i] = t >= 31
    inv = (np.float32(1.0) / (np.float32(10000.0) ** (np.arange(0, 64, 2, dtype=np.float32) / np.float32(64))))
    cf[:, C_INV] = inv.astype(np.float32)[p % 32]
    cf[:, C_EPS] = EPS
    cf[:, C_HPI] = np.pi / 2
    cf[:, C_RM:C_RM + 512] = (np.arange(512) % 64 != 0)[None, :]
    cb = np.zeros((128, 640), np.float32)
    cb[:, 0:128] = np.eye(128)
    cb[:, 128:256] = -1e30
    low = np.where(p[None, :] <= p[:, None], 0.0, -1e30)
    cb[:, 256:384] = low
    cb[:, 384:512] = np.where(p[None, :] > p[:, None], 0.0, -1e30)
    cb[:, 512:640] = low
    ci = np.zeros((128, 8 * 128), np.float32)
    for lv in range(7):
        m = 1 << lv
        s, t = p[:, None], p[None, :]
        ci[:, lv * 128:(lv + 1) * 128] = (s // (2 * m) == t // (2 * m)) & (s % (2 * m) < m) & (t % (2 * m) >= m)
    return cf, cb, ci


def kernel(**inputs):
    import ml_dtypes
    import concourse.bacc as _bacc
    from concourse.bass_utils import run_bass_kernel_spmd as _run

    a = {k: np.asarray(v) for k, v in inputs.items()}

    def cols(w, n):
        k, m = w.shape
        return w.reshape(k // 128, 128, m // n, n).transpose(2, 1, 0, 3).reshape(m // n, 128, (k // 128) * n)

    def rows(w, per):
        k, m = w.shape
        return w.reshape(k // 128 // per, per, 128, m).transpose(0, 2, 1, 3).reshape(k // 128 // per, 128, per * m)

    cf, cb, ci = constants()
    w = a["w_in"][0]
    o = [0]
    for s in (512, 128, 128, 128, 128, 128, 128, 24, 512, 512, 512, 512):
        o.append(o[-1] + s)
    part = [w[:, o[i]:o[i + 1]] for i in range(12)]
    wq, wkc, wvc, wks, wvs, wkw, wvw, wg, whq, whf, whi, whg = part
    D = {"c_f": cf, "c_b": cb.astype(ml_dtypes.bfloat16), "c_i": ci}
    D["xT"] = a["x"][0].reshape(512, 8, 128).transpose(2, 1, 0)
    D["pos"] = a["positions_2"].reshape(512)
    D["w_in"] = cols(np.concatenate([wkc, wvc, wks, wkw, wq], 1), 128)
    D["w_ing"] = rows(np.concatenate([wvs, wvw, wg], 1), 2)
    D["w_inh"] = cols(np.concatenate([whf, whq, whg], 1), 128)
    D["w_inv"] = rows(whi, 2)
    D["w_out"] = cols(a["w_out"][0], 128)
    for n, gu, dn in ((1, a["w_gate_up"][0], a["w_down"][0]), (2, a["w_gate_up_2"][0], a["w_down_2"][0]),
                      (3, a["w_gate_up_2"][1], a["w_down_2"][1])):
        D[f"wgu{n}"] = cols(gu, 128)
        D[f"wd{n}"] = cols(dn, 128)
    qkv = a["da_w_qkv_2"][0]
    D["da_v"] = np.concatenate([rows(qkv[:, 2048:2560], 2), rows(qkv[:, 2560:3072], 2)], 0)
    qk = np.stack([qkv[:, 0:1024].reshape(1024, 8, 128), qkv[:, 1024:2048].reshape(1024, 8, 128)], 2)
    D["da_qk"] = cols(qk.reshape(1024, 2048), 128)
    D["da_o"] = cols(a["da_w_o_2"][0], 128)
    D["sw_k"] = cols(a["w_kv_2"][:, 0:256], 128)
    D["sw_v"] = rows(a["w_kv_2"][:, 256:512], 4)
    D["sw_q"] = cols(a["sw_w_q_2"][0], 128)
    D["sw_o"] = cols(a["sw_w_o_2"][0], 128)
    w1 = [a[n][0].reshape(32, 64, 128).transpose(1, 0, 2).reshape(64, 4096) for n in ("cmp_k_w1", "cmp_v_w1")]
    D["cmp_w1"] = np.stack([np.concatenate([v, v], 0) for v in w1], 0)
    D["cmp_w2"] = np.concatenate([a["cmp_k_w2"][0], a["cmp_v_w2"][0]], 1)

    def g8(v):
        return v.reshape(8, 128).T

    def col(v):
        v = v.reshape(-1, 1)
        return np.concatenate([v, v], 0) if v.shape[0] == 64 else v

    def line(v):
        return np.broadcast_to(v.reshape(1, -1), (128, v.size))

    lb = a["hgrn_lb_logits"].reshape(2, 4, 128).transpose(2, 0, 1).reshape(128, 8)
    pk = [np.concatenate([a[n][0].T, a[n][0].T], 0) for n in ("cmp_pos_k", "cmp_pos_v")]
    D["gp"] = np.concatenate([
        g8(a["norm_mix"][0]), g8(a["norm_ffn"][0]), g8(a["attn_norm_2"][0]), g8(a["attn_norm_2"][1]),
        g8(a["ffn_norm_2"][0]), g8(a["ffn_norm_2"][1]), g8(a["kv_norm_2"]),
        col(a["q_norm"][0]), col(a["k_norm"][0, 1]), col(a["k_norm"][0, 2]), col(a["da_q_norm_2"][0]),
        col(a["da_k_norm_2"][0]), col(a["da_subln_2"][0]), col(a["sw_q_norm_2"][0]), col(a["k_norm_2"]),
        col(a["hgrn_o_norm"][0]), lb, pk[0], pk[1], line(a["k_norm"][0, 0]), line(a["sw_sinks_2"][0]),
        line(a["da_lambda_2"][0])], 1)

    nc = _bacc.Bacc("TRN2", target_bir_lowering=False, num_devices=1)
    arrays, aps = {}, {}
    for name, v in D.items():
        v = np.ascontiguousarray(v)
        arrays["in_" + name] = v
        aps[name] = nc.dram_tensor("in_" + name, v.shape, mybir.dt.from_np(v.dtype), kind="ExternalInput").ap()
    out = nc.dram_tensor("out_xT", (128, 8, 512), mybir.dt.float32, kind="ExternalOutput").ap()
    program(nc, aps, out)
    r = _run(nc, [arrays], core_ids=[0])
    y = np.asarray(r.results[0]["out_xT"])
    return np.ascontiguousarray(y.transpose(2, 1, 0).reshape(1, 512, 1024))
```

```python
from contextlib import ExitStack

import numpy as np
import concourse.bass as bass
from concourse import mybir

F = mybir.dt.float32
R = mybir.dt.float32r
BF = mybir.dt.bfloat16
I32 = mybir.dt.int32
U8 = mybir.dt.uint8
ALU = mybir.AluOpType
ACT = mybir.ActivationFunctionType
AX = mybir.AxisListType

T = 512
KT8 = 8
EPS = 1e-6
ATT1, HGR = 1.0, 0.8
PARTS = (8, 8, 6)
CH = 1024
NRAW, NW = 2, 4

C_ID, C_BO, C_ON, C_PM, C_MC, C_VA, C_INV, C_EPS, C_HPI, C_RM = 0, 128, 256, 384, 512, 640, 644, 645, 646, 704
C_N = 704 + 512
G_MIX, G_FFN, G_AT0, G_AT1, G_F0, G_F1, G_KV = 0, 8, 16, 24, 32, 40, 48
G_Q, G_KS, G_KW, G_DQ, G_DK, G_SUB, G_SQ, G_SK, G_HO = 56, 57, 58, 59, 60, 61, 62, 63, 64
G_LB, G_PK, G_PV, G_KC, G_SINK, G_LAM = 65, 73, 105, 137, 201, 217
G_N = 217 + 256
LAMBDA_INIT = 0.2


class Tok:

    def __init__(self, eng, val=0):
        self.eng, self.val, self.need = eng, val, False


class Slot:

    def __init__(self, ap):
        self.ap, self.free = ap, []


class Ring:
    def __init__(self, aps):
        self.slots, self.n = [Slot(a) for a in aps], 0

    def take(self):
        s = self.slots[self.n % len(self.slots)]
        self.n += 1
        return s


def flat(after):
    for a in after:
        if a is None:
            continue
        if isinstance(a, (list, tuple)):
            yield from flat(a)
        else:
            yield a


class Queues:

    def __init__(self):
        self.q = {k: [] for k in ("pe", "act", "dve", "pool", "sp")}

    def put(self, eng, fn, *after):
        tok = Tok(eng)
        waits = [a for a in flat(after) if not (eng == "pe" and a.eng == "pe")]
        for a in waits:
            a.need = True
        self.q[eng].append((fn, waits, tok))
        return tok

    def dma(self, eng, dsem, out, in_, *after):
        dsem[1] += 1
        tok = Tok(dsem[0], 16 * dsem[1])
        waits = list(flat(after))
        for a in waits:
            a.need = True
        sem = dsem[0]
        self.q[eng].append((lambda e: e.dma_start(out, in_).then_inc(sem, 16), waits, None))
        return tok

    def count(self):
        for q in self.q.values():
            n = 0
            for _, _, tok in q:
                if tok is not None and tok.need:
                    n += 1
                    tok.val = n

    def emit(self, name, eng, sems):
        seen = {}
        for fn, waits, tok in self.q[name]:
            need = {}
            for a in waits:
                need[a.eng] = max(need.get(a.eng, 0), a.val)
            for k, v in need.items():
                if seen.get(k, 0) < v:
                    eng.wait_ge(sems[k] if isinstance(k, str) else k, v)
                    seen[k] = v
            ins = fn(eng)
            if tok is not None and tok.need:
                ins.then_inc(sems[name], 1)


def fence_of(queues):
    return [q[-1][2] for k, q in queues.q.items() if k != "sp" and q]


def step(g):
    try:
        next(g)
        return True
    except StopIteration:
        return False


def drain(g):
    for _ in g:
        pass


def pipeline(steps, lags):
    n = len(steps)
    for t in range(n + lags[-1]):
        for k, lag in enumerate(lags):
            if 0 <= t - lag < n:
                steps[t - lag][k]()
                yield


def program(nc, D, out):
    Q = Queues()
    put = Q.put
    ctx = ExitStack()

    def sbt(stack, name, cols, dt=F, parts=128):
        return stack.enter_context(nc.sbuf_tensor(name, [parts, cols], dt))

    def sem(name):
        return ctx.enter_context(nc.semaphore(name))

    with ctx:
        XT = sbt(ctx, "XT", 8 * T)
        hx = ExitStack()
        HH = sbt(hx, "HH", 8 * T, R)
        HL = sbt(hx, "HL", 8 * T, R)
        hx.close()
        HX = sbt(ctx, "HX", 16 * T)
        RAW = sbt(ctx, "RAW", NRAW * CH)
        WH = sbt(ctx, "WH", NW * CH, R)
        WL = sbt(ctx, "WL", NW * CH, R)
        CF = sbt(ctx, "CF", C_N)
        CB = sbt(ctx, "CB", 128 * 5, BF)
        CI = sbt(ctx, "CI", 128 * 8, U8)
        GP = sbt(ctx, "GP", G_N)
        RC = sbt(ctx, "RC", T)
        RSN = sbt(ctx, "RSN", T)
        SQB = sbt(ctx, "SQB", 2 * T)
        ACC = sbt(ctx, "ACC", T)
        RST = sbt(ctx, "RST", T)
        TMP = sbt(ctx, "TMP", 4 * T)
        PB = sbt(ctx, "PB", 6 * T)
        SM = sbt(ctx, "SM", 256)
        LBT = sbt(ctx, "LBT", 64)

        banks = [Slot(ctx.enter_context(nc.psum_tensor(f"bank{i}", [128, 512], F))[:, :]) for i in range(8)]
        sems = {k: sem("s_" + k) for k in ("pe", "act", "dve", "pool", "sp")}
        d_raw = [[sem(f"d_raw{i}"), 0] for i in range(NRAW)]
        d_one = {}

        def dsem(name):
            d_one[name] = [sem("d_" + name), 0]
            return d_one[name]

        ident = CF[:, C_ID:C_ID + 128]
        bones = CF[:, C_BO:C_BO + 128]
        ones = CF[:, C_ON:C_ON + 128]
        perm = CF[:, C_PM:C_PM + 128]
        eps = CF[:, C_EPS:C_EPS + 1]
        identb = CB[:, 0:128]
        m_fl = CB[:, 128:384]
        m_l = CB[:, 256:384]
        m_ul = CB[:, 384:640]

        t_cf = Q.dma("sp", dsem("cf"), CF[:, :], D["c_f"])
        t_gp = Q.dma("sp", dsem("gp"), GP[:, :], D["gp"])
        t_x = [Q.dma("sp", dsem(f"x{m}"), XT[:, m * T:(m + 1) * T], D["xT"][:, m, :]) for m in range(8)]
        t_cb = Q.dma("sp", dsem("cb"), CB[:, :], D["c_b"])

        raw = [RAW[:, i * CH:(i + 1) * CH] for i in range(NRAW)]
        whs = [WH[:, i * CH:(i + 1) * CH] for i in range(NW)]
        wls = [WL[:, i * CH:(i + 1) * CH] for i in range(NW)]
        units = []
        st = {"load": 0, "split": 0, "use": 0, "done": 0}
        t_load, t_split, t_used = {}, {}, {}

        def load_to(j):
            while st["load"] < min(j, len(units)):
                s = st["load"]
                n = units[s].shape[1]
                t_load[s] = Q.dma("sp", d_raw[s % NRAW], raw[s % NRAW][:, 0:n], units[s], t_split.get(s - NRAW))
                st["load"] += 1

        def pump():
            while st["split"] < min(st["done"] + NW, len(units)):
                s = st["split"]
                load_to(s + 1)
                n = units[s].shape[1]
                r_, h_, l_ = raw[s % NRAW][:, 0:n], whs[s % NW][:, 0:n], wls[s % NW][:, 0:n]
                th = put("act", lambda e, r_=r_, h_=h_: e.activation(h_, r_, ACT.Copy),
                         t_load[s], t_used.get(s - NW))
                tl = put("dve", lambda e, r_=r_, h_=h_, l_=l_: e.tensor_tensor(
                    l_, r_, h_.bitcast(F), ALU.subtract), th)
                t_split[s] = (th, tl)
                st["split"] += 1
            load_to(st["split"] + NRAW)

        def next_unit():
            pump()
            j = st["use"]
            st["use"] += 1
            return j, whs[j % NW], wls[j % NW], t_split[j]

        def unit_done(j, tok):
            t_used[j] = tok
            while st["done"] in t_used:
                st["done"] += 1

        waiting = []

        def later(n, fn):
            waiting.append([n, fn])

        def tick():
            for w in waiting:
                w[0] -= 1
            while waiting and waiting[0][0] <= 0:
                waiting.pop(0)[1]()

        def drive(a, b, ratio, gate=lambda: True):
            acc, left = 0.0, True
            while step(a):
                acc += ratio
                while acc >= 1:
                    acc -= 1
                    if not left:
                        tick()
                    elif gate():
                        left = step(b)
            return left

        def flush():
            while waiting:
                waiting.pop(0)[1]()

        hh = [HH[:, k * T:(k + 1) * T] for k in range(8)]
        hl = [HL[:, k * T:(k + 1) * T] for k in range(8)]
        sqr = Ring([SQB[:, i * T:(i + 1) * T] for i in range(2)])
        tmp = Ring([TMP[:, i * T:(i + 1) * T] for i in range(4)])
        dring = Ring([None, None])
        dring.slots = banks[0:2]
        xt = [XT[:, m * T:(m + 1) * T] for m in range(8)]
        x_tok = [[t] for t in t_x]
        h_busy = [[]]
        acc_st = {"n": 0, "tok": None, "free": []}
        rst_free = [[]]
        last_pe = [None]
        g_tok = [None]

        def three(bank, w, x, first, last, wait, n=None, tok_major=False):
            (wh_, wl_), (xh_, xl_) = w, x
            pairs = ((wh_, xh_), (wh_, xl_), (wl_, xh_))
            t = None
            for k, (a, b) in enumerate(pairs):
                l_, r_ = (b, a) if tok_major else (a, b)
                t = put("pe", lambda e, l_=l_, r_=r_, s=(first and k == 0), p=(last and k == 2): e.matmul(
                    bank, l_, r_, start=s, stop=p), wait if k == 0 else ())
            return t

        def fm(n_m, xs, x_toks, evac, k_units=((0, 8),), lead=1):
            m, k_end = 0, k_units[-1][1]
            while m < n_m:
                g = min(lead if m == 0 else 1, n_m - m)
                bk = [dring.take() for _ in range(g)]
                us = [next_unit() for _ in range(g)]
                for k in range(k_end):
                    for q in range(g):
                        j, w_h, w_l, w_t = us[q]
                        c = k * 128
                        tok = three(bk[q].ap, (w_h[:, c:c + 128], w_l[:, c:c + 128]), (xs[0][k], xs[1][k]),
                                    k == 0, k == k_end - 1, [w_t, x_toks[k], bk[q].free if k == 0 else None])
                        last_pe[0] = tok
                        if k == k_end - 1:
                            unit_done(j, tok)
                            evac(m + q, bk[q], tok)
                        tick()
                        yield
                m += g

        tbanks = [banks[0:4]]

        def tm(ncols, per_unit, x_toks, evac):
            k = 0
            for u in range(8 // per_unit):
                j, w_h, w_l, w_t = next_unit()
                for kk in range(per_unit):
                    c = kk * ncols
                    for i in range(4):
                        bk = tbanks[0][i]
                        tok = three(bk.ap[:, 0:ncols], (w_h[:, c:c + ncols], w_l[:, c:c + ncols]),
                                    (hh[k][:, i * 128:(i + 1) * 128], hl[k][:, i * 128:(i + 1) * 128]),
                                    k == 0, k == 7, [w_t, x_toks[k], bk.free if k == 0 else None],
                                    tok_major=True)
                        last_pe[0] = tok
                        if kk == per_unit - 1 and i == 3:
                            unit_done(j, tok)
                        if k == 7:
                            evac(i, bk, tok)
                        tick()
                        yield
                    k += 1

        def stat_add(m):
            s = sqr.take()
            t = put("act", lambda e: e.activation(s.ap, xt[m], ACT.Square), x_tok[m], s.free)
            x_tok[m] = x_tok[m] + [t]
            if acc_st["n"] == 0:
                acc_st["tok"] = put("pool", lambda e: e.tensor_copy(ACC[:, :], s.ap), t, acc_st["free"])
            else:
                acc_st["tok"] = put("pool", lambda e: e.tensor_tensor(ACC[:, :], ACC[:, :], s.ap, ALU.add),
                                    t, acc_st["tok"])
            s.free = [acc_st["tok"]]
            acc_st["n"] = (acc_st["n"] + 1) % 8

        def rstd_from(bank, tok, scale, dst, dst_free):
            s = tmp.take()
            t1 = put("act", lambda e: e.activation(s.ap, bank.ap, ACT.Ln, bias=eps, scale=scale), tok, s.free)
            bank.free = [t1]
            t2 = put("act", lambda e: e.activation(dst, s.ap, ACT.Exp, scale=-0.5), t1, dst_free)
            s.free = [t2]
            return t2

        def stat_finish():
            b = banks[3]
            t = put("pe", lambda e: e.matmul(b.ap, ones, ACC[:, :], start=True, stop=True),
                    acc_st["tok"], b.free, t_cf)
            acc_st["free"] = [t]
            return rstd_from(b, t, 1.0 / 1024, RST[:, :], rst_free[0])

        def split_to(dh, dl, src, tok, busy):
            th = put("act", lambda e: e.activation(dh, src, ACT.Copy), tok, busy)
            tl = put("dve", lambda e: e.tensor_tensor(dl, src, dh.bitcast(F), ALU.subtract), th, busy)
            return [th, tl]

        def norm_apply(g0, t_rs):
            toks = []
            busy = h_busy[0]
            rst_free[0] = []
            for k in range(8):
                s = tmp.take()
                t = put("dve", lambda e, k=k, s=s: e.scalar_tensor_tensor(
                    s.ap, xt[k], GP[:, g0 + k:g0 + k + 1], RST[:, :], ALU.mult, ALU.mult), t_rs, x_tok[k], s.free, t_gp)
                x_tok[k] = x_tok[k] + [t]
                rst_free[0].append(t)
                pair = split_to(hh[k], hl[k], s.ap, t, busy)
                s.free = pair
                toks.append(pair)
            return toks

        def residual(m, bank, tok, stats):
            t = put("dve", lambda e: e.tensor_tensor(xt[m], bank.ap, xt[m], ALU.add), tok, x_tok[m])
            bank.free = [t]
            x_tok[m] = [t]
            if stats:
                stat_add(m)

        def qk_norm(bank, tok, gcol, rope, dst, dst_free, done):
            s = sqr.take()
            t0 = put("act", lambda e: e.activation(s.ap, bank.ap, ACT.Square), tok, s.free)
            b3 = banks[3]

            def scale():
                t1 = put("pe", lambda e: e.matmul(b3.ap, bones, s.ap, start=True, stop=True), t0, b3.free)
                s.free = [t1]
                r = tmp.take()
                t2 = rstd_from(b3, t1, 1.0 / 64, r.ap, r.free)
                if not rope:
                    t3 = put("dve", lambda e: e.scalar_tensor_tensor(
                        dst, bank.ap, gcol, r.ap, ALU.mult, ALU.mult), t2, t0, dst_free, g_tok[0])
                    bank.free = [t3]
                    r.free = [t3]
                    done(t3)
                    return
                n = tmp.take()
                t3 = put("dve", lambda e: e.scalar_tensor_tensor(
                    n.ap, bank.ap, gcol, r.ap, ALU.mult, ALU.mult), t2, t0, n.free, g_tok[0])
                bank.free = [t3]
                t5 = put("pool", lambda e: e.tensor_tensor(dst, n.ap, RC[:, :], ALU.mult), t3, dst_free, t_rope)

                def turned():
                    t4 = put("pe", lambda e: e.matmul(b3.ap, perm, n.ap, start=True, stop=True), t3, b3.free)
                    n.free = [t4, t5]
                    t6 = put("dve", lambda e: e.tensor_tensor(r.ap, b3.ap, RSN[:, :], ALU.mult), t4, t_rope, t3)
                    b3.free = [t6]
                    t7 = put("dve", lambda e: e.tensor_tensor(dst, dst, r.ap, ALU.add), t6, t5)
                    r.free = [t7]
                    done(t7)
                later(5, turned)
            later(2, scale)

        def head_norm(bank, tok, gcol, dst, dst_free, done, stat_bank=None, wait=2):
            s = sqr.take()
            t0 = put("act", lambda e: e.activation(s.ap, bank.ap, ACT.Square), tok, s.free)
            tc = put("act", lambda e: e.activation(dst, bank.ap, ACT.Copy), tok, dst_free)
            bank.free = [t0, tc]

            def scale():
                b3 = stat_bank.take() if stat_bank else banks[3]
                t1 = put("pe", lambda e: e.matmul(b3.ap, ones, s.ap, start=True, stop=True), t0, b3.free)
                s.free = [t1]
                r = tmp.take()
                t2 = rstd_from(b3, t1, 1.0 / 128, r.ap, r.free)
                t3 = put("dve", lambda e: e.scalar_tensor_tensor(
                    dst, dst, gcol, r.ap, ALU.mult, ALU.mult), t2, tc, g_tok[0])
                r.free = [t3]
                done(t3)
            later(wait, scale)

        ph = ExitStack()
        P1 = sbt(ph, "P1", 38 * T + 352)
        ph.close()

        def p1(a, n):
            return P1[:, a * T:a * T + n]

        ktt = [[p1(2 * b + g, T) for g in range(2)] for b in range(2)]
        qtt = [p1(4 + p, T) for p in range(4)]
        VP, PTC = p1(8, 6 * T), p1(14, 2 * T)
        OM, HV = p1(16, 4 * T), p1(20, 4 * T)
        w1k, w1v = p1(16, 4 * T), p1(20, 4 * T)
        xc = [p1(32, T), p1(33, T)]
        xb = p1(34, 992).rearrange("p (l g n) -> p l g n", l=16, g=2)
        hf, hq, hg = p1(24, 4 * T), p1(28, 4 * T), p1(32, 4 * T)
        h3 = [p1(24 + k, T) for k in range(12)]
        VC = p1(36, T)
        W2, KC, KCT = P1[:, 37 * T:37 * T + 128], P1[:, 37 * T + 128:37 * T + 192], P1[:, 37 * T + 192:37 * T + 320]
        HG = P1[:, 38 * T:38 * T + 256]
        GT = P1[:, 38 * T + 256:38 * T + 352]
        ra, rk, ri = [PB[:, k * T:(k + 1) * T] for k in range(3)]

        t_pos = Q.dma("sp", dsem("pos"), ri.bitcast(I32), D["pos"].partition_broadcast(128))
        t_ci = Q.dma("sp", dsem("ci"), p1(8, 1024), D["c_i"])

        def ffn_units(gu, dn):
            found, j0 = [], 0
            for n in PARTS:
                for j in range(j0, j0 + n):
                    found += [gu[j], gu[22 + j]]
                found += [dn[m, :, j0 * 128:(j0 + n) * 128] for m in range(8)]
                j0 += n
            return found

        for name, n in (("w_in", 8), ("w_ing", 4), ("w_inv", 4), ("w_inh", 12), ("w_out", 8)):
            units += [D[name][u] for u in range(n)]
        units += ffn_units(D["wgu1"], D["wd1"])
        for name, n in (("da_v", 8), ("da_qk", 16), ("da_o", 8)):
            units += [D[name][u] for u in range(n)]
        units += ffn_units(D["wgu2"], D["wd2"])
        for name, n in (("sw_k", 2), ("sw_v", 2), ("sw_q", 8), ("sw_o", 8)):
            units += [D[name][u] for u in range(n)]
        units += ffn_units(D["wgu3"], D["wd3"])

        t_rope, t_tab = [], [None]

        def table(name, tok=None):
            put("act", lambda e: e.preload_act_table_set(name), tok)

        def rope_tables():
            t = put("dve", lambda e: e.tensor_copy(ra, ri.bitcast(I32)), t_pos)
            t = put("dve", lambda e: e.tensor_scalar(ra, ra, CF[:, C_INV:C_INV + 1], None, ALU.mult), t, t_cf)
            magic = 12582912.0
            c = [6.28125]
            rest = 2 * np.pi - c[0]
            for bits in (7, 7):
                sc = 2.0 ** (bits - 1 - np.floor(np.log2(rest)))
                c.append(float(np.floor(rest * sc) / sc))
                rest -= c[-1]
            c.append(float(rest))
            for big in (4096.0, 1.0):
                t = put("dve", lambda e, big=big: e.tensor_scalar(
                    rk, ra, float(1.0 / (2 * np.pi * big)), magic, ALU.mult, ALU.add), t)
                t = put("dve", lambda e: e.tensor_scalar(rk, rk, -magic, None, ALU.add), t)
                yield
                for cc in c:
                    t = put("dve", lambda e, v=-cc * big: e.scalar_tensor_tensor(
                        ra, rk, v, ra, ALU.mult, ALU.add), t)
                    yield
            pi = 3.1415925
            t = put("dve", lambda e: e.tensor_scalar(ra, ra, -pi, pi, ALU.max, ALU.min), t)
            t1 = put("act", lambda e: e.activation(RSN[:, :], ra, ACT.Sin), t)
            t2 = put("act", lambda e: e.activation(rk, ra, ACT.Abs), t)
            t3 = put("act", lambda e: e.activation(RC[:, :], rk, ACT.Sin, scale=-1.0,
                                                   bias=CF[:, C_HPI:C_HPI + 1]), t2)
            table("natural_log_exp_and_others")
            t_rope.extend([t1, t3])

        table("natural_log_exp_and_others")
        for m in range(8):
            stat_add(m)
        h_tok = norm_apply(G_MIX, stat_finish())
        t_w1 = []

        t_xc, t_kt, t_qt = [None, None], {}, [None] * 4
        t_ci = put("pool", lambda e: e.tensor_copy(CI[:, :], p1(8, 1024)), t_ci)
        t_z = put("pool", lambda e: e.memset(VP, 0.0), t_ci)
        t_zc = put("pool", lambda e: e.memset(VC, 0.0))
        t_zk = put("pool", lambda e: e.memset(KC, 0.0))
        t_zg = put("pool", lambda e: e.memset(HG, 0.0))

        def evac_in(m, bank, tok):
            if m < 2:
                t_xc[m] = put("act", lambda e: e.activation(xc[m], bank.ap, ACT.Copy), tok)
                bank.free = [t_xc[m]]
            elif m < 4:
                s = tmp.take()

                def done(t):
                    us = []
                    for g in range(2):
                        for half in range(2):
                            us.append(put("act", lambda e, g=g, half=half: e.activation(
                                ktt[m - 2][g][64 * half:64 * half + 64, :], s.ap[64 * g:64 * g + 64, :], ACT.Copy),
                                t))
                        t_kt[m - 2, g] = us[-2:]
                    s.free = us
                qk_norm(bank, tok, GP[:, G_KS + m - 2:G_KS + m - 1], False, s.ap, s.free, done)
            else:
                def done(t):
                    t_qt[m - 4] = t
                qk_norm(bank, tok, gq8[0], False, qtt[m - 4], None, done)

        t_g8 = put("dve", lambda e: e.tensor_scalar(LBT[:, 32:33], GP[:, G_Q:G_Q + 1], 0.125, None, ALU.mult), t_gp)
        t_g8 = put("dve", lambda e: e.tensor_scalar(LBT[:, 33:34], GP[:, G_DQ:G_DQ + 1], 0.125, None, ALU.mult), t_g8)
        t_g8 = put("dve", lambda e: e.tensor_scalar(LBT[:, 34:35], GP[:, G_SQ:G_SQ + 1], 0.125, None, ALU.mult), t_g8)
        t_g8 = put("dve", lambda e: e.tensor_scalar(LBT[:, 35:36], GP[:, G_SUB:G_SUB + 1], 1.0 - LAMBDA_INIT,
                                                    None, ALU.mult), t_g8)
        t_g8 = put("dve", lambda e: e.tensor_scalar(LBT[:, 36:37], GP[:, G_HO:G_HO + 1], 0.5, None, ALU.mult), t_g8)
        gq8 = [LBT[:, 32:33], LBT[:, 33:34], LBT[:, 34:35]]
        g_tok[0] = t_g8

        rope = rope_tables()
        prj = fm(8, (hh, hl), h_tok, evac_in, lead=2)
        for k in range(24):
            step(prj)
        t_w1 += [Q.dma("sp", dsem("w1k"), w1k, D["cmp_w1"][0]), Q.dma("sp", dsem("w1v"), w1v, D["cmp_w1"][1])]
        t_w2 = Q.dma("sp", dsem("w2"), W2, D["cmp_w2"])
        for k in range(12):
            step(prj)
        drive(rope, prj, 2)
        drain(prj)

        vp = VP.rearrange("p (i b c) -> p i b c", i=4, b=4)
        t_vp, t_gt = [None] * 4, [None] * 4

        def evac_vg(i, bank, tok):
            t_vp[i] = put("act", lambda e: e.activation(
                vp[:, i, :, 64:128], bank.ap[:, 0:256].rearrange("p (b c) -> p b c", b=4), ACT.Copy), tok, t_z)
            g = GT[:, i * 24:(i + 1) * 24]
            t = put("act", lambda e: e.activation(g, bank.ap[:, 256:280], ACT.Exp, scale=-1.0), tok)
            bank.free = [t_vp[i], t]
            t = put("dve", lambda e: e.tensor_scalar(g, g, 1.0, None, ALU.add), t)
            t_gt[i] = put("dve", lambda e: e.reciprocal(g, g), t)

        tbanks[0] = banks[4:8]
        drain(tm(280, 2, h_tok, evac_vg))

        t_kc, t_vc, t_cmp_pe, t_ptc = [None, None], [], [], []
        pr = Ring([PB[:, i * T:(i + 1) * T] for i in range(4)])
        ptr_ = Ring([PB[:, (4 + i) * T:(5 + i) * T] for i in range(2)])
        for k in range(3):
            pr.slots[k].free = list(t_rope)

        def compress():
            xb_free, hg_free = [], [t_zg]
            for kv in range(2):
                w1 = (w1k, w1v)[kv]
                pos0 = (G_PK, G_PV)[kv]
                tb = []
                for g in range(2):
                    src = xc[kv][64 * g:64 * g + 64, :].rearrange("p (n l) -> p l n", l=16)
                    for par in range(2):
                        for r in range(2):
                            c = pos0 + 16 * r + par
                            tb.append(put("dve", lambda e, g=g, par=par, r=r, c=c, src=src: e.tensor_tensor(
                                xb[64 * par:64 * par + 64, 8 * r:8 * r + 8, g, :], src[:, par::2, r:r + 31],
                                GP[64 * g:64 * g + 64, c:c + 15:2].unsqueeze(2).to_broadcast([64, 8, 31]),
                                ALU.add), t_xc[kv], t_gp, xb_free))
                        yield
                hid = banks[4]
                for l in range(16):
                    t = put("pe", lambda e, l=l, w1=w1: e.matmul(
                        hid.ap[:, 0:62], w1[:, l * 128:(l + 1) * 128], xb[:, l, :, :],
                        start=(l == 0), stop=(l == 15)), tb, t_w1[kv], hid.free)
                    if l % 4 == 3:
                        yield
                xb_free = [t]
                t_cmp_pe.extend([t, t_w2])
                tgs = []
                for r in range(4):
                    tgs.append(put("act", lambda e, r=r: e.activation(
                        HG.rearrange("p (g r n) -> p g r n", g=2, r=4)[:, :, r, 0:31],
                        hid.ap[:, 0:62].rearrange("p (g n) -> p g n", g=2), ACT.Gelu_apprx_tanh), t, hg_free))
                hid.free = tgs
                yield
                for g in range(2):
                    b6 = banks[6]
                    if kv == 0:
                        t = put("pe", lambda e, g=g: e.matmul(
                            b6.ap[0:32, 0:64], HG[:, g * 128:g * 128 + 32], W2[:, 0:64], start=True, stop=True),
                            tgs, t_w2, b6.free)
                        hg_free = [t]
                        o = 8 * g
                        ta = put("act", lambda e, o=o: e.activation(
                            KCT[0:32, 0:64], b6.ap[0:32, 0:64], ACT.Square, accum_out=SM[0:32, o:o + 1]), t, t_kc)
                        ta = put("act", lambda e, o=o: e.activation(
                            SM[0:32, o + 1:o + 2], SM[0:32, o:o + 1], ACT.Ln, bias=eps[0:32, :], scale=1.0 / 64), ta)
                        ta = put("act", lambda e, o=o: e.activation(
                            SM[0:32, o + 2:o + 3], SM[0:32, o + 1:o + 2], ACT.Exp, scale=-0.5), ta)
                        t1 = None
                        for half in range(2):
                            t1 = put("dve", lambda e, o=o, half=half: e.scalar_tensor_tensor(
                                KCT[0:32, 64 * half:64 * half + 64], b6.ap[0:32, 0:64], SM[0:32, o + 2:o + 3],
                                GP[0:32, G_KC:G_KC + 64], ALU.mult, ALU.mult), ta)
                        yield
                        b7 = banks[7]
                        t2 = put("pe", lambda e: e.transpose(b7.ap[:, 0:32], KCT[0:32, :], ident[0:32, 0:32]), t1, b7.free)
                        b6.free = [t1]
                        t_kc[g] = put("act", lambda e, g=g: e.activation(
                            KC[:, g * 32:g * 32 + 31], b7.ap[:, 0:31], ACT.Copy), t2, t_zk)
                        b7.free = [t_kc[g]]
                    else:
                        t = put("pe", lambda e, g=g: e.matmul(
                            b6.ap[:, 0:64], HG[:, g * 128:(g + 1) * 128], W2[:, 64:128], start=True, stop=True),
                            tgs, t_w2, b6.free)
                        cs = []
                        for r in range(4):
                            c = (2 * g + r // 2) * 128 + 64 * (r % 2)
                            cs.append(put("act", lambda e, r=r, c=c: e.activation(
                                VC[32 * r:32 * r + 32, c:c + 64], b6.ap[32 * r:32 * r + 32, 0:64], ACT.Copy), t, t_zc))
                        b6.free = cs
                        t_vc.extend(cs)

            flush()
            for i in range(4):
                for h in range(8):
                    half = h % 2
                    bk = banks[4 + half]
                    t = put("pe", lambda e, h=h, half=half, i=i, bk=bk: e.matmul(
                        bk.ap[:, 32 * (h // 2):32 * (h // 2) + 32], qtt[h // 2][64 * half:64 * half + 64, i * 128:(i + 1) * 128],
                        KC[64 * half:64 * half + 64, 32 * (h // 4):32 * (h // 4) + 32], start=True, stop=True),
                        t_qt[h // 2], t_kc, bk.free)
                yield
                p = pr.take()
                p3 = p.ap[:, 0:256].rearrange("p (h n) -> p h n", h=8)
                o = 32 + 32 * (i % 2)
                tms = []
                for half in range(2):
                    bk = banks[4 + half]
                    tms.append(put("dve", lambda e, i=i, p3=p3, bk=bk, half=half: e.tensor_tensor(
                        p3.rearrange("p (h c) n -> p h c n", c=2)[:, :, half, :],
                        bk.ap[:, 0:128].rearrange("p (h n) -> p h n", h=4),
                        CF[:, C_MC + 32 * i:C_MC + 32 * i + 32].unsqueeze(1).to_broadcast([128, 4, 32]), ALU.add),
                        t, p.free))
                    bk.free = [tms[-1]]
                t = tms
                t = put("dve", lambda e, p3=p3, o=o: e.tensor_reduce(SM[:, o:o + 8], p3, AX.X, ALU.max), t)
                t = put("dve", lambda e, p3=p3, o=o: e.tensor_tensor(
                    p3, p3, SM[:, o:o + 8].unsqueeze(2).to_broadcast([128, 8, 32]), ALU.subtract), t)
                t = put("act", lambda e, p=p: e.activation(p.ap[:, 0:256], p.ap[:, 0:256], ACT.Exp), t)
                t = put("dve", lambda e, p3=p3, o=o: e.tensor_reduce(SM[:, o + 8:o + 16], p3, AX.X, ALU.add), t)
                t = put("dve", lambda e, o=o: e.reciprocal(SM[:, o + 16:o + 24], SM[:, o + 8:o + 16]), t)
                t = put("dve", lambda e, o=o, i=i: e.scalar_tensor_tensor(
                    SM[:, o + 24:o + 32], SM[:, o + 16:o + 24], CF[:, C_VA + i:C_VA + i + 1],
                    GT[:, i * 24:(i + 1) * 24].rearrange("p (h c) -> p h c", c=3)[:, :, 0], ALU.mult, ALU.mult),
                    t, t_gt[i])
                t = put("dve", lambda e, p3=p3, o=o: e.tensor_tensor(
                    p3, p3, SM[:, o + 24:o + 32].unsqueeze(2).to_broadcast([128, 8, 32]), ALU.mult), t)
                for _ in range(4):
                    yield
                b6 = banks[6]
                for g in range(2):
                    t2 = put("pe", lambda e, g=g, p=p: e.transpose(
                        b6.ap[:, g * 128:(g + 1) * 128], p.ap[:, g * 128:(g + 1) * 128], ident), t, b6.free)
                p.free = [t2]
                t3 = put("act", lambda e, i=i: e.activation(
                    PTC.rearrange("p (g t) -> p g t", g=2)[:, :, i * 128:(i + 1) * 128],
                    b6.ap[:, 0:256].rearrange("p (g t) -> p g t", g=2), ACT.Copy), t2)
                b6.free = [t3]
                t_ptc.append(t3)

        sring = Ring([None, None])
        sring.slots = [banks[4], banks[5], banks[2]]
        pt_bank, ob = banks[6], banks[7]
        sm_free, sm_n = {}, [0]

        def softmax_stage(lhs, rhs, mask, mcol, n, deps, sink=None):
            bk = sring.take()
            put("pe", lambda e: e.matmul(bk.ap[:, 0:n], lhs, rhs, start=True, stop=False, skip_group_check=True),
                deps, bk.free)
            t = put("pe", lambda e: e.matmul(bk.ap[:, mcol:n], identb, mask, start=False, stop=True,
                                             skip_group_check=True), t_cb)
            o = 96 + 8 * (sm_n[0] % 16)
            sm_n[0] += 1
            p = pr.take()
            t1 = put("dve", lambda e: e.tensor_reduce(SM[:, o:o + 1], bk.ap[:, 0:n], AX.X, ALU.max, negate=True),
                     t, sm_free.get(o))
            t_sink = None
            if sink is not None:
                t1 = put("dve", lambda e: e.tensor_scalar(SM[:, o:o + 1], SM[:, o:o + 1], sink[1], None, ALU.min),
                         t1, sink[2])
            t2 = put("act", lambda e: e.activation(p.ap[:, 0:n], bk.ap[:, 0:n], ACT.Exp, bias=SM[:, o:o + 1],
                                                   accum_out=SM[:, o + 1:o + 2]), t1, p.free)
            bk.free = [t2]
            if sink is not None:
                t_sink = put("act", lambda e: e.activation(SM[:, o + 3:o + 4], sink[0], ACT.Exp,
                                                           bias=SM[:, o:o + 1]), t1)
            return p, o, [t2, t_sink]

        def turn(p, blocks, tok):
            n = len(blocks) * 128
            for k, j in enumerate(blocks):
                t = put("pe", lambda e, j=j, k=k: e.transpose(
                    pt_bank.ap[:, k * 128:(k + 1) * 128], p.ap[:, j * 128:(j + 1) * 128], ident), tok, pt_bank.free)
            p.free = [t]
            s = ptr_.take()
            t2 = put("act", lambda e: e.activation(s.ap[:, 0:n], pt_bank.ap[:, 0:n], ACT.Copy), t, s.free)
            pt_bank.free = [t2]
            return s, t2

        def need(table_, key):
            while key not in table_:
                if first_over[0] or not step(prj):
                    flush()

        class Splits:

            def __init__(self, src, toks, att):
                self.src, self.toks, self.att, self.got = src, toks, att, {}

            def __getitem__(self, k):
                while self.toks[k] is None:
                    if not step(self.att):
                        flush()
                if k not in self.got:
                    self.got[k] = split_to(hh[k], hl[k], self.src[:, k * T:(k + 1) * T], self.toks[k], h_busy[0])
                return self.got[k]

        def then_out(first, splits):
            first_over[0] = False
            yield from first
            first_over[0] = True
            h_busy[0] = [last_pe[0]]
            for k in range(8):
                if splits.toks[k] is not None:
                    splits[k]
            yield from fm(8, (hh, hl), splits, lambda m, bank, tok: residual(m, bank, tok, True), lead=2)
            h_busy[0] = [last_pe[0]]

        t_om, acc_att, first_over = [None] * 4, [0.0], [False]

        def nsa_step(h, b, i):
            pair, half, g = h // 2, h % 2, h // 4
            n = (i + 1) * 128
            z = {}

            def scores():
                z["p"], z["o"], z["t"] = softmax_stage(
                    qtt[pair][64 * half:64 * half + 64, i * 128:(i + 1) * 128],
                    ktt[b][g][64 * half:64 * half + 64, 0:n], m_l, i * 128, n, [t_qt[pair], t_kt[b, g]])

            def weights():
                o, p = z["o"], z["p"]
                gate = GT[:, i * 24 + 3 * h + 1 + b:i * 24 + 3 * h + 2 + b]
                t = put("dve", lambda e: e.reciprocal(SM[:, o + 2:o + 3], SM[:, o + 1:o + 2]), z["t"])
                t = put("dve", lambda e: e.tensor_scalar(
                    p.ap[:, 0:n], p.ap[:, 0:n], SM[:, o + 2:o + 3], gate, ALU.mult, ALU.mult), t, t_gt[i])
                sm_free[o] = [t]
                z["s"], z["t2"] = turn(p, range(i + 1), t)

            def values():
                if half == 0 and b == 0 and i == 0:
                    cc = (2 * g + pair % 2) * 128
                    put("pe", lambda e: e.matmul(ob.ap, VC[:, cc:cc + 128], PTC[:, g * T:(g + 1) * T],
                                                 start=True, stop=False, skip_group_check=True),
                        t_vc, t_ptc, ob.free)
                last = half == 1 and b == 1 and i == 3
                for j in range(i + 1):
                    v = vp[:, j, 2 * b + g, :]
                    v = v[:, 64:192] if half == 0 else v[:, 0:128]
                    t = put("pe", lambda e, j=j, v=v: e.matmul(
                        ob.ap[:, i * 128:(i + 1) * 128], v, z["s"].ap[:, j * 128:(j + 1) * 128],
                        start=False, stop=(last and j == i), skip_group_check=True), z["t2"], t_vp)
                z["s"].free = [t]
                if last:
                    t_om[pair] = put("act", lambda e: e.activation(OM[:, pair * T:(pair + 1) * T], ob.ap, ACT.Copy),
                                     t, t_cmp_pe)
                    ob.free = [t_om[pair]]
            return scores, weights, values

        t_h3, t_hv = [None] * 12, [None] * 4

        def evac_h(m, bank, tok):
            if m < 4:
                t_h3[m] = put("act", lambda e: e.activation(h3[m], bank.ap, ACT.Tanh, scale=0.5), tok, t_cmp_pe)
                bank.free = [t_h3[m]]
                return
            s = tmp.take()
            t = put("act", lambda e: e.activation(s.ap, bank.ap, ACT.Tanh, scale=0.5), tok, s.free)
            t_h3[m] = put("dve", lambda e: e.scalar_tensor_tensor(
                h3[m], s.ap, 1.0, bank.ap, ALU.add, ALU.mult), t, t_cmp_pe)
            s.free = [t_h3[m]]
            bank.free = [t_h3[m]]

        def evac_hv(i, bank, tok):
            t_hv[i] = put("act", lambda e: e.activation(HV[:, i * T:(i + 1) * T], bank.ap, ACT.Copy), tok, t_cmp_pe)
            bank.free = [t_hv[i]]

        l0, l1 = GP[:, G_LB:G_LB + 4], GP[:, G_LB + 4:G_LB + 8]
        t = put("dve", lambda e: e.tensor_tensor(LBT[:, 0:4], l0, l1, ALU.max), t_gp)
        ta = put("dve", lambda e: e.tensor_tensor(LBT[:, 4:8], l0, LBT[:, 0:4], ALU.subtract), t)
        tb = put("dve", lambda e: e.tensor_tensor(LBT[:, 8:12], l1, LBT[:, 0:4], ALU.subtract), t)
        t = put("act", lambda e: e.activation(LBT[:, 4:12], LBT[:, 4:12], ACT.Exp), ta, tb)
        t = put("dve", lambda e: e.tensor_tensor(LBT[:, 0:4], LBT[:, 4:8], LBT[:, 8:12], ALU.add), t)
        t = put("dve", lambda e: e.reciprocal(LBT[:, 0:4], LBT[:, 0:4]), t)
        t = put("dve", lambda e: e.tensor_tensor(LBT[:, 12:16], LBT[:, 4:8], LBT[:, 0:4], ALU.mult), t)
        t = put("dve", lambda e: e.tensor_scalar(LBT[:, 16:20], LBT[:, 12:16], -0.5, 0.5, ALU.mult, ALU.add), t)
        t_lb = put("dve", lambda e: e.tensor_tensor(LBT[:, 20:24], LBT[:, 16:20], LBT[:, 12:16], ALU.add), t)

        def first_mixer():
            yield from compress()
            table("exp_and_others")
            yield from pipeline([nsa_step(h, b, i) for h in range(8) for b in range(2) for i in range(4)], (0, 2, 3))

        att = first_mixer()
        tbanks[0] = banks[0:4]
        prj = tm(512, 2, h_tok, evac_hv)
        for k in range(31):
            step(att)
            step(prj)
        while not t_cmp_pe[2:]:
            step(att)
        drain(prj)
        prj = fm(12, (hh, hl), h_tok, evac_h)
        while step(prj):
            acc_att[0] += ATT1
            while acc_att[0] >= 1:
                acc_att[0] -= 1
                step(att)
        flush()
        fx = fence_of(Q)
        table("natural_log_exp_and_others")

        hx_ = [HX[:, k * T:(k + 1) * T] for k in range(16)]
        er = Ring(hx_[8:11])
        arr = Ring(hx_[12:14])
        for s in er.slots + arr.slots:
            s.free = list(fx)
        eq = Slot(hx_[11])
        eq.free = list(fx)
        set_free = [list(fx), list(fx)]
        aring = Ring([None] * 2)
        aring.slots = banks[0:2]
        head = {}
        t_mix = [None] * 4

        def levels(h):
            b = h % 2
            bc, kk, _, at_ = hx_[4 * b:4 * b + 4]
            at = at_.rearrange("p (i t) -> p i t", i=4)
            f, q = hf[:, h * T:(h + 1) * T], hq[:, h * T:(h + 1) * T]
            fr = set_free[b]
            t = put("dve", lambda e: e.tensor_scalar(
                f, f, LBT[:, 16 + h:17 + h], LBT[:, 20 + h:21 + h], ALU.mult, ALU.add), t_h3[h], t_lb)
            t_k = put("dve", lambda e: e.tensor_scalar(kk, f, -0.5, 0.5, ALU.mult, ALU.add), t, fr)
            t = put("act", lambda e: e.activation(f, f, ACT.Ln), t_k)
            t_b = put("dve", lambda e: e.tensor_tensor_scan(
                bc, CF[:, C_RM:C_RM + T], f, 0.0, ALU.mult, ALU.add), t, fr)
            yield
            bk = aring.take()
            for i in range(4):
                t = put("pe", lambda e, i=i, bk=bk: e.matmul(
                    bk.ap[:, i * 128:(i + 1) * 128], kk[:, i * 128:(i + 1) * 128], q[:, i * 128:(i + 1) * 128],
                    start=True, stop=True), t_k, t_h3[4 + h], bk.free)
            t_at = put("dve", lambda e, bk=bk: e.tensor_tensor(
                at, bk.ap.rearrange("p (i t) -> p i t", i=4), ident.unsqueeze(1).to_broadcast([128, 4, 128]),
                ALU.mult), t, fr)
            bk.free = [t_at]
            readers = []

            def decay(lv):
                m = 1 << lv
                eb = er.take()
                v, b3, k3, q3 = [a.rearrange("p (n c) -> p n c", c=2 * m) for a in (eb.ap, bc, kk, q)]
                edge = b3[:, :, m - 1:m].to_broadcast([128, 256 // m, m])
                t1 = put("dve", lambda e: e.tensor_tensor(v[:, :, 0:m], edge, b3[:, :, 0:m], ALU.subtract),
                         t_b, eb.free)
                if m < 64:
                    t2 = put("pool", lambda e: e.tensor_tensor(
                        v[:, :, m:2 * m], b3[:, :, m:2 * m], edge, ALU.subtract), t_b, eb.free)
                else:
                    t2 = put("pool", lambda e: e.tensor_copy(v[:, :, m:2 * m], b3[:, :, m:2 * m]), t_b, eb.free)
                readers.extend([t1, t2])
                t = put("act", lambda e: e.activation(eb.ap, eb.ap, ACT.Exp), t1, t2)
                ta = put("dve", lambda e: e.tensor_tensor(v[:, :, 0:m], v[:, :, 0:m], k3[:, :, 0:m], ALU.mult), t, t_k)
                tb = put("pool", lambda e: e.tensor_tensor(
                    v[:, :, m:2 * m], v[:, :, m:2 * m], q3[:, :, m:2 * m], ALU.mult), t, t_h3[4 + h])
                return eb, [ta, tb]

            made = {0: decay(0)}
            for lv in range(7):
                if lv < 6:
                    made[lv + 1] = decay(lv + 1)
                yield
                eb, te = made[lv]
                bk = aring.take()
                for i in range(4):
                    c = slice(i * 128, (i + 1) * 128)
                    t = put("pe", lambda e, c=c, eb=eb, bk=bk: e.matmul(
                        bk.ap[:, c], eb.ap[:, c], eb.ap[:, c], start=True, stop=True), te, bk.free)
                eb.free = [t]
                t_at = put("dve", lambda e, bk=bk, lv=lv: e.copy_predicated(
                    at, CI[:, lv * 128:(lv + 1) * 128].unsqueeze(1).to_broadcast([128, 4, 128]),
                    bk.ap.rearrange("p (i t) -> p i t", i=4)), t, t_ci, t_at)
                bk.free = [t_at]
                yield
            head[h] = (t_k, t_b, t_at, readers)

        def whole(h):
            b = h % 2
            bc, kk, kh, at_ = hx_[4 * b:4 * b + 4]
            at = at_.rearrange("p (i t) -> p i t", i=4)
            q = hq[:, h * T:(h + 1) * T]
            t_k, t_b, t_at, readers = head[h]
            b4 = bc.rearrange("p (n c) -> p n c", c=128)
            t = put("dve", lambda e: e.tensor_tensor(
                b4[:, :, 64:128], b4[:, :, 64:128], b4[:, :, 63:64].to_broadcast([128, 4, 64]), ALU.add), readers)
            tk = put("dve", lambda e: e.tensor_tensor(
                kh.rearrange("p (n c) -> p n c", c=128), b4[:, :, 127:128].to_broadcast([128, 4, 128]), b4,
                ALU.subtract), t, set_free[b])
            tk = put("act", lambda e: e.activation(kh, kh, ACT.Exp), tk)
            tq = put("act", lambda e: e.activation(eq.ap, bc, ACT.Exp), t, eq.free)
            EB = LBT[:, 40 + 4 * h:44 + 4 * h]
            te = put("act", lambda e: e.activation(EB, b4[:, :, 127], ACT.Exp), t)
            tk = put("dve", lambda e: e.tensor_tensor(kh, kh, kk, ALU.mult), tk)
            tq = put("pool", lambda e: e.tensor_tensor(eq.ap, eq.ap, q, ALU.mult), tq)
            yield
            ks_ = {}
            for n, (j, i) in enumerate(((0, 2), (0, 3), (1, 3))):
                dst = hx_[14 + b][:, n * 128:(n + 1) * 128]
                src = kh[:, j * 128:(j + 1) * 128]
                two = i - j == 3
                ks_[j, i] = (dst, put("dve", lambda e, dst=dst, src=src, j=j, two=two: e.tensor_scalar(
                    dst, src, EB[:, j + 1:j + 2], EB[:, j + 2:j + 3] if two else None, ALU.mult,
                    *([ALU.mult] if two else [])), tk, te, set_free[b]))
            for j in range(3):
                ks_[j, j + 1] = (kh[:, j * 128:(j + 1) * 128], tk)
            yield
            o_b = banks[3]
            kept = {}
            for i in (1, 0, 2, 3, 4):
                if 0 < i < 4:
                    bk = aring.take()
                    for j in range(i):
                        k_, t_ = ks_[j, i]
                        t = put("pe", lambda e, i=i, j=j, k_=k_, bk=bk: e.matmul(
                            bk.ap[:, j * 128:(j + 1) * 128], k_, eq.ap[:, i * 128:(i + 1) * 128],
                            start=True, stop=True), t_, tq, bk.free)
                    t_eq = t
                    s = arr.take()
                    t = put("act", lambda e, s=s, i=i, bk=bk: e.activation(
                        s.ap[:, 0:i * 128], bk.ap[:, 0:i * 128], ACT.Copy), t, s.free)
                    bk.free = [t]
                    kept[i] = (s, t)
                    yield
                    if i == 1:
                        continue
                if i == 0:
                    t = put("pe", lambda e: e.matmul(
                        o_b.ap[:, 0:128], HV[:, h * 128:(h + 1) * 128], at[:, 0, :], start=True, stop=False,
                        skip_group_check=True), t_at, t_hv, o_b.free)
                    continue
                n = i - 1
                s, ts_ = kept[n]
                for j in range(n + 1):
                    rhs = s.ap[:, j * 128:(j + 1) * 128] if j < n else at[:, n, :]
                    t = put("pe", lambda e, n=n, j=j, rhs=rhs: e.matmul(
                        o_b.ap[:, n * 128:(n + 1) * 128], HV[:, j * T + h * 128:j * T + (h + 1) * 128], rhs,
                        start=False, stop=(n == 3 and j == 3), skip_group_check=True), ts_, t_at, t_hv)
                s.free = [t]
                yield
            eq.free = [t_eq]
            set_free[b] = [t, t_eq]

            def done(t):
                t_mix[h] = put("dve", lambda e: e.tensor_tensor(
                    h3[h + 4], h3[h + 4], h3[h + 8], ALU.mult), t, t_h3[h + 8])
            head_norm(o_b, t, LBT[:, 36:37], h3[h + 4], [tq, t_eq, readers, t_at], done, aring, 1)
            yield

        def second_mixer():
            def ticks(g):
                for _ in g:
                    tick()
                    yield
            yield from ticks(levels(0))
            for h in range(4):
                a, b = whole(h), (levels(h + 1) if h < 3 else iter(()))
                live = [True, True]
                while live[0] or live[1]:
                    for n, g in enumerate((a, b)):
                        if live[n]:
                            live[n] = step(g)
                            tick()
                            yield

        prj = second_mixer()
        left = drive(att, prj, HGR)
        drain(prj)
        flush()
        fence = fence_of(Q)
        h_busy[0] = list(fence)
        om = [(OM[:, k * T:(k + 1) * T], t_om[k]) for k in range(4)] + [(h3[4 + k], t_mix[k]) for k in range(4)]
        mix_tok = [split_to(hh[k], hl[k], src, t, h_busy[0]) for k, (src, t) in enumerate(om)]

        def out_proj(tok8):
            dring.slots = banks[0:3]
            drain(fm(8, (hh, hl), tok8, lambda m, bank, tok: residual(m, bank, tok, True), lead=3))
            h_busy[0] = [last_pe[0]]

        out_proj(mix_tok)

        def ffn(name, g0, fence, last):
            table("natural_log_exp_and_others")
            h_tok = norm_apply(g0, stat_finish())
            st_ = ExitStack()
            FH = sbt(st_, "FH" + name, 8 * T, R)
            FL = sbt(st_, "FL" + name, 8 * T, R)
            st_.close()
            fh = [FH[:, k * T:(k + 1) * T] for k in range(8)]
            fl = [FL[:, k * T:(k + 1) * T] for k in range(8)]
            dring.slots = [banks[0], banks[1], banks[4], banks[5]]
            busy = [fence]
            for part, n in enumerate(PARTS):
                toks, keep = [], {}

                def evac(m, bank, tok, toks=toks, keep=keep, busy=busy):
                    if m % 2 == 0:
                        s = tmp.take()
                        t = put("act", lambda e: e.activation(s.ap, bank.ap, ACT.Silu), tok, s.free)
                        bank.free = [t]
                        keep["s"], keep["t"] = s, t
                    else:
                        s, t0, k = keep["s"], keep["t"], m // 2
                        t = put("dve", lambda e: e.tensor_tensor(s.ap, bank.ap, s.ap, ALU.mult), tok, t0)
                        bank.free = [t]
                        pair = split_to(fh[k], fl[k], s.ap, t, busy[0])
                        s.free = pair
                        toks.append(pair)
                drain(fm(2 * n, (hh, hl), h_tok, evac, lead=3 if part == 0 else 1))
                if part == 2:
                    h_busy[0] = [last_pe[0]]

                def evac_d(m, bank, tok, part=part):
                    residual(m, bank, tok, part == 2 and not last)
                    if part == 2 and last:
                        t_out.append(Q.dma("sp", dsem(f"out{m}"), out[:, m, :], xt[m], x_tok[m]))
                drain(fm(8, (fh, fl), toks, evac_d, ((0, n),), lead=2))
                busy = [[last_pe[0]]]
            return fence_of(Q)

        t_out = []
        fence = ffn("a", G_FFN, fence_of(Q), False)

        ph = ExitStack()
        P2 = sbt(ph, "P2", 20 * T)
        ph.close()
        VD, OM2 = P2[:, 0:8 * T], P2[:, 8 * T:16 * T]
        qr = Ring([P2[:, (16 + k) * T:(17 + k) * T] for k in range(2)])
        kr = Ring([P2[:, (18 + k) * T:(19 + k) * T] for k in range(2)])
        for s in qr.slots + kr.slots:
            s.free = [fence]
        table("natural_log_exp_and_others")
        h_tok = norm_apply(G_AT0, stat_finish())
        lam = LBT[:, 60:61]
        lp = GP[:, G_LAM:G_LAM + 256]
        tl = []
        for k in range(2):
            t = put("dve", lambda e, k=k: e.tensor_tensor(
                SM[:, 64 * k:64 * k + 64], lp[:, 128 * k:128 * k + 64], lp[:, 128 * k + 64:128 * k + 128], ALU.mult),
                fence, t_gp)
            tl.append(put("dve", lambda e, k=k: e.tensor_reduce(
                LBT[:, 56 + k:57 + k], SM[:, 64 * k:64 * k + 64], AX.X, ALU.add), t))
        t = put("act", lambda e: e.activation(LBT[:, 58:60], LBT[:, 56:58], ACT.Exp), tl)
        t = put("dve", lambda e: e.tensor_tensor(lam, LBT[:, 59:60], LBT[:, 58:59], ALU.subtract), t)
        t_lam = put("dve", lambda e: e.tensor_scalar(lam, lam, -LAMBDA_INIT, None, ALU.add), t)
        sm_free.clear()

        t_vd = []
        for half_ in range(2):
            def evac_v(i, bank, tok, half_=half_):
                c = i * 1024 + half_ * 512
                t = put("act", lambda e: e.activation(VD[:, c:c + 512], bank.ap, ACT.Copy), tok, fence)
                bank.free = [t]
                t_vd.append(t)
            tbanks[0] = banks[4:8] if half_ else banks[0:4]
            drain(tm(512, 2, h_tok, evac_v))

        heads, cur, over = {}, [0], [0]

        def evac_qk(m, bank, tok):
            ring, gc = (qr, gq8[1]) if m % 2 == 0 else (kr, GP[:, G_DK:G_DK + 1])
            s = ring.take()
            cur[0] = m + 1

            def done(t):
                heads[m] = (s, t)
            qk_norm(bank, tok, gc, True, s.ap, s.free, done)

        t_om2 = [None] * 8

        def da_step(hd, i):
            n = (i + 1) * 128
            z = {}

            def scores():
                need(heads, 2 * hd + 1)
                (qs, tq_), (ks, tk_) = heads[2 * hd], heads[2 * hd + 1]
                for c in range(2):
                    z[c] = softmax_stage(qs.ap[64 * c:64 * c + 64, i * 128:(i + 1) * 128],
                                         ks.ap[64 * c:64 * c + 64, 0:n], m_l, i * 128, n, [tq_, tk_])
                if i == 3:
                    last = Q.q["pe"][-1][2]
                    qs.free, ks.free = [last], [last]
                    over[0] += 1

            def weights():
                (p0, o0, t0), (p1_, o1, t1) = z[0], z[1]
                ta = put("dve", lambda e: e.reciprocal(SM[:, o0 + 2:o0 + 3], SM[:, o0 + 1:o0 + 2]), t0)
                tb = put("dve", lambda e: e.reciprocal(SM[:, o1 + 2:o1 + 3], SM[:, o1 + 1:o1 + 2]), t1)
                tb = put("dve", lambda e: e.tensor_scalar(
                    p1_.ap[:, 0:n], p1_.ap[:, 0:n], SM[:, o1 + 2:o1 + 3], lam, ALU.mult, ALU.mult), tb, t_lam)
                t = put("dve", lambda e: e.scalar_tensor_tensor(
                    p0.ap[:, 0:n], p0.ap[:, 0:n], SM[:, o0 + 2:o0 + 3], p1_.ap[:, 0:n], ALU.mult, ALU.add), ta, tb)
                sm_free[o0], sm_free[o1] = [t], [t]
                p1_.free = [t]
                z["s"], z["t2"] = turn(p0, range(i + 1), t)

            def values():
                for j in range(i + 1):
                    t = put("pe", lambda e, j=j: e.matmul(
                        ob.ap[:, i * 128:(i + 1) * 128], VD[:, j * 1024 + hd * 128:j * 1024 + (hd + 1) * 128],
                        z["s"].ap[:, j * 128:(j + 1) * 128], start=(i == 0), stop=(i == 3 and j == 3),
                        skip_group_check=True), z["t2"], t_vd, ob.free)
                z["s"].free = [t]
                if i == 3:
                    def done(t):
                        t_om2[hd] = t
                    head_norm(ob, t, LBT[:, 35:36], OM2[:, hd * T:(hd + 1) * T], fence, done)
            return scores, weights, values

        dring.slots = banks[0:2]
        att = pipeline([da_step(hd, i) for hd in range(8) for i in range(4)], (0, 1, 2))
        first_over[0] = False
        prj = then_out(fm(16, (hh, hl), h_tok, evac_qk), Splits(OM2, t_om2, att))
        drive(att, prj, 1.33, lambda: first_over[0] or cur[0] // 2 <= over[0] + 1)
        drain(prj)
        fence = ffn("b", G_F0, fence_of(Q), False)

        ph = ExitStack()
        P3 = sbt(ph, "P3", 23 * T)
        ph.close()
        KW = P3[:, 0:4 * 640].rearrange("p (k t) -> p k t", k=4)
        VW = P3[:, 5 * T:11 * T].rearrange("p (i k c) -> p i k c", i=4, k=4)
        OM3 = P3[:, 11 * T:19 * T]
        qw = Ring([P3[:, (19 + k) * T:(20 + k) * T] for k in range(3)])
        for s in qw.slots:
            s.free = [fence]
        t_zp = put("pool", lambda e: e.memset(P3[:, 0:11 * T], 0.0), fence)
        table("natural_log_exp_and_others")
        t_rs = stat_finish()
        h_tok = norm_apply(G_KV, t_rs)
        NS = SM[:, 64:80]
        t_ns = put("dve", lambda e: e.tensor_scalar(NS, GP[:, G_SINK:G_SINK + 16], -1.0, None, ALU.mult), fence)
        t_kw, t_vw = {}, []

        def evac_k(m, bank, tok):
            s = qw.take()

            def done(t):
                us = []
                for a in range(2):
                    for half in range(2):
                        us.append(put("act", lambda e, a=a, half=half: e.activation(
                            KW[64 * half:64 * half + 64, 2 * m + a, 128:640], s.ap[64 * a:64 * a + 64, :], ACT.Copy),
                            t, t_zp))
                    t_kw[2 * m + a] = us[-2:]
                s.free = us
            qk_norm(bank, tok, GP[:, G_SK:G_SK + 1], True, s.ap, s.free, done)

        def evac_vw(i, bank, tok):
            t = put("act", lambda e: e.activation(
                VW[:, i, :, 64:128], bank.ap[:, 0:256].rearrange("p (k c) -> p k c", k=4), ACT.Copy), tok, t_zp)
            bank.free = [t]
            t_vw.append(t)

        dring.slots = banks[0:2]
        drain(fm(2, (hh, hl), h_tok, evac_k))
        tbanks[0] = banks[4:8]
        drain(tm(256, 4, h_tok, evac_vw))
        flush()
        h_busy[0] = [last_pe[0]]
        h_tok = norm_apply(G_AT1, t_rs)
        pairs, cur, over = {}, [0], [0]

        def evac_qw(m, bank, tok):
            s = qw.take()
            cur[0] = m + 1

            def done(t):
                pairs[m] = (s, t)
            qk_norm(bank, tok, gq8[2], True, s.ap, s.free, done)

        t_om3 = [None] * 8

        def sw_step(h, i):
            pair, half, kv = h // 2, h % 2, h // 4
            z = {}

            def scores():
                need(pairs, pair)
                qs, tq_ = pairs[pair]
                z["p"], z["o"], z["t"] = softmax_stage(
                    qs.ap[64 * half:64 * half + 64, i * 128:(i + 1) * 128],
                    KW[64 * half:64 * half + 64, kv, i * 128:i * 128 + 256], m_ul if i else m_fl, 0, 256,
                    [tq_, t_kw[kv], t_zp], (GP[:, G_SINK + h:G_SINK + h + 1], NS[:, h:h + 1], t_ns))
                if half == 1 and i == 3:
                    qs.free = [Q.q["pe"][-1][2]]
                    over[0] += 1

            def weights():
                o, p = z["o"], z["p"]
                t = put("dve", lambda e: e.tensor_tensor(
                    SM[:, o + 2:o + 3], SM[:, o + 1:o + 2], SM[:, o + 3:o + 4], ALU.add), z["t"])
                t = put("dve", lambda e: e.reciprocal(SM[:, o + 4:o + 5], SM[:, o + 2:o + 3]), t)
                t = put("dve", lambda e: e.tensor_scalar(p.ap[:, 0:256], p.ap[:, 0:256], SM[:, o + 4:o + 5],
                                                         None, ALU.mult), t)
                sm_free[o] = [t]
                z["s"], z["t2"] = turn(p, (0, 1) if i else (1,), t)

            def values():
                js = (i - 1, i) if i else (0,)
                for k, j in enumerate(js):
                    v = VW[:, j, kv, :]
                    v = v[:, 64:192] if half == 0 else v[:, 0:128]
                    t = put("pe", lambda e, k=k, v=v: e.matmul(
                        ob.ap[:, i * 128:(i + 1) * 128], v, z["s"].ap[:, k * 128:(k + 1) * 128],
                        start=(half == 0 and i == 0), stop=(half == 1 and i == 3 and k == 1),
                        skip_group_check=True), z["t2"], t_vw, t_zp, ob.free)
                z["s"].free = [t]
                if half == 1 and i == 3:
                    t_om3[pair] = put("act", lambda e: e.activation(
                        OM3[:, pair * T:(pair + 1) * T], ob.ap, ACT.Copy), t, fence)
                    ob.free = [t_om3[pair]]
            return scores, weights, values

        att = pipeline([sw_step(h, i) for h in range(16) for i in range(4)], (0, 2, 3))
        first_over[0] = False
        prj = then_out(fm(8, (hh, hl), h_tok, evac_qw), Splits(OM3, t_om3, att))
        drive(att, prj, 0.34, lambda: first_over[0] or cur[0] <= over[0] + 2)
        drain(prj)
        ffn("c", G_F1, fence_of(Q), True)

        Q.count()
        block = ctx.enter_context(nc.Block())

        @block.sync
        def _(e):
            Q.emit("sp", e, sems)
            for t in t_out:
                e.wait_ge(t.eng, t.val)

        @block.gpsimd
        def _(e):
            Q.emit("pool", e, sems)

        @block.scalar
        def _(e):
            Q.emit("act", e, sems)

        @block.vector
        def _(e):
            Q.emit("dve", e, sems)

        @block.tensor
        def _(e):
            Q.emit("pe", e, sems)


def constants():
    p = np.arange(128)
    cf = np.zeros((128, C_N), np.float32)
    cf[:, C_ID:C_ID + 128] = np.eye(128)
    cf[:, C_BO:C_BO + 128] = (p[:, None] // 64) == (p[None, :] // 64)
    cf[:, C_ON:C_ON + 128] = 1.0
    for d in range(128):
        if d % 64 < 32:
            cf[d + 32, C_PM + d] = -1.0
        else:
            cf[d - 32, C_PM + d] = 1.0
    end = np.arange(32) * 16 + 31
    for i in range(4):
        t = i * 128 + p
        cf[:, C_MC + 32 * i:C_MC + 32 * i + 32] = np.where(end[None, :] <= t[:, None], 0.0, -1e30)
        cf[:, C_MC + 32 * i + 31] = -1e30
        cf[:, C_VA + i] = t >= 31
    inv = (np.float32(1.0) / (np.float32(10000.0) ** (np.arange(0, 64, 2, dtype=np.float32) / np.float32(64))))
    cf[:, C_INV] = inv.astype(np.float32)[p % 32]
    cf[:, C_EPS] = EPS
    cf[:, C_HPI] = np.pi / 2
    cf[:, C_RM:C_RM + 512] = (np.arange(512) % 64 != 0)[None, :]
    cb = np.zeros((128, 640), np.float32)
    cb[:, 0:128] = np.eye(128)
    cb[:, 128:256] = -1e30
    low = np.where(p[None, :] <= p[:, None], 0.0, -1e30)
    cb[:, 256:384] = low
    cb[:, 384:512] = np.where(p[None, :] > p[:, None], 0.0, -1e30)
    cb[:, 512:640] = low
    ci = np.zeros((128, 8 * 128), np.float32)
    for lv in range(7):
        m = 1 << lv
        s, t = p[:, None], p[None, :]
        ci[:, lv * 128:(lv + 1) * 128] = (s // (2 * m) == t // (2 * m)) & (s % (2 * m) < m) & (t % (2 * m) >= m)
    return cf, cb, ci


def kernel(**inputs):
    import ml_dtypes
    import concourse.bacc as _bacc
    from concourse.bass_utils import run_bass_kernel_spmd as _run

    a = {k: np.asarray(v) for k, v in inputs.items()}

    def cols(w, n):
        k, m = w.shape
        return w.reshape(k // 128, 128, m // n, n).transpose(2, 1, 0, 3).reshape(m // n, 128, (k // 128) * n)

    def rows(w, per):
        k, m = w.shape
        return w.reshape(k // 128 // per, per, 128, m).transpose(0, 2, 1, 3).reshape(k // 128 // per, 128, per * m)

    cf, cb, ci = constants()
    w = a["w_in"][0]
    o = [0]
    for s in (512, 128, 128, 128, 128, 128, 128, 24, 512, 512, 512, 512):
        o.append(o[-1] + s)
    part = [w[:, o[i]:o[i + 1]] for i in range(12)]
    wq, wkc, wvc, wks, wvs, wkw, wvw, wg, whq, whf, whi, whg = part
    D = {"c_f": cf, "c_b": cb.astype(ml_dtypes.bfloat16), "c_i": ci}
    D["xT"] = a["x"][0].reshape(512, 8, 128).transpose(2, 1, 0)
    D["pos"] = a["positions_2"].reshape(512)
    D["w_in"] = cols(np.concatenate([wkc, wvc, wks, wkw, wq], 1), 128)
    D["w_ing"] = rows(np.concatenate([wvs, wvw, wg], 1), 2)
    D["w_inh"] = cols(np.concatenate([whf, whq, whg], 1), 128)
    D["w_inv"] = rows(whi, 2)
    D["w_out"] = cols(a["w_out"][0], 128)
    for n, gu, dn in ((1, a["w_gate_up"][0], a["w_down"][0]), (2, a["w_gate_up_2"][0], a["w_down_2"][0]),
                      (3, a["w_gate_up_2"][1], a["w_down_2"][1])):
        D[f"wgu{n}"] = cols(gu, 128)
        D[f"wd{n}"] = cols(dn, 128)
    qkv = a["da_w_qkv_2"][0]
    D["da_v"] = np.concatenate([rows(qkv[:, 2048:2560], 2), rows(qkv[:, 2560:3072], 2)], 0)
    qk = np.stack([qkv[:, 0:1024].reshape(1024, 8, 128), qkv[:, 1024:2048].reshape(1024, 8, 128)], 2)
    D["da_qk"] = cols(qk.reshape(1024, 2048), 128)
    D["da_o"] = cols(a["da_w_o_2"][0], 128)
    D["sw_k"] = cols(a["w_kv_2"][:, 0:256], 128)
    D["sw_v"] = rows(a["w_kv_2"][:, 256:512], 4)
    D["sw_q"] = cols(a["sw_w_q_2"][0], 128)
    D["sw_o"] = cols(a["sw_w_o_2"][0], 128)
    D["cmp_w1"] = np.stack([a[n][0].reshape(16, 128, 128).transpose(1, 0, 2).reshape(128, 2048)
                            for n in ("cmp_k_w1", "cmp_v_w1")], 0)
    D["cmp_w2"] = np.concatenate([a["cmp_k_w2"][0], a["cmp_v_w2"][0]], 1)

    def g8(v):
        return v.reshape(8, 128).T

    def col(v):
        v = v.reshape(-1, 1)
        return np.concatenate([v, v], 0) if v.shape[0] == 64 else v

    def line(v):
        return np.broadcast_to(v.reshape(1, -1), (128, v.size))

    lb = a["hgrn_lb_logits"].reshape(2, 4, 128).transpose(2, 0, 1).reshape(128, 8)
    pk = [np.concatenate([a[n][0].T, a[n][0].T], 0) for n in ("cmp_pos_k", "cmp_pos_v")]
    D["gp"] = np.concatenate([
        g8(a["norm_mix"][0]), g8(a["norm_ffn"][0]), g8(a["attn_norm_2"][0]), g8(a["attn_norm_2"][1]),
        g8(a["ffn_norm_2"][0]), g8(a["ffn_norm_2"][1]), g8(a["kv_norm_2"]),
        col(a["q_norm"][0]), col(a["k_norm"][0, 1]), col(a["k_norm"][0, 2]), col(a["da_q_norm_2"][0]),
        col(a["da_k_norm_2"][0]), col(a["da_subln_2"][0]), col(a["sw_q_norm_2"][0]), col(a["k_norm_2"]),
        col(a["hgrn_o_norm"][0]), lb, pk[0], pk[1], line(a["k_norm"][0, 0]), line(a["sw_sinks_2"][0]),
        line(a["da_lambda_2"][0])], 1)

    nc = _bacc.Bacc("TRN2", target_bir_lowering=False, num_devices=1)
    arrays, aps = {}, {}
    for name, v in D.items():
        v = np.ascontiguousarray(v)
        arrays["in_" + name] = v
        aps[name] = nc.dram_tensor("in_" + name, v.shape, mybir.dt.from_np(v.dtype), kind="ExternalInput").ap()
    out = nc.dram_tensor("out_xT", (128, 8, 512), mybir.dt.float32, kind="ExternalOutput").ap()
    program(nc, aps, out)
    r = _run(nc, [arrays], core_ids=[0])
    y = np.asarray(r.results[0]["out_xT"])
    return np.ascontiguousarray(y.transpose(2, 1, 0).reshape(1, 512, 1024))
```

```python
from contextlib import ExitStack

import numpy as np
import concourse.bass as bass
from concourse import mybir

F = mybir.dt.float32
R = mybir.dt.float32r
BF = mybir.dt.bfloat16
I32 = mybir.dt.int32
U8 = mybir.dt.uint8
ALU = mybir.AluOpType
ACT = mybir.ActivationFunctionType
AX = mybir.AxisListType

T = 512
EPS = 1e-6
NSA_PER_PROJ, HGRN_PER_NSA, PROJ_PER_DA, PROJ_PER_SW = 1.3, 0.65, 1.2, 0.25
DA_LEAD, SW_LEAD = 64, 20
PARTS = (8, 8, 6)
CH = 1024
NRAW, NW = 2, 4
AHEAD = 8
ORDER = ((2, 3), (0, 0), (1, 1), (3, 4))

C_ID, C_BO, C_ON, C_PM, C_MC, C_VA, C_INV, C_EPS, C_HPI, C_RM = 0, 128, 256, 384, 512, 640, 644, 645, 646, 704
C_N = 704 + 512
G_MIX, G_FFN, G_AT0, G_AT1, G_F0, G_F1, G_KV = 0, 8, 16, 24, 32, 40, 48
G_Q, G_KS, G_KW, G_DQ, G_DK, G_SUB, G_SQ, G_SK, G_HO = 56, 57, 58, 59, 60, 61, 62, 63, 64
G_LB, G_PK, G_PV, G_KC, G_SINK, G_LAM = 65, 73, 105, 137, 201, 217
G_N = 217 + 256
LAMBDA_INIT = 0.2


class Tok:

    def __init__(self, eng, val=0):
        self.eng, self.val, self.need = eng, val, False


class Slot:

    def __init__(self, ap):
        self.ap, self.held, self.after = ap, False, []

    @property
    def free(self):
        return self.after

    @free.setter
    def free(self, after):
        self.after, self.held = after, False


class Ring:
    def __init__(self, aps):
        self.slots, self.n = [Slot(a) for a in aps], 0

    def take(self):
        s = self.slots[self.n % len(self.slots)]
        self.n += 1
        assert not s.held, "the slot's last user has not given it back"
        s.held = True
        return s


class Operand:

    def __init__(self, hi, lo):
        self.hi, self.lo, self.busy = hi, lo, []


def flat(after):
    for a in after:
        if a is None:
            continue
        if isinstance(a, (list, tuple)):
            yield from flat(a)
        else:
            yield a


class Queues:

    def __init__(self):
        self.q = {k: [] for k in ("pe", "act", "dve", "pool", "sp")}

    def put(self, eng, fn, *after):
        tok = Tok(eng)
        waits = [a for a in flat(after) if not (eng == "pe" and a.eng == "pe")]
        for a in waits:
            a.need = True
        self.q[eng].append((fn, waits, tok))
        return tok

    def dma(self, eng, dsem, out, in_, *after):
        dsem[1] += 1
        tok = Tok(dsem[0], 16 * dsem[1])
        waits = list(flat(after))
        for a in waits:
            a.need = True
        sem = dsem[0]
        self.q[eng].append((lambda e: e.dma_start(out, in_).then_inc(sem, 16), waits, None))
        return tok

    def count(self):
        for q in self.q.values():
            n = 0
            for _, _, tok in q:
                if tok is not None and tok.need:
                    n += 1
                    tok.val = n

    def emit(self, name, eng, sems):
        seen = {}
        for fn, waits, tok in self.q[name]:
            need = {}
            for a in waits:
                need[a.eng] = max(need.get(a.eng, 0), a.val)
            for k, v in need.items():
                if seen.get(k, 0) < v:
                    eng.wait_ge(sems[k] if isinstance(k, str) else k, v)
                    seen[k] = v
            ins = fn(eng)
            if tok is not None and tok.need:
                ins.then_inc(sems[name], 1)


def fence_of(queues):
    return [q[-1][2] for k, q in queues.q.items() if k != "sp" and q]


def step(g):
    try:
        next(g)
        return True
    except StopIteration:
        return False


def drain(g):
    for _ in g:
        pass


def pipeline(steps, order):
    n = len(steps)
    for t in range(n + max(lag for _, lag in order)):
        for k, lag in order:
            if 0 <= t - lag < n:
                steps[t - lag][k]()
                yield


def program(nc, D, out):
    Q = Queues()
    put = Q.put
    ctx = ExitStack()

    def sbt(stack, name, cols, dt=F, parts=128):
        return stack.enter_context(nc.sbuf_tensor(name, [parts, cols], dt))

    def sem(name):
        return ctx.enter_context(nc.semaphore(name))

    with ctx:
        XT = sbt(ctx, "XT", 8 * T)
        hx = ExitStack()
        HH = sbt(hx, "HH", 8 * T, R)
        HL = sbt(hx, "HL", 8 * T, R)
        hx.close()
        HX = sbt(ctx, "HX", 16 * T)
        RAW = sbt(ctx, "RAW", NRAW * CH)
        WH = sbt(ctx, "WH", NW * CH, R)
        WL = sbt(ctx, "WL", NW * CH, R)
        CF = sbt(ctx, "CF", C_N)
        CB = sbt(ctx, "CB", 128 * 5, BF)
        CI = sbt(ctx, "CI", 128 * 8, U8)
        GP = sbt(ctx, "GP", G_N)
        RC = sbt(ctx, "RC", T)
        RSN = sbt(ctx, "RSN", T)
        SQB = sbt(ctx, "SQB", 2 * T)
        ACC = sbt(ctx, "ACC", T)
        RST = sbt(ctx, "RST", T)
        TMP = sbt(ctx, "TMP", 4 * T)
        PB = sbt(ctx, "PB", 6 * T)
        SM = sbt(ctx, "SM", 256)
        LBT = sbt(ctx, "LBT", 64)

        banks = [Slot(ctx.enter_context(nc.psum_tensor(f"bank{i}", [128, 512], F))[:, :]) for i in range(8)]
        sems = {k: sem("s_" + k) for k in ("pe", "act", "dve", "pool", "sp")}
        d_raw = [[sem(f"d_raw{i}"), 0] for i in range(NRAW)]
        d_one = {}

        def dsem(name):
            d_one[name] = [sem("d_" + name), 0]
            return d_one[name]

        ident = CF[:, C_ID:C_ID + 128]
        bones = CF[:, C_BO:C_BO + 128]
        ones = CF[:, C_ON:C_ON + 128]
        perm = CF[:, C_PM:C_PM + 128]
        eps = CF[:, C_EPS:C_EPS + 1]
        identb = CB[:, 0:128]
        m_fl = CB[:, 128:384]
        m_l = CB[:, 256:384]
        m_ul = CB[:, 384:640]

        t_gp = Q.dma("sp", dsem("gp"), GP[:, :], D["gp"])
        t_x = [Q.dma("sp", dsem(f"x{m}"), XT[:, m * T:(m + 1) * T], D["xT"][:, m, :]) for m in range(2)]

        raw = [RAW[:, i * CH:(i + 1) * CH] for i in range(NRAW)]
        whs = [WH[:, i * CH:(i + 1) * CH] for i in range(NW)]
        wls = [WL[:, i * CH:(i + 1) * CH] for i in range(NW)]
        units = []
        st = {"load": 0, "split": 0, "use": 0, "done": 0}
        t_load, t_split, t_used, work = {}, {}, {}, []

        def load_to(j):
            while st["load"] < min(j, len(units)):
                s = st["load"]
                n = units[s].shape[1]
                t_load[s] = Q.dma("sp", d_raw[s % NRAW], raw[s % NRAW][:, 0:n], units[s], t_split.get(s - NRAW))
                st["load"] += 1

        def pump():
            while st["split"] < min(st["done"] + NW, len(units)):
                s = st["split"]
                st["split"] += 1
                n = units[s].shape[1]
                half = (n // 2 + 1) // 2 * 2
                toks = [None, None]

                def high(c, a, b, s=s, toks=toks):
                    load_to(s + 1)
                    toks[c] = put("act", lambda e: e.activation(
                        whs[s % NW][:, a:b], raw[s % NRAW][:, a:b], ACT.Copy), t_load[s], t_used.get(s - NW))

                def low(c, a, b, s=s, toks=toks):
                    t = put("dve", lambda e: e.tensor_tensor(
                        wls[s % NW][:, a:b], raw[s % NRAW][:, a:b], whs[s % NW][:, a:b].bitcast(F), ALU.subtract),
                        toks[c], t_used.get(s - NW))
                    toks[c] = [toks[c], t]
                    if c == 1:
                        t_split[s] = toks
                        load_to(s + 1 + NRAW)
                work.extend([lambda f=high, b=half: f(0, 0, b), lambda f=high, a=half, b=n: f(1, a, b),
                             lambda f=low, b=half: f(0, 0, b), lambda f=low, a=half, b=n: f(1, a, b)])

        def next_unit():
            pump()
            j = st["use"]
            while j not in t_split:
                work.pop(0)()
            st["use"] += 1
            return j, whs[j % NW], wls[j % NW], t_split[j]

        def unit_done(j, tok):
            t_used[j] = tok
            while st["done"] in t_used:
                st["done"] += 1
            pump()

        waiting = []

        def later(n, fn):
            waiting.append([n, fn])

        def tick():
            if work:
                work.pop(0)()
            for w in waiting:
                w[0] -= 1
            due = [w for w in waiting if w[0] <= 0]
            waiting[:] = [w for w in waiting if w[0] > 0]
            for _, fn in due:
                fn()

        def drive(a, b, ratio, gate=lambda: True):
            acc, left = 0.0, True
            while step(a):
                acc += ratio
                while acc >= 1:
                    acc -= 1
                    if left and gate():
                        left = step(b)
                    else:
                        tick()
            return left

        def flush():
            while waiting:
                waiting.pop(0)[1]()

        hh = [HH[:, k * T:(k + 1) * T] for k in range(8)]
        hl = [HL[:, k * T:(k + 1) * T] for k in range(8)]
        sqr = Ring([SQB[:, i * T:(i + 1) * T] for i in range(2)])
        tmp = Ring([TMP[:, i * T:(i + 1) * T] for i in range(4)])
        dring = Ring([None, None])
        dring.slots = banks[0:2]
        xt = [XT[:, m * T:(m + 1) * T] for m in range(8)]
        acc_st = {"n": 0, "tok": None, "free": []}
        last_pe = [None]
        t_scan = []
        E2 = [PB[:, 3 * T:4 * T]]
        g_tok = [None]

        def three(bank, w, x, first, last, wait, n=None, tok_major=False):
            (wh_, wl_), (xh_, xl_) = w, x
            pairs = ((wh_, xh_), (wh_, xl_), (wl_, xh_))
            t = None
            for k, (a, b) in enumerate(pairs):
                l_, r_ = (b, a) if tok_major else (a, b)
                t = put("pe", lambda e, l_=l_, r_=r_, s=(first and k == 0), p=(last and k == 2): e.matmul(
                    bank, l_, r_, start=s, stop=p), wait if k == 0 else ())
            return t

        def fm(n_m, xs, x_toks, evac, k_units=((0, 8),), lead=1):
            m, k_end = 0, k_units[-1][1]
            while m < n_m:
                g = min(lead if m == 0 else 1, n_m - m)
                while any(dring.slots[(dring.n + q) % len(dring.slots)].held for q in range(g)):
                    tick()
                bk = [dring.take() for _ in range(g)]
                us = [next_unit() for _ in range(g)]
                for k in range(k_end):
                    for q in range(g):
                        j, w_h, w_l, w_t = us[q]
                        c = k * 128
                        tok = three(bk[q].ap, (w_h[:, c:c + 128], w_l[:, c:c + 128]), (xs[0][k], xs[1][k]),
                                    k == 0, k == k_end - 1, [w_t, x_toks[k], bk[q].free if k == 0 else None])
                        last_pe[0] = tok
                        if k == k_end - 1:
                            unit_done(j, tok)
                            evac(m + q, bk[q], tok)
                        tick()
                        yield
                m += g

        tbanks = [banks[0:4]]

        def tm(ncols, per_unit, x_toks, evac, op=None):
            k = 0
            for u in range(8 // per_unit):
                j, w_h, w_l, w_t = next_unit()
                for kk in range(per_unit):
                    c = kk * ncols
                    for i in range(4):
                        bk = tbanks[0][i]
                        tok = three(bk.ap[:, 0:ncols], (w_h[:, c:c + ncols], w_l[:, c:c + ncols]),
                                    [(a[k] if op is None else b[k])[:, i * 128:(i + 1) * 128]
                                     for a, b in ((hh, op and op.hi), (hl, op and op.lo))],
                                    k == 0, k == 7, [w_t, x_toks[k], bk.free if k == 0 else None],
                                    tok_major=True)
                        last_pe[0] = tok
                        if kk == per_unit - 1 and i == 3:
                            unit_done(j, tok)
                        if k == 7:
                            evac(i, bk, tok)
                        tick()
                        yield
                    k += 1

        def stat_add(m):
            s = sqr.take()
            t = put("act", lambda e: e.activation(s.ap, xt[m], ACT.Square), list(x_tok[m]), s.free)
            x_tok[m] = x_tok[m] + [t]
            if acc_st["n"] == 0:
                acc_st["tok"] = put("pool", lambda e: e.tensor_copy(ACC[:, :], s.ap), t, acc_st["free"])
            else:
                acc_st["tok"] = put("pool", lambda e: e.tensor_tensor(ACC[:, :], ACC[:, :], s.ap, ALU.add),
                                    t, acc_st["tok"])
            s.free = [acc_st["tok"]]
            acc_st["n"] = (acc_st["n"] + 1) % 8

        def rstd_from(bank, tok, scale, dst, dst_free):
            s = tmp.take()
            t1 = put("act", lambda e: e.activation(s.ap, bank.ap, ACT.Ln, bias=eps, scale=scale), tok, s.free)
            bank.free = [t1]
            t2 = put("act", lambda e: e.activation(dst, s.ap, ACT.Exp, scale=-0.5), t1, dst_free)
            s.free = [t2]
            return t2

        def split_to(dh, dl, src, tok, busy):
            th = put("act", lambda e: e.activation(dh, src, ACT.Copy), tok, busy)
            tl = put("dve", lambda e: e.tensor_tensor(dl, src, dh.bitcast(F), ALU.subtract), th, busy)
            return [th, tl]

        def scaled_split(m, g0, dst):
            g = GP[:, g0 + m:g0 + m + 1]
            hi, lo = dst.hi[m], dst.lo[m]
            th = put("dve", lambda e: e.tensor_scalar(hi, xt[m], g, None, ALU.mult), x_tok[m], dst.busy, t_gp)
            tl = put("dve", lambda e: e.scalar_tensor_tensor(
                lo, xt[m], g, hi.bitcast(F), ALU.mult, ALU.subtract), th)
            x_tok[m] += [th, tl]
            return [th, tl]

        rs = {"rst": None, "e2": None, "tok": None, "readers": []}

        def stat_lazy():
            b = banks[3]
            busy = rs["readers"]
            t = put("pe", lambda e: e.matmul(b.ap, ones, ACC[:, :], start=True, stop=True),
                    acc_st["tok"], b.free, t_cf)
            e2 = E2[0]
            t2 = put("dve", lambda e: e.tensor_scalar(e2, b.ap, EPS / 1024, EPS * EPS, ALU.mult, ALU.add),
                     t, busy, t_scan)
            b.free = [t2]
            s = tmp.take()
            t3 = put("act", lambda e: e.activation(s.ap, e2, ACT.Ln, scale=1.0 / EPS), t2, s.free)
            rs["rst"] = put("act", lambda e: e.activation(RST[:, :], s.ap, ACT.Exp, scale=-0.5), t3, busy)
            s.free = [rs["rst"]]
            rs["e2"] = t2
            for i in range(4):
                t = put("pe", lambda e, i=i: e.matmul(b.ap[:, 2 * i:2 * i + 2], ACC[:, i * 128:(i + 1) * 128],
                                                      ones[:, 0:2], start=True, stop=True), b.free, t2)
            acc_st["free"] = [t]
            c = LBT[:, 24:28]
            t = put("act", lambda e: e.activation(c, b.ap[:, 0:8:2], ACT.Ln, bias=eps, scale=1.0 / 1024), t, busy)
            b.free = [t]
            rs["tok"] = put("act", lambda e: e.activation(c, c, ACT.Exp, scale=-0.5), t)
            rs["readers"] = []

        def residual(m, bank, tok, nxt):
            t = put("dve", lambda e: e.tensor_tensor(xt[m], bank.ap, xt[m], ALU.add), tok, x_tok[m])
            bank.free = [t]
            x_tok[m] = [t]
            if nxt:
                stat_add(m)
                nxt[2].append(scaled_split(m, nxt[0], nxt[1]))
                if m == 7:
                    later(10, stat_lazy)

        def qk_norm(bank, tok, gcol, rope, dst, dst_free, done):
            s = sqr.take()
            t0 = put("act", lambda e: e.activation(s.ap, bank.ap, ACT.Square), tok, s.free)
            b3 = banks[3]

            def scale():
                t1 = put("pe", lambda e: e.matmul(b3.ap, bones, s.ap, start=True, stop=True), t0, b3.free)
                s.free = [t1]
                r = tmp.take()
                e2 = E2[0]
                t2 = put("dve", lambda e: e.scalar_tensor_tensor(
                    r.ap, b3.ap, 1.0 / 64, e2, ALU.mult, ALU.add), t1, rs["e2"], r.free)
                rs["readers"].append(t2)
                b3.free = [t2]
                t2 = put("act", lambda e: e.activation(r.ap, r.ap, ACT.Ln), t2)
                t2 = put("act", lambda e: e.activation(r.ap, r.ap, ACT.Exp, scale=-0.5), t2)
                if not rope:
                    t3 = put("dve", lambda e: e.scalar_tensor_tensor(
                        dst, bank.ap, gcol, r.ap, ALU.mult, ALU.mult), t2, t0, dst_free, g_tok[0])
                    bank.free = [t3]
                    r.free = [t3]
                    done(t3)
                    return
                n = tmp.take()
                t3 = put("dve", lambda e: e.scalar_tensor_tensor(
                    n.ap, bank.ap, gcol, r.ap, ALU.mult, ALU.mult), t2, t0, n.free, g_tok[0])
                bank.free = [t3]
                t5 = put("pool", lambda e: e.tensor_tensor(dst, n.ap, RC[:, :], ALU.mult), t3, dst_free, t_rope)

                def turned():
                    t4 = put("pe", lambda e: e.matmul(b3.ap, perm, n.ap, start=True, stop=True), t3, b3.free)
                    n.free = [t4, t5]
                    t6 = put("dve", lambda e: e.tensor_tensor(r.ap, b3.ap, RSN[:, :], ALU.mult), t4, t_rope, t3)
                    b3.free = [t6]
                    t7 = put("dve", lambda e: e.tensor_tensor(dst, dst, r.ap, ALU.add), t6, t5)
                    r.free = [t7]
                    done(t7)
                later(5, turned)
            later(2, scale)

        def head_norm(bank, tok, gcol, dst, dst_free, done, stat_bank=None, wait=2):
            s = sqr.take()
            t0 = put("act", lambda e: e.activation(s.ap, bank.ap, ACT.Square), tok, s.free)
            tc = put("act", lambda e: e.activation(dst, bank.ap, ACT.Copy), tok, dst_free)
            bank.free = [t0, tc]

            def scale():
                b3 = stat_bank.take() if stat_bank else banks[3]
                t1 = put("pe", lambda e: e.matmul(b3.ap, ones, s.ap, start=True, stop=True), t0, b3.free)
                s.free = [t1]
                r = tmp.take()
                t2 = rstd_from(b3, t1, 1.0 / 128, r.ap, r.free)
                t3 = put("dve", lambda e: e.scalar_tensor_tensor(
                    dst, dst, gcol, r.ap, ALU.mult, ALU.mult), t2, tc, g_tok[0])
                r.free = [t3]
                done(t3)
            later(wait, scale)

        ph = ExitStack()
        P1 = sbt(ph, "P1", 38 * T + 352)
        ph.close()

        def p1(a, n):
            return P1[:, a * T:a * T + n]

        ktt = [[p1(2 * b + g, T) for g in range(2)] for b in range(2)]
        qtt = [p1(4 + p, T) for p in range(4)]
        VP, PTC = p1(8, 6 * T), p1(14, 2 * T)
        OM, HV = p1(16, 4 * T), p1(20, 4 * T)
        w1k, w1v = p1(16, 4 * T), p1(20, 4 * T)
        xc = [p1(32, T), p1(33, T)]
        xb = p1(34, 992).rearrange("p (l g n) -> p l g n", l=16, g=2)
        hf, hq, hg = p1(24, 4 * T), p1(28, 4 * T), p1(32, 4 * T)
        h3 = [p1(24 + k, T) for k in range(12)]
        VC = p1(36, T)
        W2, KC, KCT = P1[:, 37 * T:37 * T + 128], P1[:, 37 * T + 128:37 * T + 192], P1[:, 37 * T + 192:37 * T + 320]
        HG = P1[:, 38 * T:38 * T + 256]
        GT = P1[:, 38 * T + 256:38 * T + 352]
        ra, rk, ri = [PB[:, k * T:(k + 1) * T] for k in range(3)]

        def ffn_units(gu, dn):
            found, j0 = [], 0
            for n in PARTS:
                for j in range(j0, j0 + n):
                    found += [gu[j], gu[22 + j]]
                found += [dn[m, :, j0 * 128:(j0 + n) * 128] for m in range(8)]
                j0 += n
            return found

        for name, n in (("w_in", 8), ("w_ing", 4), ("w_inv", 4), ("w_inh", 12), ("w_out", 8)):
            units += [D[name][u] for u in range(n)]
        units += ffn_units(D["wgu1"], D["wd1"])
        for name, n in (("da_v", 8), ("da_qk", 16), ("da_o", 8)):
            units += [D[name][u] for u in range(n)]
        units += ffn_units(D["wgu2"], D["wd2"])
        for name, n in (("sw_k", 2), ("sw_v", 2), ("sw_q", 8), ("sw_o", 8)):
            units += [D[name][u] for u in range(n)]
        units += ffn_units(D["wgu3"], D["wd3"])

        load_to(2)
        t_x += [Q.dma("sp", dsem(f"x{m}"), XT[:, m * T:(m + 1) * T], D["xT"][:, m, :]) for m in range(2, 8)]
        x_tok = [[t] for t in t_x]
        t_cf = Q.dma("sp", dsem("cf"), CF[:, :], D["c_f"])
        t_cb = Q.dma("sp", dsem("cb"), CB[:, :], D["c_b"])
        t_pos = Q.dma("sp", dsem("pos"), ri.bitcast(I32), D["pos"].partition_broadcast(128))
        t_ci = Q.dma("sp", dsem("ci"), p1(8, 1024), D["c_i"])

        t_rope = []

        def table(name, tok=None):
            put("act", lambda e: e.preload_act_table_set(name), tok)

        def rope_tables():
            t = put("dve", lambda e: e.tensor_copy(ra, ri.bitcast(I32)), t_pos)
            t = put("dve", lambda e: e.tensor_scalar(ra, ra, CF[:, C_INV:C_INV + 1], None, ALU.mult), t, t_cf)
            magic = 12582912.0
            c = [6.28125]
            rest = 2 * np.pi - c[0]
            for bits in (7, 7):
                sc = 2.0 ** (bits - 1 - np.floor(np.log2(rest)))
                c.append(float(np.floor(rest * sc) / sc))
                rest -= c[-1]
            c.append(float(rest))
            for big in (4096.0, 1.0):
                t = put("dve", lambda e, big=big: e.tensor_scalar(
                    rk, ra, float(1.0 / (2 * np.pi * big)), magic, ALU.mult, ALU.add), t)
                t = put("dve", lambda e: e.tensor_scalar(rk, rk, -magic, None, ALU.add), t)
                yield
                for cc in c:
                    t = put("dve", lambda e, v=-cc * big: e.scalar_tensor_tensor(
                        ra, rk, v, ra, ALU.mult, ALU.add), t)
                    yield
            pi = 3.1415925
            t = put("dve", lambda e: e.tensor_scalar(ra, ra, -pi, pi, ALU.max, ALU.min), t)
            t1 = put("act", lambda e: e.activation(RSN[:, :], ra, ACT.Sin), t)
            t2 = put("act", lambda e: e.activation(rk, ra, ACT.Abs), t)
            t3 = put("act", lambda e: e.activation(RC[:, :], rk, ACT.Sin, scale=-1.0,
                                                   bias=CF[:, C_HPI:C_HPI + 1]), t2)
            table("natural_log_exp_and_others")
            t_rope.extend([t1, t3])

        table("natural_log_exp_and_others")
        oa = Operand(hh, hl)
        h_tok = []
        for m in range(8):
            stat_add(m)
            h_tok.append(scaled_split(m, G_MIX, oa))
            if m == 1:
                pump()
            if m in (1, 3, 5):
                for _ in range(4):
                    work.pop(0)()
        later(16, stat_lazy)
        t_w1 = []

        t_xc, t_kt, t_qt = [None, None], {}, [None] * 4
        t_ci = put("pool", lambda e: e.tensor_copy(CI[:, :], p1(8, 1024)), t_ci)
        t_z = put("pool", lambda e: e.memset(VP, 0.0), t_ci)
        t_zc = put("pool", lambda e: e.memset(VC, 0.0))
        t_zk = put("pool", lambda e: e.memset(KC, 0.0))
        t_zg = put("pool", lambda e: e.memset(HG, 0.0))

        def evac_in(m, bank, tok):
            if m < 2:
                t_xc[m] = put("dve", lambda e: e.tensor_tensor(xc[m], bank.ap, RST[:, :], ALU.mult), tok, rs["rst"])
                rs["readers"].append(t_xc[m])
                bank.free = [t_xc[m]]
            elif m < 4:
                s = tmp.take()

                def done(t):
                    us = []
                    for g in range(2):
                        for half in range(2):
                            us.append(put("act", lambda e, g=g, half=half: e.activation(
                                ktt[m - 2][g][64 * half:64 * half + 64, :], s.ap[64 * g:64 * g + 64, :], ACT.Copy),
                                t))
                        t_kt[m - 2, g] = us[-2:]
                    s.free = us
                qk_norm(bank, tok, GP[:, G_KS + m - 2:G_KS + m - 1], False, s.ap, s.free, done)
            else:
                def done(t):
                    t_qt[m - 4] = t
                qk_norm(bank, tok, gq8[0], False, qtt[m - 4], None, done)

        t_g8 = put("dve", lambda e: e.tensor_scalar(LBT[:, 32:33], GP[:, G_Q:G_Q + 1], 0.125, None, ALU.mult), t_gp)
        t_g8 = put("dve", lambda e: e.tensor_scalar(LBT[:, 33:34], GP[:, G_DQ:G_DQ + 1], 0.125, None, ALU.mult), t_g8)
        t_g8 = put("dve", lambda e: e.tensor_scalar(LBT[:, 34:35], GP[:, G_SQ:G_SQ + 1], 0.125, None, ALU.mult), t_g8)
        t_g8 = put("dve", lambda e: e.tensor_scalar(LBT[:, 35:36], GP[:, G_SUB:G_SUB + 1], 1.0 - LAMBDA_INIT,
                                                    None, ALU.mult), t_g8)
        t_g8 = put("dve", lambda e: e.tensor_scalar(LBT[:, 36:37], GP[:, G_HO:G_HO + 1], 0.5, None, ALU.mult), t_g8)
        gq8 = [LBT[:, 32:33], LBT[:, 33:34], LBT[:, 34:35]]
        g_tok[0] = t_g8

        rope = rope_tables()
        dring.slots = banks[0:3]
        prj = fm(8, (hh, hl), h_tok, evac_in, lead=3)
        for k in range(24):
            step(prj)
        t_w1 += [Q.dma("sp", dsem("w1k"), w1k, D["cmp_w1"][0]), Q.dma("sp", dsem("w1v"), w1v, D["cmp_w1"][1])]
        t_w2 = Q.dma("sp", dsem("w2"), W2, D["cmp_w2"])
        for k in range(12):
            step(prj)
        drive(rope, prj, 2)
        drain(prj)

        vp = VP.rearrange("p (i b c) -> p i b c", i=4, b=4)
        t_vp, t_gt = [None] * 4, [None] * 4

        def evac_vg(i, bank, tok):
            r_ = LBT[:, 24 + i:25 + i]
            t_vp[i] = put("dve", lambda e: e.tensor_scalar(
                vp[:, i, :, 64:128], bank.ap[:, 0:256].rearrange("p (b c) -> p b c", b=4), r_, None, ALU.mult),
                tok, t_z, rs["tok"])
            g = GT[:, i * 24:(i + 1) * 24]
            t = put("dve", lambda e: e.tensor_scalar(g, bank.ap[:, 256:280], r_, None, ALU.mult), tok, rs["tok"])
            bank.free = [t_vp[i], t]
            rs["readers"] += [t_vp[i], t]
            t = put("act", lambda e: e.activation(g, g, ACT.Exp, scale=-1.0), t)
            t = put("dve", lambda e: e.tensor_scalar(g, g, 1.0, None, ALU.add), t)
            t_gt[i] = put("dve", lambda e: e.reciprocal(g, g), t)

        tbanks[0] = banks[4:8]
        drain(tm(280, 2, h_tok, evac_vg))

        t_kc, t_vc, t_cmp_pe, t_ptc = [None, None], [], [], []
        pr = Ring([PB[:, i * T:(i + 1) * T] for i in range(4)])
        ptr_ = Ring([PB[:, (4 + i) * T:(5 + i) * T] for i in range(2)])
        for k in range(3):
            pr.slots[k].free = list(t_rope)
        pr.slots[3].free = list(rs["readers"])

        def compress():
            xb_free, hg_free = [], [t_zg]
            for kv in range(2):
                w1 = (w1k, w1v)[kv]
                pos0 = (G_PK, G_PV)[kv]
                tb = []
                for g in range(2):
                    src = xc[kv][64 * g:64 * g + 64, :].rearrange("p (n l) -> p l n", l=16)
                    for par in range(2):
                        for r in range(2):
                            c = pos0 + 16 * r + par
                            tb.append(put("dve", lambda e, g=g, par=par, r=r, c=c, src=src: e.tensor_tensor(
                                xb[64 * par:64 * par + 64, 8 * r:8 * r + 8, g, :], src[:, par::2, r:r + 31],
                                GP[64 * g:64 * g + 64, c:c + 15:2].unsqueeze(2).to_broadcast([64, 8, 31]),
                                ALU.add), t_xc[kv], t_gp, xb_free))
                        yield
                hid = banks[4]
                for l in range(16):
                    t = put("pe", lambda e, l=l, w1=w1: e.matmul(
                        hid.ap[:, 0:62], w1[:, l * 128:(l + 1) * 128], xb[:, l, :, :],
                        start=(l == 0), stop=(l == 15)), tb, t_w1[kv], hid.free)
                    if l % 4 == 3:
                        yield
                xb_free = [t]
                t_cmp_pe.extend([t, t_w2])
                tgs = []
                for r in range(4):
                    tgs.append(put("act", lambda e, r=r: e.activation(
                        HG.rearrange("p (g r n) -> p g r n", g=2, r=4)[:, :, r, 0:31],
                        hid.ap[:, 0:62].rearrange("p (g n) -> p g n", g=2), ACT.Gelu_apprx_tanh), t, hg_free))
                hid.free = tgs
                if kv == 0:
                    table("natural_log_exp_and_others")
                yield
                for g in range(2):
                    b6 = banks[6]
                    if kv == 0:
                        t = put("pe", lambda e, g=g: e.matmul(
                            b6.ap[0:32, 0:64], HG[:, g * 128:g * 128 + 32], W2[:, 0:64], start=True, stop=True),
                            tgs, t_w2, b6.free)
                        hg_free = [t]
                        o = 8 * g
                        ta = put("act", lambda e, o=o: e.activation(
                            KCT[0:32, 0:64], b6.ap[0:32, 0:64], ACT.Square, accum_out=SM[0:32, o:o + 1]), t, t_kc)
                        ta = put("act", lambda e, o=o: e.activation(
                            SM[0:32, o + 1:o + 2], SM[0:32, o:o + 1], ACT.Ln, bias=eps[0:32, :], scale=1.0 / 64), ta)
                        ta = put("act", lambda e, o=o: e.activation(
                            SM[0:32, o + 2:o + 3], SM[0:32, o + 1:o + 2], ACT.Exp, scale=-0.5), ta)
                        t1 = None
                        for half in range(2):
                            t1 = put("dve", lambda e, o=o, half=half: e.scalar_tensor_tensor(
                                KCT[0:32, 64 * half:64 * half + 64], b6.ap[0:32, 0:64], SM[0:32, o + 2:o + 3],
                                GP[0:32, G_KC:G_KC + 64], ALU.mult, ALU.mult), ta)
                        yield
                        b7 = banks[7]
                        t2 = put("pe", lambda e: e.transpose(b7.ap[:, 0:32], KCT[0:32, :], ident[0:32, 0:32]), t1, b7.free)
                        b6.free = [t1]
                        t_kc[g] = put("act", lambda e, g=g: e.activation(
                            KC[:, g * 32:g * 32 + 31], b7.ap[:, 0:31], ACT.Copy), t2, t_zk)
                        b7.free = [t_kc[g]]
                    else:
                        t = put("pe", lambda e, g=g: e.matmul(
                            b6.ap[:, 0:64], HG[:, g * 128:(g + 1) * 128], W2[:, 64:128], start=True, stop=True),
                            tgs, t_w2, b6.free)
                        cs = []
                        for r in range(4):
                            c = (2 * g + r // 2) * 128 + 64 * (r % 2)
                            cs.append(put("act", lambda e, r=r, c=c: e.activation(
                                VC[32 * r:32 * r + 32, c:c + 64], b6.ap[32 * r:32 * r + 32, 0:64], ACT.Copy), t, t_zc))
                        b6.free = cs
                        t_vc.extend(cs)

            flush()
            for i in range(4):
                for h in range(8):
                    half = h % 2
                    bk = banks[4 + half]
                    t = put("pe", lambda e, h=h, half=half, i=i, bk=bk: e.matmul(
                        bk.ap[:, 32 * (h // 2):32 * (h // 2) + 32], qtt[h // 2][64 * half:64 * half + 64, i * 128:(i + 1) * 128],
                        KC[64 * half:64 * half + 64, 32 * (h // 4):32 * (h // 4) + 32], start=True, stop=True),
                        t_qt[h // 2], t_kc, bk.free)
                yield
                p = pr.take()
                p3 = p.ap[:, 0:256].rearrange("p (h n) -> p h n", h=8)
                o = 32 + 32 * (i % 2)
                tms = []
                for half in range(2):
                    bk = banks[4 + half]
                    tms.append(put("dve", lambda e, i=i, p3=p3, bk=bk, half=half: e.tensor_tensor(
                        p3.rearrange("p (h c) n -> p h c n", c=2)[:, :, half, :],
                        bk.ap[:, 0:128].rearrange("p (h n) -> p h n", h=4),
                        CF[:, C_MC + 32 * i:C_MC + 32 * i + 32].unsqueeze(1).to_broadcast([128, 4, 32]), ALU.add),
                        t, p.free))
                    bk.free = [tms[-1]]
                t = tms
                t = put("dve", lambda e, p3=p3, o=o: e.tensor_reduce(SM[:, o:o + 8], p3, AX.X, ALU.max), t)
                t = put("dve", lambda e, p3=p3, o=o: e.tensor_tensor(
                    p3, p3, SM[:, o:o + 8].unsqueeze(2).to_broadcast([128, 8, 32]), ALU.subtract), t)
                t = put("act", lambda e, p=p: e.activation(p.ap[:, 0:256], p.ap[:, 0:256], ACT.Exp), t)
                t = put("dve", lambda e, p3=p3, o=o: e.tensor_reduce(SM[:, o + 8:o + 16], p3, AX.X, ALU.add), t)
                t = put("dve", lambda e, o=o: e.reciprocal(SM[:, o + 16:o + 24], SM[:, o + 8:o + 16]), t)
                t = put("dve", lambda e, o=o, i=i: e.scalar_tensor_tensor(
                    SM[:, o + 24:o + 32], SM[:, o + 16:o + 24], CF[:, C_VA + i:C_VA + i + 1],
                    GT[:, i * 24:(i + 1) * 24].rearrange("p (h c) -> p h c", c=3)[:, :, 0], ALU.mult, ALU.mult),
                    t, t_gt[i])
                t = put("dve", lambda e, p3=p3, o=o: e.tensor_tensor(
                    p3, p3, SM[:, o + 24:o + 32].unsqueeze(2).to_broadcast([128, 8, 32]), ALU.mult), t)
                for _ in range(4):
                    yield
                b6 = banks[6]
                for g in range(2):
                    t2 = put("pe", lambda e, g=g, p=p: e.transpose(
                        b6.ap[:, g * 128:(g + 1) * 128], p.ap[:, g * 128:(g + 1) * 128], ident), t, b6.free)
                p.free = [t2]
                t3 = put("act", lambda e, i=i: e.activation(
                    PTC.rearrange("p (g t) -> p g t", g=2)[:, :, i * 128:(i + 1) * 128],
                    b6.ap[:, 0:256].rearrange("p (g t) -> p g t", g=2), ACT.Copy), t2)
                b6.free = [t3]
                t_ptc.append(t3)

        sring = Ring([None, None])
        sring.slots = [banks[4], banks[5], banks[2]]
        pt_bank, ob = banks[6], banks[7]
        sm_free, sm_n = {}, [0]

        def softmax_stage(lhs, rhs, mask, mcol, n, deps, sink=None):
            bk = sring.take()
            put("pe", lambda e: e.matmul(bk.ap[:, 0:n], lhs, rhs, start=True, stop=False, skip_group_check=True),
                deps, bk.free)
            t = put("pe", lambda e: e.matmul(bk.ap[:, mcol:n], identb, mask, start=False, stop=True,
                                             skip_group_check=True), t_cb)
            o = 96 + 8 * (sm_n[0] % 16)
            sm_n[0] += 1
            p = pr.take()
            t1 = put("dve", lambda e: e.tensor_reduce(SM[:, o:o + 1], bk.ap[:, 0:n], AX.X, ALU.max, negate=True),
                     t, sm_free.get(o))
            t_sink = None
            if sink is not None:
                t1 = put("dve", lambda e: e.tensor_scalar(SM[:, o:o + 1], SM[:, o:o + 1], sink[1], None, ALU.min),
                         t1, sink[2])
            t2 = put("act", lambda e: e.activation(p.ap[:, 0:n], bk.ap[:, 0:n], ACT.Exp, bias=SM[:, o:o + 1],
                                                   accum_out=SM[:, o + 1:o + 2]), t1, p.free)
            bk.free = [t2]
            if sink is not None:
                t_sink = put("act", lambda e: e.activation(SM[:, o + 3:o + 4], sink[0], ACT.Exp,
                                                           bias=SM[:, o:o + 1]), t1)
            return p, o, [t2, t_sink]

        def turn(p, blocks, tok):
            n = len(blocks) * 128
            for k, j in enumerate(blocks):
                t = put("pe", lambda e, j=j, k=k: e.transpose(
                    pt_bank.ap[:, k * 128:(k + 1) * 128], p.ap[:, j * 128:(j + 1) * 128], ident), tok, pt_bank.free)
            p.free = [t]
            s = ptr_.take()
            t2 = put("act", lambda e: e.activation(s.ap[:, 0:n], pt_bank.ap[:, 0:n], ACT.Copy), t, s.free)
            pt_bank.free = [t2]
            return s, t2

        def need(table_, key):
            while key not in table_:
                if first_over[0] or not step(prj):
                    flush()

        class Splits:

            def __init__(self, src, toks, dst):
                self.src, self.toks, self.dst, self.att, self.got = src, toks, dst, None, {}

            def __getitem__(self, k):
                late = self.toks[k] is None
                while self.toks[k] is None:
                    if step(self.att):
                        tick()
                    else:
                        flush()
                for _ in range(AHEAD if late else 0):
                    if step(self.att):
                        tick()
                if k not in self.got:
                    self.got[k] = split_to(
                        self.dst.hi[k], self.dst.lo[k], self.src[k], self.toks[k], self.dst.busy)
                return self.got[k]

        def then_out(first, read, splits, nxt):
            yield from first
            read.busy = [last_pe[0]]
            first_over[0] = True
            d = splits.dst
            yield from fm(8, (d.hi, d.lo), splits, lambda m, bank, tok: residual(m, bank, tok, nxt), lead=2)
            d.busy = [last_pe[0]]

        t_om, acc_att, first_over = [None] * 4, [0.0], [False]

        def nsa_step(h, b, i):
            pair, half, g = h // 2, h % 2, h // 4
            n = (i + 1) * 128
            z = {}

            def scores():
                z["p"], z["o"], z["t"] = softmax_stage(
                    qtt[pair][64 * half:64 * half + 64, i * 128:(i + 1) * 128],
                    ktt[b][g][64 * half:64 * half + 64, 0:n], m_l, i * 128, n, [t_qt[pair], t_kt[b, g]])

            def weights():
                o, p = z["o"], z["p"]
                gate = GT[:, i * 24 + 3 * h + 1 + b:i * 24 + 3 * h + 2 + b]
                t = put("dve", lambda e: e.reciprocal(SM[:, o + 2:o + 3], SM[:, o + 1:o + 2]), z["t"])
                t = put("dve", lambda e: e.tensor_scalar(
                    p.ap[:, 0:n], p.ap[:, 0:n], SM[:, o + 2:o + 3], gate, ALU.mult, ALU.mult), t, t_gt[i])
                sm_free[o] = [t]
                z["t"] = t

            def turned():
                z["s"], z["t2"] = turn(z["p"], range(i + 1), z["t"])

            def values():
                if half == 0 and b == 0 and i == 0:
                    cc = (2 * g + pair % 2) * 128
                    put("pe", lambda e: e.matmul(ob.ap, VC[:, cc:cc + 128], PTC[:, g * T:(g + 1) * T],
                                                 start=True, stop=False, skip_group_check=True),
                        t_vc, t_ptc, ob.free)
                last = half == 1 and b == 1 and i == 3
                for j in range(i + 1):
                    v = vp[:, j, 2 * b + g, :]
                    v = v[:, 64:192] if half == 0 else v[:, 0:128]
                    t = put("pe", lambda e, j=j, v=v: e.matmul(
                        ob.ap[:, i * 128:(i + 1) * 128], v, z["s"].ap[:, j * 128:(j + 1) * 128],
                        start=False, stop=(last and j == i), skip_group_check=True), z["t2"], t_vp)
                z["s"].free = [t]
                if last:
                    t_om[pair] = put("act", lambda e: e.activation(OM[:, pair * T:(pair + 1) * T], ob.ap, ACT.Copy),
                                     t, t_cmp_pe)
                    ob.free = [t_om[pair]]
            return scores, weights, turned, values

        t_h3, t_hv = [None] * 12, [None] * 4

        def evac_h(m, bank, tok):
            s = tmp.take() if m >= 4 else Slot(h3[m])
            t = put("dve", lambda e: e.tensor_tensor(s.ap, bank.ap, RST[:, :], ALU.mult),
                    tok, s.free, rs["rst"], t_cmp_pe)
            bank.free = [t]
            rs["readers"].append(t)
            t = put("act", lambda e: e.activation(h3[m], s.ap, ACT.Tanh, scale=0.5), t)
            if m >= 4:
                t = put("dve", lambda e: e.scalar_tensor_tensor(h3[m], h3[m], 1.0, s.ap, ALU.add, ALU.mult), t)
                s.free = [t]
            t_h3[m] = t

        def evac_hv(i, bank, tok):
            t_hv[i] = put("dve", lambda e: e.tensor_scalar(
                HV[:, i * T:(i + 1) * T], bank.ap, LBT[:, 24 + i:25 + i], None, ALU.mult), tok, t_cmp_pe, rs["tok"])
            rs["readers"].append(t_hv[i])
            bank.free = [t_hv[i]]

        t_lb = []

        def bounds():
            l0, l1 = GP[:, G_LB:G_LB + 4], GP[:, G_LB + 4:G_LB + 8]
            t = put("dve", lambda e: e.tensor_tensor(LBT[:, 0:4], l0, l1, ALU.max), t_gp)
            ta = put("dve", lambda e: e.tensor_tensor(LBT[:, 4:8], l0, LBT[:, 0:4], ALU.subtract), t)
            tb = put("dve", lambda e: e.tensor_tensor(LBT[:, 8:12], l1, LBT[:, 0:4], ALU.subtract), t)
            t = put("act", lambda e: e.activation(LBT[:, 4:12], LBT[:, 4:12], ACT.Exp), ta, tb)
            t = put("dve", lambda e: e.tensor_tensor(LBT[:, 0:4], LBT[:, 4:8], LBT[:, 8:12], ALU.add), t)
            t = put("dve", lambda e: e.reciprocal(LBT[:, 0:4], LBT[:, 0:4]), t)
            t = put("dve", lambda e: e.tensor_tensor(LBT[:, 12:16], LBT[:, 4:8], LBT[:, 0:4], ALU.mult), t)
            t = put("dve", lambda e: e.tensor_scalar(LBT[:, 16:20], LBT[:, 12:16], -0.5, 0.5, ALU.mult, ALU.add), t)
            t_lb.append(put("dve", lambda e: e.tensor_tensor(LBT[:, 20:24], LBT[:, 16:20], LBT[:, 12:16], ALU.add), t))

        def first_mixer():
            yield from compress()
            table("exp_and_others")
            yield from pipeline([nsa_step(h, b, i) for h in range(8) for b in range(2) for i in range(4)], ORDER)

        att = first_mixer()
        tbanks[0] = banks[0:4]
        prj = tm(512, 2, h_tok, evac_hv)
        later(24, bounds)
        for k in range(23):
            step(att)
            for _ in range(3 if k < 4 else 1 if k < 20 else 0):
                step(prj)
        while not t_cmp_pe[2:]:
            step(att)
        drain(prj)
        dring.slots = banks[0:2]
        prj = fm(12, (hh, hl), h_tok, evac_h)
        while step(prj):
            acc_att[0] += NSA_PER_PROJ
            while acc_att[0] >= 1:
                acc_att[0] -= 1
                step(att)
        flush()
        fx = fence_of(Q)
        table("natural_log_exp_and_others")

        hx_ = [HX[:, k * T:(k + 1) * T] for k in range(16)]
        er = Ring(hx_[8:11])
        arr = Ring(hx_[12:14])
        for s in er.slots + arr.slots:
            s.free = list(fx)
        eq = Slot(hx_[11])
        eq.free = list(fx)
        set_free = [list(fx), list(fx)]
        aring = Ring([None] * 2)
        aring.slots = banks[0:2]
        head = {}
        t_mix = [None] * 4

        def levels(h):
            b = h % 2
            bc, kk, _, at_ = hx_[4 * b:4 * b + 4]
            at = at_.rearrange("p (i t) -> p i t", i=4)
            f, q = hf[:, h * T:(h + 1) * T], hq[:, h * T:(h + 1) * T]
            fr = set_free[b]
            t = put("dve", lambda e: e.tensor_scalar(
                f, f, LBT[:, 16 + h:17 + h], LBT[:, 20 + h:21 + h], ALU.mult, ALU.add), t_h3[h], t_lb)
            t_k = put("dve", lambda e: e.tensor_scalar(kk, f, -0.5, 0.5, ALU.mult, ALU.add), t, fr)
            t = put("act", lambda e: e.activation(f, f, ACT.Ln), t_k)
            t_b = put("dve", lambda e: e.tensor_tensor_scan(
                bc, CF[:, C_RM:C_RM + T], f, 0.0, ALU.mult, ALU.add), t, fr)
            t_scan[:] = [t_b]
            yield
            bk = aring.take()
            for i in range(4):
                t = put("pe", lambda e, i=i, bk=bk: e.matmul(
                    bk.ap[:, i * 128:(i + 1) * 128], kk[:, i * 128:(i + 1) * 128], q[:, i * 128:(i + 1) * 128],
                    start=True, stop=True), t_k, t_h3[4 + h], bk.free)
            t_at = put("dve", lambda e, bk=bk: e.tensor_tensor(
                at, bk.ap.rearrange("p (i t) -> p i t", i=4), ident.unsqueeze(1).to_broadcast([128, 4, 128]),
                ALU.mult), t, fr)
            bk.free = [t_at]
            readers = []

            def decay(lv):
                m = 1 << lv
                eb = er.take()
                v, b3, k3, q3 = [a.rearrange("p (n c) -> p n c", c=2 * m) for a in (eb.ap, bc, kk, q)]
                edge = b3[:, :, m - 1:m].to_broadcast([128, 256 // m, m])
                t1 = put("dve", lambda e: e.tensor_tensor(v[:, :, 0:m], edge, b3[:, :, 0:m], ALU.subtract),
                         t_b, eb.free)
                if m < 64:
                    t2 = put("pool", lambda e: e.tensor_tensor(
                        v[:, :, m:2 * m], b3[:, :, m:2 * m], edge, ALU.subtract), t_b, eb.free)
                else:
                    t2 = put("pool", lambda e: e.tensor_copy(v[:, :, m:2 * m], b3[:, :, m:2 * m]), t_b, eb.free)
                readers.extend([t1, t2])
                t = put("act", lambda e: e.activation(eb.ap, eb.ap, ACT.Exp), t1, t2)
                ta = put("dve", lambda e: e.tensor_tensor(v[:, :, 0:m], v[:, :, 0:m], k3[:, :, 0:m], ALU.mult), t, t_k)
                tb = put("pool", lambda e: e.tensor_tensor(
                    v[:, :, m:2 * m], v[:, :, m:2 * m], q3[:, :, m:2 * m], ALU.mult), t, t_h3[4 + h])
                return eb, [ta, tb]

            made = {0: decay(0)}
            for lv in range(7):
                if lv < 6:
                    made[lv + 1] = decay(lv + 1)
                yield
                eb, te = made[lv]
                bk = aring.take()
                for i in range(4):
                    c = slice(i * 128, (i + 1) * 128)
                    t = put("pe", lambda e, c=c, eb=eb, bk=bk: e.matmul(
                        bk.ap[:, c], eb.ap[:, c], eb.ap[:, c], start=True, stop=True), te, bk.free)
                eb.free = [t]
                t_at = put("dve", lambda e, bk=bk, lv=lv: e.copy_predicated(
                    at, CI[:, lv * 128:(lv + 1) * 128].unsqueeze(1).to_broadcast([128, 4, 128]),
                    bk.ap.rearrange("p (i t) -> p i t", i=4)), t, t_ci, t_at)
                bk.free = [t_at]
                yield
            head[h] = (t_k, t_b, t_at, readers)

        def whole(h):
            b = h % 2
            bc, kk, kh, at_ = hx_[4 * b:4 * b + 4]
            at = at_.rearrange("p (i t) -> p i t", i=4)
            q = hq[:, h * T:(h + 1) * T]
            t_k, t_b, t_at, readers = head[h]
            b4 = bc.rearrange("p (n c) -> p n c", c=128)
            t = put("dve", lambda e: e.tensor_tensor(
                b4[:, :, 64:128], b4[:, :, 64:128], b4[:, :, 63:64].to_broadcast([128, 4, 64]), ALU.add), readers)
            tk = put("dve", lambda e: e.tensor_tensor(
                kh.rearrange("p (n c) -> p n c", c=128), b4[:, :, 127:128].to_broadcast([128, 4, 128]), b4,
                ALU.subtract), t, set_free[b])
            tk = put("act", lambda e: e.activation(kh, kh, ACT.Exp), tk)
            tq = put("act", lambda e: e.activation(eq.ap, bc, ACT.Exp), t, eq.free)
            EB = LBT[:, 40 + 4 * h:44 + 4 * h]
            te = put("act", lambda e: e.activation(EB, b4[:, :, 127], ACT.Exp), t)
            tk = put("dve", lambda e: e.tensor_tensor(kh, kh, kk, ALU.mult), tk)
            tq = put("pool", lambda e: e.tensor_tensor(eq.ap, eq.ap, q, ALU.mult), tq)
            yield
            ks_ = {}
            for n, (j, i) in enumerate(((0, 2), (0, 3), (1, 3))):
                dst = hx_[14 + b][:, n * 128:(n + 1) * 128]
                src = kh[:, j * 128:(j + 1) * 128]
                two = i - j == 3
                ks_[j, i] = (dst, put("dve", lambda e, dst=dst, src=src, j=j, two=two: e.tensor_scalar(
                    dst, src, EB[:, j + 1:j + 2], EB[:, j + 2:j + 3] if two else None, ALU.mult,
                    *([ALU.mult] if two else [])), tk, te, set_free[b]))
            for j in range(3):
                ks_[j, j + 1] = (kh[:, j * 128:(j + 1) * 128], tk)
            yield
            o_b = banks[3]
            kept = {}
            for i in (1, 0, 2, 3, 4):
                if 0 < i < 4:
                    bk = aring.take()
                    for j in range(i):
                        k_, t_ = ks_[j, i]
                        t = put("pe", lambda e, i=i, j=j, k_=k_, bk=bk: e.matmul(
                            bk.ap[:, j * 128:(j + 1) * 128], k_, eq.ap[:, i * 128:(i + 1) * 128],
                            start=True, stop=True), t_, tq, bk.free)
                    t_eq = t
                    s = arr.take()
                    t = put("act", lambda e, s=s, i=i, bk=bk: e.activation(
                        s.ap[:, 0:i * 128], bk.ap[:, 0:i * 128], ACT.Copy), t, s.free)
                    bk.free = [t]
                    kept[i] = (s, t)
                    yield
                    if i == 1:
                        continue
                if i == 0:
                    t = put("pe", lambda e: e.matmul(
                        o_b.ap[:, 0:128], HV[:, h * 128:(h + 1) * 128], at[:, 0, :], start=True, stop=False,
                        skip_group_check=True), t_at, t_hv, o_b.free)
                    continue
                n = i - 1
                s, ts_ = kept[n]
                for j in range(n + 1):
                    rhs = s.ap[:, j * 128:(j + 1) * 128] if j < n else at[:, n, :]
                    t = put("pe", lambda e, n=n, j=j, rhs=rhs: e.matmul(
                        o_b.ap[:, n * 128:(n + 1) * 128], HV[:, j * T + h * 128:j * T + (h + 1) * 128], rhs,
                        start=False, stop=(n == 3 and j == 3), skip_group_check=True), ts_, t_at, t_hv)
                s.free = [t]
                yield
            eq.free = [t_eq]
            set_free[b] = [t, t_eq]

            def done(t):
                t_mix[h] = put("dve", lambda e: e.tensor_tensor(
                    h3[h + 4], h3[h + 4], h3[h + 8], ALU.mult), t, t_h3[h + 8])
            head_norm(o_b, t, LBT[:, 36:37], h3[h + 4], [tq, t_eq, readers, t_at], done, aring, 1)
            yield

        def second_mixer():
            def ticks(g):
                for _ in g:
                    tick()
                    yield
            yield from ticks(levels(0))
            for h in range(4):
                a, b = whole(h), (levels(h + 1) if h < 3 else iter(()))
                live = [True, True]
                while live[0] or live[1]:
                    for n, g in enumerate((a, b)):
                        if live[n]:
                            live[n] = step(g)
                            tick()
                            yield

        prj = second_mixer()
        drive(att, prj, HGRN_PER_NSA)
        drain(prj)
        flush()
        fence = fence_of(Q)
        om = [(OM[:, k * T:(k + 1) * T], t_om[k]) for k in range(4)] + [(h3[4 + k], t_mix[k]) for k in range(4)]
        mix_tok = [split_to(hh[k], hl[k], src, t, fence) for k, (src, t) in enumerate(om)]

        ph = ExitStack()
        PX = sbt(ph, "PX", 22 * T)
        GH = sbt(ph, "GH", 8 * T, R)
        GL = sbt(ph, "GL", 8 * T, R)
        ph.close()
        og = Operand([GH[:, k * T:(k + 1) * T] for k in range(8)], [GL[:, k * T:(k + 1) * T] for k in range(8)])
        og.busy = [fence, mix_tok]
        E2[0] = CF[:, C_RM:C_RM + T]
        h_tok = []
        dring.slots = banks[0:3]
        drain(fm(8, (oa.hi, oa.lo), mix_tok, lambda m, bank, tok: residual(m, bank, tok, (G_FFN, og, h_tok)), lead=3))
        oa.busy = [last_pe[0]]

        def ffn(src, dst, h_tok, g_next):
            h_next = []
            dring.slots = [banks[0], banks[1], banks[4], banks[5]]
            for part, n in enumerate(PARTS):
                toks, keep = [], {}

                def evac(m, bank, tok, toks=toks, keep=keep):
                    if m % 2 == 0:
                        s = tmp.take()
                        t = put("dve", lambda e: e.tensor_tensor(s.ap, bank.ap, RST[:, :], ALU.mult),
                                tok, s.free, rs["rst"])
                        bank.free = [t]
                        rs["readers"].append(t)
                        keep["s"], keep["t"] = s, put("act", lambda e: e.activation(s.ap, s.ap, ACT.Silu), t)
                    else:
                        s, t0, k = keep["s"], keep["t"], m // 2
                        t = put("dve", lambda e: e.tensor_tensor(s.ap, bank.ap, s.ap, ALU.mult), tok, t0)
                        bank.free = [t]
                        t = put("pool", lambda e: e.tensor_tensor(s.ap, s.ap, RST[:, :], ALU.mult), t)
                        rs["readers"].append(t)
                        pair = split_to(dst.hi[k], dst.lo[k], s.ap, t, dst.busy)
                        s.free = pair
                        toks.append(pair)
                drain(fm(2 * n, (src.hi, src.lo), h_tok, evac, lead=3 if part == 0 else 1))
                if part == 2:
                    src.busy = [last_pe[0]]
                    if g_next is not None:
                        table("natural_log_exp_and_others")

                def evac_d(m, bank, tok, part=part):
                    residual(m, bank, tok, (g_next, src, h_next) if part == 2 and g_next is not None else None)
                    if part == 2 and g_next is None:
                        t_out.append(Q.dma("sp", dsem(f"out{m}"), out[:, m, :], xt[m], x_tok[m]))
                drain(fm(8, (dst.hi, dst.lo), toks, evac_d, ((0, n),), lead=2))
                dst.busy = [last_pe[0]]
            return h_next

        t_out = []
        h_tok = ffn(og, oa, h_tok, G_AT0)

        P2 = PX
        VD = P2[:, 0:8 * T]
        om2 = Ring([P2[:, (8 + k) * T:(9 + k) * T] for k in range(2)])
        qr = Ring([P2[:, (10 + k) * T:(11 + k) * T] for k in range(4)])
        kr = Ring([P2[:, (14 + k) * T:(15 + k) * T] for k in range(4)])
        more = Ring([P2[:, (18 + k) * T:(19 + k) * T] for k in range(2)]).slots
        pr.slots = pr.slots + more
        for s in qr.slots + kr.slots + om2.slots + more:
            s.free = [fence]
        lam = LBT[:, 60:61]
        lp = GP[:, G_LAM:G_LAM + 256]
        tl = []
        for k in range(2):
            t = put("dve", lambda e, k=k: e.tensor_tensor(
                SM[:, 64 * k:64 * k + 64], lp[:, 128 * k:128 * k + 64], lp[:, 128 * k + 64:128 * k + 128], ALU.mult),
                fence, t_gp)
            tl.append(put("dve", lambda e, k=k: e.tensor_reduce(
                LBT[:, 56 + k:57 + k], SM[:, 64 * k:64 * k + 64], AX.X, ALU.add), t))
        t = put("act", lambda e: e.activation(LBT[:, 58:60], LBT[:, 56:58], ACT.Exp), tl)
        t = put("dve", lambda e: e.tensor_tensor(lam, LBT[:, 59:60], LBT[:, 58:59], ALU.subtract), t)
        t_lam = put("dve", lambda e: e.tensor_scalar(lam, lam, -LAMBDA_INIT, None, ALU.add), t)
        sm_free.clear()

        t_vd = []
        for half_ in range(2):
            def evac_v(i, bank, tok, half_=half_):
                c = i * 1024 + half_ * 512
                t = put("dve", lambda e: e.tensor_scalar(VD[:, c:c + 512], bank.ap, LBT[:, 24 + i:25 + i], None,
                                                         ALU.mult), tok, fence, rs["tok"])
                bank.free = [t]
                rs["readers"].append(t)
                t_vd.append(t)
            tbanks[0] = banks[0:4] if half_ else banks[4:8]
            drain(tm(512, 2, h_tok, evac_v, og))

        heads, cur, over = {}, [0], [0]

        def evac_qk(m, bank, tok):
            ring, gc = (qr, gq8[1]) if m % 2 == 0 else (kr, GP[:, G_DK:G_DK + 1])
            s = ring.take()
            cur[0] = m + 1

            def done(t):
                heads[m] = (s, t)
            qk_norm(bank, tok, gc, True, s.ap, s.free, done)

        t_om2 = [None] * 8

        def da_step(hd, i):
            n = (i + 1) * 128
            z = {}

            def scores():
                need(heads, 2 * hd + 1)
                (qs, tq_), (ks, tk_) = heads[2 * hd], heads[2 * hd + 1]
                for c in range(2):
                    z[c] = softmax_stage(qs.ap[64 * c:64 * c + 64, i * 128:(i + 1) * 128],
                                         ks.ap[64 * c:64 * c + 64, 0:n], m_l, i * 128, n, [tq_, tk_])
                if i == 3:
                    last = Q.q["pe"][-1][2]
                    qs.free, ks.free = [last], [last]
                    over[0] += 1

            def weights():
                (p0, o0, t0), (p1_, o1, t1) = z[0], z[1]
                ta = put("dve", lambda e: e.reciprocal(SM[:, o0 + 2:o0 + 3], SM[:, o0 + 1:o0 + 2]), t0)
                tb = put("dve", lambda e: e.reciprocal(SM[:, o1 + 2:o1 + 3], SM[:, o1 + 1:o1 + 2]), t1)
                tb = put("dve", lambda e: e.tensor_scalar(
                    p1_.ap[:, 0:n], p1_.ap[:, 0:n], SM[:, o1 + 2:o1 + 3], lam, ALU.mult, ALU.mult), tb, t_lam)
                t = put("dve", lambda e: e.scalar_tensor_tensor(
                    p0.ap[:, 0:n], p0.ap[:, 0:n], SM[:, o0 + 2:o0 + 3], p1_.ap[:, 0:n], ALU.mult, ALU.add), ta, tb)
                sm_free[o0], sm_free[o1] = [t], [t]
                p1_.free = [t]
                z["t"] = t

            def turned():
                z["s"], z["t2"] = turn(z[0][0], range(i + 1), z["t"])

            def values():
                for j in range(i + 1):
                    t = put("pe", lambda e, j=j: e.matmul(
                        ob.ap[:, i * 128:(i + 1) * 128], VD[:, j * 1024 + hd * 128:j * 1024 + (hd + 1) * 128],
                        z["s"].ap[:, j * 128:(j + 1) * 128], start=(i == 0), stop=(i == 3 and j == 3),
                        skip_group_check=True), z["t2"], t_vd, ob.free)
                z["s"].free = [t]
                if i == 3:
                    s = om2.take()
                    srcs[hd] = s.ap

                    def done(t):
                        t_om2[hd] = t
                        s.free = splits[hd]
                    head_norm(ob, t, LBT[:, 35:36], s.ap, s.free, done)
            return scores, weights, turned, values

        dring.slots = banks[0:2]
        att = pipeline([da_step(hd, i) for hd in range(8) for i in range(4)], ORDER)
        first_over[0] = False
        h_next = []
        srcs = [None] * 8
        splits = Splits(srcs, t_om2, oa)
        splits.att = att
        prj = then_out(fm(16, (og.hi, og.lo), h_tok, evac_qk), og, splits, (G_F0, og, h_next))
        for k in range(DA_LEAD):
            step(prj)
        drive(att, prj, PROJ_PER_DA, lambda: first_over[0] or cur[0] // 2 <= over[0] + 3)
        drain(prj)
        fence = fence_of(Q)
        t_zp = put("pool", lambda e: e.memset(PX[:, 0:11 * T], 0.0), fence)
        h_tok = ffn(og, oa, h_next, G_KV)

        P3 = PX
        pr.slots = pr.slots[0:4]
        KW = P3[:, 0:4 * 640].rearrange("p (k t) -> p k t", k=4)
        VW = P3[:, 5 * T:11 * T].rearrange("p (i k c) -> p i k c", i=4, k=4)
        OM3 = P3[:, 11 * T:19 * T]
        qw = Ring([P3[:, (19 + k) * T:(20 + k) * T] for k in range(3)])
        for s in qw.slots:
            s.free = [fence]
        NS = SM[:, 64:80]
        t_ns = put("dve", lambda e: e.tensor_scalar(NS, GP[:, G_SINK:G_SINK + 16], -1.0, None, ALU.mult), fence)
        t_kw, t_vw = {}, []

        q_tok = []
        for m in range(8):
            later(14 + 3 * m, lambda m=m: q_tok.append(scaled_split(m, G_AT1, oa)))

        def evac_k(m, bank, tok):
            s = qw.take()

            def done(t):
                us = []
                for a in range(2):
                    for half in range(2):
                        us.append(put("act", lambda e, a=a, half=half: e.activation(
                            KW[64 * half:64 * half + 64, 2 * m + a, 128:640], s.ap[64 * a:64 * a + 64, :], ACT.Copy),
                            t, t_zp))
                    t_kw[2 * m + a] = us[-2:]
                s.free = us
            qk_norm(bank, tok, GP[:, G_SK:G_SK + 1], True, s.ap, s.free, done)

        def evac_vw(i, bank, tok):
            t = put("dve", lambda e: e.tensor_scalar(
                VW[:, i, :, 64:128], bank.ap[:, 0:256].rearrange("p (k c) -> p k c", k=4), LBT[:, 24 + i:25 + i],
                None, ALU.mult), tok, t_zp, rs["tok"])
            bank.free = [t]
            rs["readers"].append(t)
            t_vw.append(t)

        dring.slots = banks[0:2]
        drain(fm(2, (og.hi, og.lo), h_tok, evac_k, lead=2))
        tbanks[0] = banks[4:8]
        drain(tm(256, 4, h_tok, evac_vw, og))
        flush()
        og.busy = [last_pe[0]]
        pairs, cur, over = {}, [0], [0]

        def evac_qw(m, bank, tok):
            s = qw.take()
            cur[0] = m + 1

            def done(t):
                pairs[m] = (s, t)
            qk_norm(bank, tok, gq8[2], True, s.ap, s.free, done)

        t_om3 = [None] * 8

        def sw_step(h, i):
            pair, half, kv = h // 2, h % 2, h // 4
            z = {}

            def scores():
                need(pairs, pair)
                qs, tq_ = pairs[pair]
                z["p"], z["o"], z["t"] = softmax_stage(
                    qs.ap[64 * half:64 * half + 64, i * 128:(i + 1) * 128],
                    KW[64 * half:64 * half + 64, kv, i * 128:i * 128 + 256], m_ul if i else m_fl, 0, 256,
                    [tq_, t_kw[kv], t_zp], (GP[:, G_SINK + h:G_SINK + h + 1], NS[:, h:h + 1], t_ns))
                if half == 1 and i == 3:
                    qs.free = [Q.q["pe"][-1][2]]
                    over[0] += 1

            def weights():
                o, p = z["o"], z["p"]
                t = put("dve", lambda e: e.tensor_tensor(
                    SM[:, o + 2:o + 3], SM[:, o + 1:o + 2], SM[:, o + 3:o + 4], ALU.add), z["t"])
                t = put("dve", lambda e: e.reciprocal(SM[:, o + 4:o + 5], SM[:, o + 2:o + 3]), t)
                t = put("dve", lambda e: e.tensor_scalar(p.ap[:, 0:256], p.ap[:, 0:256], SM[:, o + 4:o + 5],
                                                         None, ALU.mult), t)
                sm_free[o] = [t]
                z["t"] = t

            def turned():
                z["s"], z["t2"] = turn(z["p"], (0, 1) if i else (1,), z["t"])

            def values():
                js = (i - 1, i) if i else (0,)
                for k, j in enumerate(js):
                    v = VW[:, j, kv, :]
                    v = v[:, 64:192] if half == 0 else v[:, 0:128]
                    t = put("pe", lambda e, k=k, v=v: e.matmul(
                        ob.ap[:, i * 128:(i + 1) * 128], v, z["s"].ap[:, k * 128:(k + 1) * 128],
                        start=(half == 0 and i == 0), stop=(half == 1 and i == 3 and k == 1),
                        skip_group_check=True), z["t2"], t_vw, t_zp, ob.free)
                z["s"].free = [t]
                if half == 1 and i == 3:
                    t_om3[pair] = put("act", lambda e: e.activation(
                        OM3[:, pair * T:(pair + 1) * T], ob.ap, ACT.Copy), t, fence)
                    ob.free = [t_om3[pair]]
                    splits[pair]
            return scores, weights, turned, values

        att = pipeline([sw_step(h, i) for h in range(16) for i in range(4)], ORDER)
        first_over[0] = False
        h_next = []
        splits = Splits([OM3[:, k * T:(k + 1) * T] for k in range(8)], t_om3, og)
        splits.att = att
        prj = then_out(fm(8, (oa.hi, oa.lo), q_tok, evac_qw), oa, splits, (G_F1, oa, h_next))
        for k in range(SW_LEAD):
            step(prj)
        drive(att, prj, PROJ_PER_SW, lambda: first_over[0] or cur[0] <= over[0] + 2)
        drain(prj)
        ffn(oa, og, h_next, None)

        Q.count()
        block = ctx.enter_context(nc.Block())

        @block.sync
        def _(e):
            Q.emit("sp", e, sems)
            for t in t_out:
                e.wait_ge(t.eng, t.val)

        @block.gpsimd
        def _(e):
            Q.emit("pool", e, sems)

        @block.scalar
        def _(e):
            Q.emit("act", e, sems)

        @block.vector
        def _(e):
            Q.emit("dve", e, sems)

        @block.tensor
        def _(e):
            Q.emit("pe", e, sems)


def constants():
    p = np.arange(128)
    cf = np.zeros((128, C_N), np.float32)
    cf[:, C_ID:C_ID + 128] = np.eye(128)
    cf[:, C_BO:C_BO + 128] = (p[:, None] // 64) == (p[None, :] // 64)
    cf[:, C_ON:C_ON + 128] = 1.0
    for d in range(128):
        if d % 64 < 32:
            cf[d + 32, C_PM + d] = -1.0
        else:
            cf[d - 32, C_PM + d] = 1.0
    end = np.arange(32) * 16 + 31
    for i in range(4):
        t = i * 128 + p
        cf[:, C_MC + 32 * i:C_MC + 32 * i + 32] = np.where(end[None, :] <= t[:, None], 0.0, -1e30)
        cf[:, C_MC + 32 * i + 31] = -1e30
        cf[:, C_VA + i] = t >= 31
    inv = (np.float32(1.0) / (np.float32(10000.0) ** (np.arange(0, 64, 2, dtype=np.float32) / np.float32(64))))
    cf[:, C_INV] = inv.astype(np.float32)[p % 32]
    cf[:, C_EPS] = EPS
    cf[:, C_HPI] = np.pi / 2
    cf[:, C_RM:C_RM + 512] = (np.arange(512) % 64 != 0)[None, :]
    cb = np.zeros((128, 640), np.float32)
    cb[:, 0:128] = np.eye(128)
    cb[:, 128:256] = -1e30
    low = np.where(p[None, :] <= p[:, None], 0.0, -1e30)
    cb[:, 256:384] = low
    cb[:, 384:512] = np.where(p[None, :] > p[:, None], 0.0, -1e30)
    cb[:, 512:640] = low
    ci = np.zeros((128, 8 * 128), np.float32)
    for lv in range(7):
        m = 1 << lv
        s, t = p[:, None], p[None, :]
        ci[:, lv * 128:(lv + 1) * 128] = (s // (2 * m) == t // (2 * m)) & (s % (2 * m) < m) & (t % (2 * m) >= m)
    return cf, cb, ci


def kernel(**inputs):
    import ml_dtypes
    import concourse.bacc as _bacc
    from concourse.bass_utils import run_bass_kernel_spmd as _run

    a = {k: np.asarray(v) for k, v in inputs.items()}

    def cols(w, n):
        k, m = w.shape
        return w.reshape(k // 128, 128, m // n, n).transpose(2, 1, 0, 3).reshape(m // n, 128, (k // 128) * n)

    def rows(w, per):
        k, m = w.shape
        return w.reshape(k // 128 // per, per, 128, m).transpose(0, 2, 1, 3).reshape(k // 128 // per, 128, per * m)

    cf, cb, ci = constants()
    w = a["w_in"][0]
    o = [0]
    for s in (512, 128, 128, 128, 128, 128, 128, 24, 512, 512, 512, 512):
        o.append(o[-1] + s)
    part = [w[:, o[i]:o[i + 1]] for i in range(12)]
    wq, wkc, wvc, wks, wvs, wkw, wvw, wg, whq, whf, whi, whg = part
    D = {"c_f": cf, "c_b": cb.astype(ml_dtypes.bfloat16), "c_i": ci}
    D["xT"] = a["x"][0].reshape(512, 8, 128).transpose(2, 1, 0)
    D["pos"] = a["positions_2"].reshape(512)
    D["w_in"] = cols(np.concatenate([wkc, wvc, wks, wkw, wq], 1), 128)
    D["w_ing"] = rows(np.concatenate([wvs, wvw, wg], 1), 2)
    D["w_inh"] = cols(np.concatenate([whf, whq, whg], 1), 128)
    D["w_inv"] = rows(whi, 2)
    D["w_out"] = cols(a["w_out"][0], 128)
    for n, gu, dn in ((1, a["w_gate_up"][0], a["w_down"][0]), (2, a["w_gate_up_2"][0], a["w_down_2"][0]),
                      (3, a["w_gate_up_2"][1], a["w_down_2"][1])):
        D[f"wgu{n}"] = cols(gu, 128)
        D[f"wd{n}"] = cols(dn, 128)
    qkv = a["da_w_qkv_2"][0]
    D["da_v"] = np.concatenate([rows(qkv[:, 2048:2560], 2), rows(qkv[:, 2560:3072], 2)], 0)
    qk = np.stack([qkv[:, 0:1024].reshape(1024, 8, 128), qkv[:, 1024:2048].reshape(1024, 8, 128)], 2)
    D["da_qk"] = cols(qk.reshape(1024, 2048), 128)
    D["da_o"] = cols(a["da_w_o_2"][0], 128)
    D["sw_k"] = cols(a["w_kv_2"][:, 0:256], 128)
    D["sw_v"] = rows(a["w_kv_2"][:, 256:512], 4)
    D["sw_q"] = cols(a["sw_w_q_2"][0], 128)
    D["sw_o"] = cols(a["sw_w_o_2"][0], 128)
    D["cmp_w1"] = np.stack([a[n][0].reshape(16, 128, 128).transpose(1, 0, 2).reshape(128, 2048)
                            for n in ("cmp_k_w1", "cmp_v_w1")], 0)
    D["cmp_w2"] = np.concatenate([a["cmp_k_w2"][0], a["cmp_v_w2"][0]], 1)

    def g8(v):
        return v.reshape(8, 128).T

    def col(v):
        v = v.reshape(-1, 1)
        return np.concatenate([v, v], 0) if v.shape[0] == 64 else v

    def line(v):
        return np.broadcast_to(v.reshape(1, -1), (128, v.size))

    lb = a["hgrn_lb_logits"].reshape(2, 4, 128).transpose(2, 0, 1).reshape(128, 8)
    pk = [np.concatenate([a[n][0].T, a[n][0].T], 0) for n in ("cmp_pos_k", "cmp_pos_v")]
    D["gp"] = np.concatenate([
        g8(a["norm_mix"][0]), g8(a["norm_ffn"][0]), g8(a["attn_norm_2"][0]), g8(a["attn_norm_2"][1]),
        g8(a["ffn_norm_2"][0]), g8(a["ffn_norm_2"][1]), g8(a["kv_norm_2"]),
        col(a["q_norm"][0]), col(a["k_norm"][0, 1]), col(a["k_norm"][0, 2]), col(a["da_q_norm_2"][0]),
        col(a["da_k_norm_2"][0]), col(a["da_subln_2"][0]), col(a["sw_q_norm_2"][0]), col(a["k_norm_2"]),
        col(a["hgrn_o_norm"][0]), lb, pk[0], pk[1], line(a["k_norm"][0, 0]), line(a["sw_sinks_2"][0]),
        line(a["da_lambda_2"][0])], 1)

    nc = _bacc.Bacc("TRN2", target_bir_lowering=False, num_devices=1)
    arrays, aps = {}, {}
    for name, v in D.items():
        v = np.ascontiguousarray(v)
        arrays["in_" + name] = v
        aps[name] = nc.dram_tensor("in_" + name, v.shape, mybir.dt.from_np(v.dtype), kind="ExternalInput").ap()
    out = nc.dram_tensor("out_xT", (128, 8, 512), mybir.dt.float32, kind="ExternalOutput").ap()
    program(nc, aps, out)
    r = _run(nc, [arrays], core_ids=[0])
    y = np.asarray(r.results[0]["out_xT"])
    return np.ascontiguousarray(y.transpose(2, 1, 0).reshape(1, 512, 1024))
```
